# Optimizing a Trainium2 kernel written in Bass

```python
import jax, jax.numpy as jnp
from jax import lax
import numpy as np

D_MODEL = 1024
BATCH = 1
SEQ = 512
DEPTH = 2
DEC_BATCH = 8
DEC_SEQ = 16
PAST_LEN = 128

CHUNK = 64
N_A = DEPTH // 2
N_B = DEPTH - N_A
GLA_HEADS = 4
GLA_DK = D_MODEL // 2 // GLA_HEADS
GLA_DV = D_MODEL // GLA_HEADS
GLA_RANK = 16
GLA_TAU = 16.0
GLA_BLOCK = 16
QK_W = GLA_HEADS * GLA_DK
V_W = GLA_HEADS * GLA_DV
GLA_IN = 2 * QK_W + 2 * V_W + GLA_RANK
ATT_HEADS = 16
ATT_KV_HEADS = 2
ATT_GROUP = ATT_HEADS // ATT_KV_HEADS
HEAD_DIM = D_MODEL // ATT_HEADS
KV_W = ATT_KV_HEADS * HEAD_DIM
WINDOW = 128
D_FF = 2816
CONV_W = 3
EPS = 1e-6

kernel_name = 'yoco_gla_swa_sink_convffn_stream_step'

def rmsnorm(x, g):
    xf = x.astype(jnp.float32)
    y = xf * lax.rsqrt(jnp.mean(xf * xf, -1, keepdims=True) + EPS)
    return (y * g.astype(jnp.float32)).astype(x.dtype)

def gla_mixer(h, s0, w_in, w_g2, b_g2, g_onorm, w_out):
    B, T, _ = h.shape
    f32 = jnp.float32
    p = h @ w_in
    q, k, v, r, gl = jnp.split(p, [QK_W, 2 * QK_W, 2 * QK_W + V_W, 2 * QK_W + 2 * V_W], axis=-1)
    log_a = jax.nn.log_sigmoid((gl @ w_g2 + b_g2).astype(f32)) / GLA_TAU
    pad = (-T) % GLA_BLOCK
    nb = (T + pad) // GLA_BLOCK

    def blocks(a, d):
        a = a.astype(f32).reshape(B, T, GLA_HEADS, d)
        a = jnp.pad(a, ((0, 0), (0, pad), (0, 0), (0, 0)))
        return a.reshape(B, nb, GLA_BLOCK, GLA_HEADS, d).transpose(1, 0, 3, 2, 4)

    qb = blocks(q, GLA_DK) * (GLA_DK ** -0.5)
    kb = blocks(k, GLA_DK)
    vb = blocks(v, GLA_DV)
    ab = blocks(log_a, GLA_DK)
    tril = jnp.tril(jnp.ones((GLA_BLOCK, GLA_BLOCK), dtype=bool))

    def step(S, blk):
        qc, kc, vc, ac = blk
        bcum = jnp.cumsum(ac, axis=2)
        qd = qc * jnp.exp(bcum)
        kd = kc * jnp.exp(-bcum)
        att = jnp.where(tril, jnp.einsum('bhld,bhmd->bhlm', qd, kd), 0.0)
        o = jnp.einsum('bhld,bhde->bhle', qd, S) + jnp.einsum('bhlm,bhme->bhle', att, vc)
        blast = bcum[:, :, -1:, :]
        kr = kc * jnp.exp(blast - bcum)
        S = S * jnp.exp(blast[:, :, 0, :])[..., None] + jnp.einsum('bhld,bhle->bhde', kr, vc)
        return S, o

    s_final, o = lax.scan(step, s0.astype(f32), (qb, kb, vb, ab))
    o = o.transpose(1, 0, 3, 2, 4).reshape(B, nb * GLA_BLOCK, GLA_HEADS, GLA_DV)[:, :T]
    o = o * lax.rsqrt(jnp.mean(o * o, -1, keepdims=True) + EPS) * g_onorm.astype(f32)
    o = o.reshape(B, T, V_W) * jax.nn.silu(r.astype(f32))
    return o.astype(h.dtype) @ w_out, s_final

def sink_attention(q, k, v, valid, sinks):
    s = jnp.einsum('bqngd,bknd->bngqk', q, k).astype(jnp.float32)
    s = jnp.where(valid, s, -jnp.inf)
    sk = sinks.astype(jnp.float32).reshape(1, ATT_KV_HEADS, ATT_GROUP, 1, 1)
    m = jnp.maximum(jnp.max(s, -1, keepdims=True), sk)
    e = jnp.exp(s - m)
    p = e / (jnp.sum(e, -1, keepdims=True) + jnp.exp(sk - m))
    return jnp.einsum('bngqk,bknd->bqngd', p.astype(v.dtype), v)

def swa_prompt(h, k, v, w_q, sinks, w_o):
    B, T, _ = h.shape
    q = (h @ w_q).reshape(B, T, ATT_KV_HEADS, ATT_GROUP, HEAD_DIM) * (HEAD_DIM ** -0.5)
    n_chunks = T // CHUNK
    band = WINDOW + CHUNK
    kp = jnp.pad(k, ((0, 0), (WINDOW, 0), (0, 0), (0, 0)))
    vp = jnp.pad(v, ((0, 0), (WINDOW, 0), (0, 0), (0, 0)))

    def one_chunk(c):
        qs = lax.dynamic_slice_in_dim(q, c * CHUNK, CHUNK, axis=1)
        ks = lax.dynamic_slice_in_dim(kp, c * CHUNK, band, axis=1)
        vs = lax.dynamic_slice_in_dim(vp, c * CHUNK, band, axis=1)
        valid = (c * CHUNK - WINDOW + jnp.arange(band)) >= 0
        return sink_attention(qs, ks, vs, valid, sinks)

    o = lax.map(one_chunk, jnp.arange(n_chunks))
    o = jnp.moveaxis(o, 0, 1).reshape(B, T, ATT_HEADS * HEAD_DIM)
    return o @ w_o

def swa_sample(h, k_all, v_all, w_q, sinks, w_o):
    B, T, _ = h.shape
    q = (h @ w_q).reshape(B, T, ATT_KV_HEADS, ATT_GROUP, HEAD_DIM) * (HEAD_DIM ** -0.5)
    valid = jnp.ones((k_all.shape[1],), dtype=bool)
    o = sink_attention(q, k_all, v_all, valid, sinks).reshape(B, T, ATT_HEADS * HEAD_DIM)
    return o @ w_o

def conv_ffn(h, buf, w_up, conv_w, conv_b, w_down):
    T = h.shape[1]
    u = h @ w_up
    ue = jnp.concatenate([buf.astype(u.dtype), u], axis=1)
    c = ue[:, 0:T] * conv_w[0]
    for j in range(1, CONV_W):
        c = c + ue[:, j:j + T] * conv_w[j]
    c = c + conv_b
    g, val = jnp.split(c, 2, axis=-1)
    y = (jax.nn.silu(g) * val) @ w_down
    return y, ue[:, -(CONV_W - 1):]

def trunk(x, gla_s, ffn_buf, kv_cache_k, kv_cache_v, norm_mix, norm_ffn, norm_kv, norm_final,
          gla_w_in, gla_w_g2, gla_b_g2, gla_g_onorm, gla_w_out, w_kv, att_w_q, att_sinks, att_w_o,
          ffn_w_up, ffn_conv_w, ffn_conv_b, ffn_w_down):
    B, T, _ = x.shape
    new_gla, new_buf = [], []
    k_all = v_all = None
    for layer in range(DEPTH):
        h = rmsnorm(x, norm_mix[layer])
        if layer < N_A:
            y, s = gla_mixer(h, gla_s[layer], gla_w_in[layer], gla_w_g2[layer], gla_b_g2[layer],
                             gla_g_onorm[layer], gla_w_out[layer])
            new_gla.append(s)
        else:
            j = layer - N_A
            if kv_cache_k is None:
                y = swa_prompt(h, k_all, v_all, att_w_q[j], att_sinks[j], att_w_o[j])
            else:
                y = swa_sample(h, k_all, v_all, att_w_q[j], att_sinks[j], att_w_o[j])
        x = x + y
        y, b = conv_ffn(rmsnorm(x, norm_ffn[layer]), ffn_buf[layer], ffn_w_up[layer],
                        ffn_conv_w[layer], ffn_conv_b[layer], ffn_w_down[layer])
        new_buf.append(b)
        x = x + y
        if layer == N_A - 1:
            kv = rmsnorm(x, norm_kv) @ w_kv
            k_new, v_new = jnp.split(kv, 2, axis=-1)
            k_new = k_new.reshape(B, T, ATT_KV_HEADS, HEAD_DIM)
            v_new = v_new.reshape(B, T, ATT_KV_HEADS, HEAD_DIM)
            if kv_cache_k is None:
                k_all, v_all, keep = k_new, v_new, WINDOW
            else:
                k_all = jnp.concatenate([kv_cache_k.astype(k_new.dtype), k_new], axis=1)
                v_all = jnp.concatenate([kv_cache_v.astype(v_new.dtype), v_new], axis=1)
                keep = kv_cache_k.shape[1]
    y = rmsnorm(x, norm_final)
    return y, jnp.stack(new_gla), k_all[:, -keep:], v_all[:, -keep:], jnp.stack(new_buf)

def setup_inputs(seed: int = 0) -> dict:
    key = jax.random.key(seed)
    ks = jax.random.split(key, 32)
    f32 = jnp.float32

    def nrm(k, shape, scale=1.0):
        return jax.random.normal(k, shape, f32) * scale

    win_rows = min(WINDOW, PAST_LEN)
    return {
        'x_prompt': nrm(ks[0], (BATCH, SEQ, D_MODEL)),
        'x_sample': nrm(ks[1], (DEC_BATCH, DEC_SEQ, D_MODEL)),
        'state_gla': nrm(ks[2], (N_A, DEC_BATCH, GLA_HEADS, GLA_DK, GLA_DV)),
        'cache_k': nrm(ks[3], (DEC_BATCH, win_rows, ATT_KV_HEADS, HEAD_DIM)),
        'cache_v': nrm(ks[4], (DEC_BATCH, win_rows, ATT_KV_HEADS, HEAD_DIM)),
        'state_ffn_conv': nrm(ks[5], (DEPTH, DEC_BATCH, CONV_W - 1, 2 * D_FF)),
        'norm_mix': 1.0 + nrm(ks[6], (DEPTH, D_MODEL), 0.05),
        'norm_ffn': 1.0 + nrm(ks[7], (DEPTH, D_MODEL), 0.05),
        'norm_kv': 1.0 + nrm(ks[8], (D_MODEL,), 0.05),
        'norm_final': 1.0 + nrm(ks[9], (D_MODEL,), 0.05),
        'gla_w_in': nrm(ks[10], (N_A, D_MODEL, GLA_IN), D_MODEL ** -0.5),
        'gla_w_g2': nrm(ks[11], (N_A, GLA_RANK, QK_W), GLA_RANK ** -0.5),
        'gla_b_g2': nrm(ks[12], (N_A, QK_W), 0.1),
        'gla_g_onorm': 1.0 + nrm(ks[13], (N_A, GLA_DV), 0.05),
        'gla_w_out': nrm(ks[14], (N_A, V_W, D_MODEL), V_W ** -0.5),
        'w_kv': nrm(ks[15], (D_MODEL, 2 * KV_W), D_MODEL ** -0.5),
        'att_w_q': nrm(ks[16], (N_B, D_MODEL, ATT_HEADS * HEAD_DIM), D_MODEL ** -0.5),
        'att_sinks': nrm(ks[17], (N_B, ATT_HEADS), 1.0),
        'att_w_o': nrm(ks[18], (N_B, ATT_HEADS * HEAD_DIM, D_MODEL), (ATT_HEADS * HEAD_DIM) ** -0.5),
        'ffn_w_up': nrm(ks[19], (DEPTH, D_MODEL, 2 * D_FF), D_MODEL ** -0.5),
        'ffn_conv_w': nrm(ks[20], (DEPTH, CONV_W, 2 * D_FF), CONV_W ** -0.5),
        'ffn_conv_b': nrm(ks[21], (DEPTH, 2 * D_FF), 0.02),
        'ffn_w_down': nrm(ks[22], (DEPTH, D_FF, D_MODEL), D_FF ** -0.5),
    }

def reference(x_prompt, x_sample, state_gla, cache_k, cache_v, state_ffn_conv, norm_mix, norm_ffn, norm_kv,
              norm_final, gla_w_in, gla_w_g2, gla_b_g2, gla_g_onorm, gla_w_out, w_kv, att_w_q, att_sinks,
              att_w_o, ffn_w_up, ffn_conv_w, ffn_conv_b, ffn_w_down):
    bp = x_prompt.shape[0]
    gla0 = jnp.zeros((N_A, bp, GLA_HEADS, GLA_DK, GLA_DV), jnp.float32)
    buf0 = jnp.zeros((DEPTH, bp, CONV_W - 1, 2 * D_FF), x_prompt.dtype)
    y_prompt, gla_p, k_p, v_p, buf_p = trunk(
        x_prompt, gla0, buf0, None, None, norm_mix, norm_ffn, norm_kv, norm_final,
        gla_w_in, gla_w_g2, gla_b_g2, gla_g_onorm, gla_w_out, w_kv, att_w_q, att_sinks, att_w_o,
        ffn_w_up, ffn_conv_w, ffn_conv_b, ffn_w_down)
    y_sample, gla_s, k_s, v_s, buf_s = trunk(
        x_sample, state_gla, state_ffn_conv, cache_k, cache_v, norm_mix, norm_ffn, norm_kv, norm_final,
        gla_w_in, gla_w_g2, gla_b_g2, gla_g_onorm, gla_w_out, w_kv, att_w_q, att_sinks, att_w_o,
        ffn_w_up, ffn_conv_w, ffn_conv_b, ffn_w_down)
    return (y_prompt, y_sample, gla_p, k_p, v_p, buf_p, gla_s, k_s, v_s, buf_s)


_drawn_inputs = setup_inputs


def setup_inputs(seed=0):
    import zlib

    import numpy as np

    out = dict(_drawn_inputs(seed))
    spreads = {}
    factors = {'att_sinks': 8.0, 'ffn_conv_b': 2.986}
    for name, (base, spread) in spreads.items():
        noise = np.random.default_rng([zlib.crc32(name.encode()), seed]).standard_normal(out[name].shape)
        drawn = base * np.exp(spread * noise) if base else spread * noise
        out[name] = __import__('jax').numpy.asarray(drawn.astype(out[name].dtype))
    for name, factor in factors.items():
        out[name] = (out[name] * factor).astype(out[name].dtype)
    return out
```

```python
from contextlib import ExitStack

import concourse.bass as bass
from concourse import mybir

ALU = mybir.AluOpType
ACT = mybir.ActivationFunctionType
AX = mybir.AxisListType
F32 = mybir.dt.float32
F32R = mybir.dt.float32r
BF16 = mybir.dt.bfloat16

D = 1024
SEQ = 512
NS, SL = 8, 16
T = SEQ + NS * SL
KT = D // 128
TT = T // 128
HALF = T // 2
H, DK, DV, RANK = 4, 128, 256, 16
BLK = 16
GATE = 16.0
DFF = 2816
FT = DFF // 128
NIT = FT // 2
CW = SEQ + 2 + NS * (SL + 2)
CC = CW - 2
NH, HD, KVH, WIN, CH = 16, 64, 2, 128, 64
EPS = 1e-6
MASKED = -1e30


def build(nc, A, O):
    ctx = ExitStack()
    with ctx:
        top = [16512]

        def at(name, shape, dt, offset):
            return nc.alloc_sbuf_tensor_at(name, shape, dt, offset=offset)

        def size(shape, dt):
            n = 2 if dt == BF16 else 4
            for s in shape[1:]:
                n *= s
            return (n + 31) // 32 * 32

        def sb(name, shape, dt=F32):
            o = top[0]
            top[0] += size(shape, dt)
            return at(name, shape, dt, o)

        def area(n):
            o = top[0]
            top[0] += (n + 31) // 32 * 32
            return o

        def sem(name):
            return ctx.enter_context(nc.semaphore(name))

        x_area, xs_area = area(4 * KT * T), area(8 * KT * T)
        X = at("x_res", [128, KT, T], F32, x_area)
        XH = at("x_hi", [128, KT, T], F32R, xs_area)
        XL = at("x_lo", [128, KT, T], F32R, xs_area + 4 * KT * T)
        WRAW = sb("w_raw", [128, 2, KT, 256])
        DRAW_AREA = top[0]
        DRAW = sb("d_raw", [128, 2, D])
        WH = sb("w_hi", [128, 4, KT, 128], F32R)
        WL = sb("w_lo", [128, 4, KT, 128], F32R)
        d_area = area(4 * 4 * D)
        DH = at("d_hi", [128, 2, D], F32R, d_area)
        DL = at("d_lo", [128, 2, D], F32R, d_area + 8 * D)
        e_area = area(12 * KT * T)
        ident = sb("ident", [128, 128])
        ones = sb("ones", [128, 128])
        RB = sb("rstd_cols", [128, T])
        RT = sb("rstd_rows", [128, TT])
        SS = sb("sum_sq", [128, T])
        NVEC = 54
        NW = sb("vectors", [128, NVEC])
        CWT = sb("conv_taps", [128, 4, 2 * FT])
        KTK = sb("keys_rows", [128, 4, 128])
        m_area = area(2048)
        MPR = at("masked_scores", [128, 512], F32, m_area)
        AT = sb("scores", [128, 2, 128])
        ST = sb("gla_state", [128, DV])
        DEC = sb("decay", [128, 2, 12])
        JNK = sb("unused_out", [128, DV], BF16)
        SSH = sb("head_sq", [128, 20])
        RH = sb("head_rstd", [128, 20])
        EO = sb("even_odd", [128, 2])
        HB = sb("head_bands", [128, NH])
        SKB = sb("sinks_by_head", [128, NH])
        SKT = sb("sinks_banded", [128, NH])
        SKR = sb("sinks_rows", [128, KVH])
        NM = sb("neg_max", [128, 2, 2])
        SE = sb("sink_exp", [128, 2, 2])
        ES = sb("exp_sum", [128, 2, 2])
        assert top[0] <= 229344, top[0]

        QK = at("kq_cols", [128, 2 * H, T], F32, e_area)
        V = at("v_rows", [128, TT, H * DV], F32, e_area + 4 * KT * T)
        RS = at("r_rows", [128, TT, H * DV], F32, e_area + 8 * KT * T)
        XIN = at("x_in", [128, TT, D], F32, e_area + 4 * KT * T)
        AB = at("gate_tail", [128, H, T], F32, e_area + 8 * KT * T)
        NRAW = at("vectors_raw", [NVEC, 128], F32, e_area)
        SQ = at("squares", [128, 2, T], F32, e_area + 12 * KT * T - 8 * T)
        GLS = at("gate_low", [128, T], F32, d_area)
        G2 = at("gate_up", [128, H * DK], F32, d_area + 4 * T)
        QI = at("q_inter", [128, 2, SEQ], F32, d_area)
        QM = at("q_by_seq", [128, NS * 128], F32, d_area + 4096)
        S0 = at("seq_states", [128, NS, DV], F32, d_area + 8192)
        LA = at("log_gate", [128, H, T], F32, x_area)
        M16 = at("carry16", [128, T], BF16, x_area + 4 * H * T)
        M128 = at("carry128", [128, T], BF16, x_area + 4 * H * T + 2 * T)
        B16 = at("cum16", [128, T], F32, x_area + 4 * H * T + 4 * T)
        B128 = at("cum128", [128, T], F32, x_area + 4 * H * T + 8 * T)
        MASK = at("score_mask", [128, 4, 128], F32, x_area + 4 * H * T + 12 * T)
        SW = 2 * T + 6 * SEQ + T
        SET = at("gla_operands", [128, 2, SW], F32, xs_area)

        def qd(s): return SET[:, s, 0:T]
        def kd(s): return SET[:, s, T:2 * T]
        def ql(s, l): return SET[:, s, 2 * T + (l - 1) * SEQ:2 * T + l * SEQ]
        def kl(s, l): return SET[:, s, 2 * T + (l + 2) * SEQ:2 * T + (l + 3) * SEQ]
        def kr(s): return SET[:, s, 2 * T + 6 * SEQ:SW]

        fo = [e_area]

        def fb(name, shape, dt=F32):
            o = fo[0]
            fo[0] += size(shape, dt)
            assert fo[0] <= e_area + 12 * KT * T - 8 * T
            return at(name, shape, dt, o)

        UB = fb("up_rows", [128, 4, CW])
        CB = fb("conv_out", [128, 4, CC])
        Y = fb("gated", [128, 2, T])
        YH = fb("gated_hi", [128, 2, T], F32R)
        YL = fb("gated_lo", [128, 2, T], F32R)
        TLC = fb("tail_cols", [128, NIT, 4, 18])
        TLR = fb("tail_rows", [72, NIT, 128])
        STR = fb("conv_state", [64, NIT, 128])
        STC = fb("conv_state_cols", [128, NIT, 64])
        CRAW = fb("taps_raw", [2 * FT, 4, 128])

        KCR = at("cache_k_rows", [128, NS, KVH, 2, HD], F32, e_area)
        P = at("probs", [128, 2, 512], F32, e_area)
        PT = at("probs_cols", [128, 2, 512], F32, e_area + 4096)
        KTD = at("keys_cols", [128, KVH, SEQ], F32, e_area + 8192)
        VZ = at("v_0_v", [128, TT - 1, KVH, 3 * HD], F32, e_area + 12288)
        QZ = at("q_0_q", [128, NS, KVH, 2, 4, SL], F32, e_area + 18432)
        KCT = at("seq_keys_cols", [128, KVH, NS, WIN + SL], F32, e_area + 26624)
        QF = at("q_cols", [128, KT, T], F32, e_area + 35840)
        KD = at("keys_twice", [128, TT, KVH, 2, HD], F32, d_area)
        V4 = at("v_new_rows", [128, KVH, 2, HD], F32, d_area + 5120)
        VN = at("v_new", [SL, NS, KVH, 2, HD], F32, d_area + 6144)
        VCD = at("cache_v", [128, NS, KVH, 2, HD], F32, DRAW_AREA)
        QMI = at("query_chunk", [2, 128], BF16, m_area)
        KMI = at("key_chunk", [2, 256], BF16, m_area + 256)
        NFB = at("norm_final_rows", [128, D], F32, xs_area + 4 * KT * T)
        YO = at("y_rows", [128, TT, D], F32, xs_area)

        PS = ctx.enter_context(nc.psum_tensor("ps", [128, 8, 512], F32))
        XSP = nc.dram_tensor("x_spill", [128, KT, T], F32, kind="Internal").ap()

        s_const = sem("s_const")
        s_xin = sem("s_xin")
        s_raw = [sem("s_raw0"), sem("s_raw1")]
        s_draw = sem("s_draw")
        s_setup = sem("s_setup")
        full = sem("full")
        free = sem("free")
        hi_done = sem("hi_done")
        lo_done = sem("lo_done")
        dhi = sem("dhi")
        dlo = sem("dlo")
        xh_done = sem("xh_done")
        xl_done = sem("xl_done")
        sq_done = sem("sq_done")
        ss_done = sem("ss_done")
        rt_sq = sem("rt_sq")
        rstd = sem("rstd")
        s_spill = sem("s_spill")
        s_g2 = sem("s_g2")
        s_mask = sem("s_mask")
        rt_h = sem("rt_h")
        cum = sem("cum")
        prod = sem("prod")
        s_xback = sem("s_xback")
        dve = sem("dve")
        s_mn = sem("s_mn")
        s_la = sem("s_la")
        args = sem("args")
        exps = sem("exps")
        prep = sem("prep")
        zset = sem("zset")
        tr_full = sem("tr_full")
        kt_done = sem("kt_done")
        sc_full = sem("sc_full")
        att = sem("att")
        o_full = sem("o_full")
        osq = sem("osq")
        og = sem("og")
        st_full = sem("st_full")
        st_done = sem("st_done")
        s_s0 = sem("s_s0")
        s_sout = sem("s_sout")
        s_pout = sem("s_pout")
        ogn = sem("ogn")
        t0_done = sem("t0_done")
        conv = sem("conv")
        silu = sem("silu")
        y_done = sem("y_done")
        yh = sem("yh")
        yl = sem("yl")
        st_c = sem("st_c")
        tl_g = sem("tl_g")
        s_str = sem("s_str")
        s_tout = sem("s_tout")
        s_out = sem("s_out")
        s_sink = sem("s_sink")
        s_cache = sem("s_cache")
        s_vn = sem("s_vn")
        s_nfb = sem("s_nfb")
        s_y = sem("s_y")
        azero = sem("azero")
        sink_v = sem("sink_v")
        qz = sem("qz")
        a_sc = sem("a_sc")
        a_chain = sem("a_chain")
        a_sum = sem("a_sum")
        a_nm = sem("a_nm")
        a_ex = sem("a_ex")
        a_p = sem("a_p")
        a_tr = sem("a_tr")
        a_pt = sem("a_pt")
        a_o = sem("a_o")
        a_oh = sem("a_oh")
        a_ol = sem("a_ol")

        T_GL, T_KQ, T_V, T_R, T_WO = 0, 2, 10, 18, 26
        T_F = [34, 96]
        T_KV, T_AQ, T_AO = 78, 80, 88
        w_in = A["gla_w_in"][0]
        pieces = [(w_in, 2 * H * DK + 2 * H * DV + RANK - 256)]
        pieces += [(w_in, H * DK + 256 * n) for n in range(2)] + [(w_in, 256 * n) for n in range(2)]
        pieces += [(w_in, 2 * H * DK + 256 * n) for n in range(8)]
        pieces += [(A["gla_w_out"][0], 256 * n) for n in range(4)]
        later = {T_KV // 2: (A["w_kv"], 0)}
        later.update({T_AQ // 2 + n: (A["att_w_q"][0], 256 * n) for n in range(4)})
        later.update({T_AO // 2 + n: (A["att_w_o"][0], 256 * n) for n in range(4)})
        U_C, U_X, U_GL, U_KQ, U_Z, U_V, U_R = 0, 1, 9, 12, 20, 24, 40
        U_OT, U_WO = 56, 61
        FFN_UNITS = 6 + 12 * (NIT - 1) + 2 + KT
        U_KV = 69 + FFN_UNITS
        U_KT, U_Q, U_KC = U_KV + 6, U_KV + 8, U_KV + 16
        U_AO = U_KC + 2
        U_F = [69, U_AO + KT]
        U_Y = U_F[1] + FFN_UNITS
        XF = [KT + TT, KT + TT + 3 * KT]
        XLF = [KT, 4 * KT]
        NORM_F = [1, 3]
        RC = [0, 2, 3, 5, 6]
        STATS_READ = [0, U_GL + 3, U_F[0] + 3, U_KV + 3, U_F[1] + 3]
        GO = [TT - 1] + list(range(TT - 1))
        STEPS = H * TT
        TMU = [[0], [1], [2, 3], [4]]
        NATT = (TT - 1) * KT + NS
        V_MIX, V_FFN, V_KV, V_FIN, V_ON, V_BG = 0, 16, 32, 40, 48, 50

        def unit(u, n=HALF):
            return PS[:, 2 * (u % 4):2 * (u % 4) + 2, 0:n]

        def halves(ap):
            return ap.rearrange("p (a b) -> p a b", a=2)

        def f32(ap):
            return ap.bitcast(F32)

        def round_tile(act, n0, i=0):
            p0 = n0 // 2
            act.wait_ge(s_raw[p0 % 2], 16 * (p0 // 2 + 1) + 16 * i)
            half = (n0 % 2) * 128
            act.activation(WH[:, n0 % 4, :, :], WRAW[:, p0 % 2, :, half:half + 128],
                           ACT.Copy).then_inc(hi_done, 1)

        def rest_tile(v, n0, i=0):
            p0 = n0 // 2
            half = (n0 % 2) * 128
            v.wait_ge(hi_done, n0 + 1 + 4 * i)
            v.tensor_tensor(WL[:, n0 % 4, :, :], WRAW[:, p0 % 2, :, half:half + 128],
                            f32(WH[:, n0 % 4, :, :]), ALU.subtract).then_inc(lo_done, 1)

        def fm_tile(pe, n0, u0, i=0, wstep=4, ustep=4, fresh=None, beside=None):
            pe.wait_ge(lo_done, n0 + 1 + wstep * i)
            if u0 >= 4:
                pe.wait_ge(free, u0 - 3 + ustep * i)
            for k in range(KT):
                if fresh is not None:
                    pe.wait_ge(xl_done, fresh + k + 1)
                for a, (w, x) in enumerate(((WH, XH), (WH, XL), (WL, XH))):
                    for f in range(2):
                        mm = pe.matmul(PS[:, 2 * (u0 % 4) + f, 0:HALF], w[:, n0 % 4, k, :],
                                       x[:, k, f * HALF:(f + 1) * HALF],
                                       start=(k == 0 and a == 0), stop=(k == KT - 1 and a == 2))
            if beside is not None:
                mm = beside()
            mm.then_inc(full, 1)

        def tm_unit(pe, n0, u0, groups, i=0):
            pe.wait_ge(lo_done, n0 + 2 + 4 * i)
            pe.wait_ge(free, u0 - 3 + 8 * i)
            for f, t in enumerate(groups):
                for k in range(KT):
                    for a, (x, w) in enumerate(((XH, WH), (XH, WL), (XL, WH))):
                        mm = pe.matmul(PS[:, 2 * (u0 % 4) + f, 0:256], x[:, k, 128 * t:128 * t + 128],
                                       w[:, n0 % 4:n0 % 4 + 2, k, :],
                                       start=(k == 0 and a == 0), stop=(k == KT - 1 and a == 2))
            mm.then_inc(full, 1)

        def stat_cols(pe, u, norm):
            pe.wait_ge(ss_done, (KT + 1) * (norm + 1))
            pe.wait_ge(free, u - 3)
            for f in range(2):
                mm = pe.matmul(PS[:, 2 * (u % 4) + f, 0:HALF], ones[:, :], SS[:, f * HALF:(f + 1) * HALF],
                               start=True, stop=True)
            mm.then_inc(full, 1)

        def stat_rows(pe, u):
            pe.wait_ge(free, u - 3)
            for t in range(TT):
                mm = pe.matmul(PS[:, 2 * (u % 4), t:t + 1], SS[:, 128 * t:128 * t + 128], ones[:, 0:1],
                               start=True, stop=True)
            mm.then_inc(full, 1)

        def roots(act, u, norm, rows):
            act.wait_ge(full, u + 1)
            act.activation(halves(RB[:, :]), unit(u), ACT.Sqrt, bias=eps[:, 0:1], scale=1.0 / D).then_inc(rt_sq, 1)
            if rows:
                act.wait_ge(full, u + 2)
                act.activation(RT[:, :], PS[:, 2 * ((u + 1) % 4), 0:TT], ACT.Sqrt, bias=eps[:, 0:1],
                               scale=1.0 / D).then_inc(rt_sq, 1)

        eps = EPSC = sb("eps", [128, 1])
        EV = sb("bands", [128, 4])
        assert top[0] <= 229344, top[0]

        def invert(v, count, rows):
            v.wait_ge(rt_sq, count + 1)
            v.reciprocal(RB[:, :], RB[:, :]).then_inc(rstd, 1)
            if rows:
                v.wait_ge(rt_sq, count + 2)
                v.reciprocal(RT[:, :], RT[:, :]).then_inc(rstd, 1)

        def round_x(act, k, vec):
            act.activation(XH[:, k, :], X[:, k, :], ACT.Copy, scale=NW[:, vec + k:vec + k + 1]).then_inc(xh_done, 1)

        def rest_x(v, k, vec, base):
            v.wait_ge(xh_done, base + k + 1)
            v.scalar_tensor_tensor(out=XL[:, k, :], in0=X[:, k, :], scalar=NW[:, vec + k:vec + k + 1],
                                   in1=f32(XH[:, k, :]), op0=ALU.mult, op1=ALU.subtract).then_inc(xl_done, 1)

        def square_x(act, k, norm, k2=None, i=0):
            n = KT * norm + k
            if n >= 2:
                act.wait_ge(ss_done, (KT + 1) * norm + k + 4 * i)
            x = X[:, k, :] if k2 is None else X[:, bass.ds(k2, 1), :].rearrange("p a t -> p (a t)")
            act.activation(SQ[:, k % 2, :], x, ACT.Square).then_inc(sq_done, 1)

        def clear_sums(pool, norm):
            if norm:
                pool.wait_ge(full, STATS_READ[norm])
            pool.memset(SS[:, :], 0.0).then_inc(ss_done, 1)

        def add_squares(pool, k, norm, i=0):
            n = (KT + 1) * norm + k
            pool.wait_ge(sq_done, KT * norm + k + 1 + 4 * i)
            pool.wait_ge(ss_done, n + 1 + 4 * i)
            pool.tensor_tensor(SS[:, :], SS[:, :], SQ[:, k % 2, :], ALU.add).then_inc(ss_done, 1)

        def add_x(v, m, u0, i=0, ustep=12, inc=1):
            v.wait_ge(full, u0 + 1 + ustep * i)
            v.tensor_tensor(halves(X[:, m, :]), halves(X[:, m, :]), unit(u0), ALU.add).then_inc(free, inc)

        def fu(i0):
            return 0 if i0 == 0 else 6 + 12 * (i0 - 1)

        def fpos(first):
            return ([1, 3], None, [4, 5]) if first else ([0, 1], list(range(2, 10)), [10, 11])

        TAILS = (range(6), range(6, NIT))

        def ffn_pe(pe, L):
            t0, u0 = T_F[L], U_F[L]

            def up(js, us, base, i0, i, first):
                for j, u in zip(js, us):
                    fm_tile(pe, t0 + 4 * i0 + j, u0 + base + u, i, 4, 12, fresh=XLF[L] if first and j == 0 else None)
                    if first and j == 0:
                        stat_cols(pe, u0 + 2, NORM_F[L])

            def down(base, us, i0, i):
                for m, u in enumerate(us):
                    w = u0 + base + u
                    if m == 0:
                        pe.wait_ge(yl, 2 * (NIT * L + i0) + 2 + 2 * i)
                    pe.wait_ge(dlo, 4 * (NIT * L + i0) + m // 2 + 1 + 4 * i)
                    pe.wait_ge(free, w - 3 + 12 * i)
                    for k in range(2):
                        for a, (wt, y) in enumerate(((DH, YH), (DH, YL), (DL, YH))):
                            for f in range(2):
                                mm = pe.matmul(PS[:, 2 * (w % 4) + f, 0:HALF], wt[:, k, 128 * m:128 * m + 128],
                                               y[:, k, f * HALF:(f + 1) * HALF],
                                               start=(k == 0 and a == 0), stop=(k == 1 and a == 2))
                    mm.then_inc(full, 1)

            def step(i0, i, first=False):
                gu, du, vu = fpos(first)
                b = fu(i0)
                up([0, 1], gu, b, i0, i, first)
                if du:
                    down(b, du, i0 - 1, i)
                up([2, 3], vu, b, i0, i, first)

            pe.wait_ge(s_str, 96 * (L + 1))
            pe.wait_ge(free, u0 - 3)
            for n in range(NIT):
                b = 2 * (u0 % 4) + n // 8
                pe.transpose(PS[:, b, 64 * (n % 8):64 * (n % 8) + 64], STR[:, n, :], ident[0:64, 0:64])
            for c in range(4):
                o = 64 * (NIT - 8) + 2 * FT * c
                mm = pe.transpose(PS[:, b, o:o + 2 * FT], CRAW[:, c, :], ident[0:2 * FT, 0:2 * FT])
            mm.then_inc(full, 1)
            step(0, 0, True)
            with pe.Fori(0, NIT - 2) as i:
                step(1, i)
            step(NIT - 1, 0)
            pe.wait_ge(tl_g, 2 * NIT * (L + 1))
            for q, ns in enumerate(TAILS):
                u = u0 + fu(NIT - 1) + 12 + q
                pe.wait_ge(free, u - 3)
                for j, n in enumerate(ns):
                    mm = pe.transpose(PS[0:72, 2 * (u % 4) + j // 4, 128 * (j % 4):128 * (j % 4) + 128],
                                      TLC[:, n, :, :].rearrange("p a b -> p (a b)"), ident[:, :])
                mm.then_inc(full, 1)
            down(fu(NIT - 1) + 14, range(8), NIT - 1, 0)

        def ffn_dve(v, L, last, nextvec, nextx):
            t0, u0 = T_F[L], U_F[L]

            def evac(j, u, i, i0, first):
                w = u0 + u
                if first and j == 0:
                    invert(v, RC[NORM_F[L]], False)
                    v.wait_ge(rstd, RC[NORM_F[L]] + 1)
                    inc = 2
                else:
                    inc = 1
                v.wait_ge(full, w + 1 + 12 * i)
                if j == 0 and not first:
                    v.wait_ge(tl_g, 2 * (NIT * L + i0) + 2 * i)
                if j == 0:
                    v.tensor_copy(UB[:, :, SEQ + 2:CW].rearrange("p a (s c) -> p a s c", s=NS)[:, :, :, 0:2],
                                  STC[:, bass.ds(i0 + i, 1), :].rearrange("p o (a s r) -> p (o a) s r", a=4, s=NS))
                b = 2 * (w % 4)
                nb = SEQ - HALF
                v.tensor_tensor(UB[:, j, 2:2 + HALF], PS[:, b, 0:HALF], RB[:, 0:HALF], ALU.mult)
                v.tensor_tensor(UB[:, j, 2 + HALF:2 + SEQ], PS[:, b + 1, 0:nb], RB[:, HALF:SEQ], ALU.mult)
                v.tensor_tensor(UB[:, j, SEQ + 2:CW].rearrange("p (s c) -> p s c", s=NS)[:, :, 2:2 + SL],
                                PS[:, b + 1, nb:HALF].rearrange("p (s c) -> p s c", s=NS),
                                RB[:, SEQ:T].rearrange("p (s c) -> p s c", s=NS), ALU.mult).then_inc(free, inc)

            def tile_col(j, i0, i):
                return (FT if j >= 2 else 0) + j % 2 + 2 * i0 + 2 * i

            def conv_taps(j, i0, i):
                c = tile_col(j, i0, i)
                n = 4 * (NIT * L + i0) + j
                v.wait_ge(t0_done, n + 1 + 4 * i)
                v.scalar_tensor_tensor(out=CB[:, j, :], in0=UB[:, j, 1:1 + CC], scalar=CWT[:, 1, bass.ds(c, 1)],
                                       in1=CB[:, j, :], op0=ALU.mult, op1=ALU.add).then_inc(conv, 1)
                v.wait_ge(conv, 2 * n + 1 + 8 * i)
                v.scalar_tensor_tensor(out=CB[:, j, :], in0=UB[:, j, 2:2 + CC], scalar=CWT[:, 2, bass.ds(c, 1)],
                                       in1=CB[:, j, :], op0=ALU.mult, op1=ALU.add).then_inc(conv, 1)

            def gate(j, i0, i):
                n = 2 * (NIT * L + i0) + j
                v.wait_ge(silu, n + 1 + 2 * i)
                v.wait_ge(conv, 8 * (NIT * L + i0) + 2 * (j + 2) + 2 + 8 * i)
                v.tensor_tensor(Y[:, j, 0:SEQ], CB[:, j, 0:SEQ], CB[:, 2 + j, 0:SEQ], ALU.mult)
                a = CB[:, j, SEQ:CC].rearrange("p (s c) -> p s c", s=NS)[:, :, 2:2 + SL]
                b = CB[:, 2 + j, SEQ:CC].rearrange("p (s c) -> p s c", s=NS)[:, :, 2:2 + SL]
                v.tensor_tensor(Y[:, j, SEQ:T].rearrange("p (s c) -> p s c", s=NS), a, b, ALU.mult).then_inc(y_done, 1)

            def rest_y(j, i0, i):
                n = 2 * (NIT * L + i0) + j
                v.wait_ge(yh, n + 1 + 2 * i)
                v.tensor_tensor(YL[:, j, :], Y[:, j, :], f32(YH[:, j, :]), ALU.subtract).then_inc(yl, 1)

            def rest_down(c, i0, i):
                v.wait_ge(dhi, 4 * (NIT * L + i0) + c + 1 + 4 * i)
                v.tensor_tensor(DL[:, :, 256 * c:256 * c + 256], DRAW[:, :, 256 * c:256 * c + 256],
                                f32(DH[:, :, 256 * c:256 * c + 256]), ALU.subtract).then_inc(dlo, 1)

            def step(i0, i, first=False, ahead=True):
                gu, du, vu = fpos(first)
                b = fu(i0)
                for j, u in zip((0, 1), gu):
                    evac(j, b + u, i, i0, first)
                    if ahead:
                        rest_tile(v, t0 + 4 * i0 + j + 4, i)
                    conv_taps(j, i0, i)
                if du:
                    for m, u in enumerate(du):
                        add_x(v, m, u0 + b + u, i)
                        if m % 2:
                            rest_down(m // 2, i0, i)
                else:
                    for c in range(4):
                        rest_down(c, i0, i)
                for j, u in zip((2, 3), vu):
                    evac(j, b + u, i, i0, first)
                    if ahead:
                        rest_tile(v, t0 + 4 * i0 + j + 4, i)
                    if j == 3:
                        rest_y(0, i0, i)
                    conv_taps(j, i0, i)
                    gate(j - 2, i0, i)
                rest_y(1, i0, i)

            v.memset(UB[:, :, 0:2], 0.0)
            v.wait_ge(full, u0 + 1)
            b = 2 * (u0 % 4)
            v.tensor_copy(STC[:, 0:8, :].rearrange("p n c -> p (n c)"), PS[:, b, :])
            v.tensor_copy(STC[:, 8:NIT, :].rearrange("p n c -> p (n c)"), PS[:, b + 1, 0:64 * (NIT - 8)]).then_inc(st_c, 1)
            v.tensor_copy(CWT[:, :, :].rearrange("p c t -> p (c t)"),
                          PS[:, b + 1, 64 * (NIT - 8):64 * (NIT - 8) + 8 * FT]).then_inc(free, 1)
            v.wait_ge(st_c, L + 1)
            step(0, 0, True)
            with v.Fori(0, NIT - 2) as i:
                step(1, i)
            step(NIT - 1, 0, ahead=not last)
            b = fu(NIT - 1) + 14
            for q, ns in enumerate(TAILS):
                u = u0 + b - 2 + q
                v.wait_ge(full, u + 1)
                o = TLR[:, ns[0]:ns[-1] + 1, :].rearrange("p n c -> p (n c)")
                v.tensor_copy(o[:, 0:512], PS[0:72, 2 * (u % 4), :])
                v.tensor_copy(o[:, 512:128 * len(ns)], PS[0:72, 2 * (u % 4) + 1, 0:128 * len(ns) - 512]).then_inc(free, 1)
            for m in range(8):
                add_x(v, m, u0 + b + m)
                if m and nextvec is not None:
                    rest_x(v, m - 1, nextvec, nextx)
            if nextvec is not None:
                rest_x(v, 7, nextvec, nextx)

        def ffn_act(act, L, last, nextvec, nextnorm):
            t0, u0 = T_F[L], U_F[L]

            def tap0(j, i0, i, w):
                c = (FT if j >= 2 else 0) + j % 2 + 2 * i0 + 2 * i
                act.wait_ge(free, w + 1 + 12 * i)
                act.activation(CB[:, j, :], UB[:, j, 0:CC], ACT.Identity, scale=CWT[:, 0, bass.ds(c, 1)],
                               bias=CWT[:, 3, bass.ds(c, 1)]).then_inc(t0_done, 1)

            def do_silu(j, i0, i):
                act.wait_ge(conv, 8 * (NIT * L + i0) + 2 * j + 2 + 8 * i)
                act.activation(CB[:, j, :], CB[:, j, :], ACT.Silu).then_inc(silu, 1)

            def round_y(j, i0, i):
                act.wait_ge(y_done, 2 * (NIT * L + i0) + j + 1 + 2 * i)
                act.activation(YH[:, j, :], Y[:, j, :], ACT.Copy).then_inc(yh, 1)

            def round_down(c, i0, i):
                act.activation(DH[:, :, 256 * c:256 * c + 256], DRAW[:, :, 256 * c:256 * c + 256],
                               ACT.Copy).then_inc(dhi, 1)

            def step(i0, i, first=False, ahead=True):
                gu, du, vu = fpos(first)
                b = fu(i0)
                n = NIT * L + i0
                for j, u in zip((0, 1), gu):
                    w = u0 + b + u
                    if first and j == 0:
                        roots(act, u0 + 2, NORM_F[L], False)
                    if ahead:
                        act.wait_ge(full, w + 1 + 12 * i)
                        round_tile(act, t0 + 4 * i0 + j + 4, i)
                    if j == 1:
                        do_silu(0, i0, i)
                    tap0(j, i0, i, w)
                do_silu(1, i0, i)
                for c in range(4):
                    if c == 0:
                        act.wait_ge(s_draw, 16 * (n + 1) + 16 * i)
                    if du:
                        act.wait_ge(full, u0 + b + du[2 * c + 1] + 1 + 12 * i)
                    round_down(c, i0, i)
                for j, u in zip((2, 3), vu):
                    w = u0 + b + u
                    if ahead:
                        act.wait_ge(full, w + 1 + 12 * i)
                        round_tile(act, t0 + 4 * i0 + j + 4, i)
                    if j == 3:
                        round_y(0, i0, i)
                    tap0(j, i0, i, w)
                round_y(1, i0, i)

            step(0, 0, True)
            with act.Fori(0, NIT - 2) as i:
                step(1, i)
            step(NIT - 1, 0, ahead=not last)
            b = fu(NIT - 1) + 14
            for m in range(8):
                act.wait_ge(free, u0 + b + m + 1)
                if nextvec is not None:
                    round_x(act, m, nextvec)
                square_x(act, m, nextnorm)

        def ffn_pool(pool, L):
            u0 = U_F[L]

            def gather(jj, w, i0, i):
                pool.wait_ge(free, w + 1 + 12 * i)
                a = slice(2 * jj, 2 * jj + 2)
                to = TLC[:, bass.ds(i0 + i, 1), a, :].rearrange("p o a c -> p (o a) c")
                pool.tensor_tensor(to[:, :, 0:2], UB[:, a, SEQ:SEQ + 2],
                                   ones[:, 0:4].rearrange("p (a r) -> p a r", a=2), ALU.mult)
                pool.tensor_tensor(to[:, :, 2:18].rearrange("p a (s r) -> p a s r", s=NS),
                                   UB[:, a, SEQ + 2:CW].rearrange("p a (s c) -> p a s c", s=NS)[:, :, :, SL:SL + 2],
                                   ones[:, 0:4 * NS].rearrange("p (a s r) -> p a s r", a=2, s=NS), ALU.mult)\
                    .then_inc(tl_g, 1)

            def step(i0, i, first=False):
                gu, du, vu = fpos(first)
                b = fu(i0)
                gather(0, u0 + b + gu[1], i0, i)
                gather(1, u0 + b + vu[1], i0, i)

            step(0, 0, True)
            with pool.Fori(0, NIT - 2) as i:
                step(1, i)
            step(NIT - 1, 0)

        def conv_loads(sp, L):
            for j in range(4):
                src = A["state_ffn_conv"][L].rearrange("s r (h n two c) -> (s r) h n two c", h=2, two=2, c=128)
                sp.dma_start(STR[16 * j:16 * j + 16, :, :], src[:, j // 2, :, j % 2, :]).then_inc(s_str, 16)
            sp.dma_start(CRAW[:, 0:3, :], A["ffn_conv_w"][L].rearrange("c (t p) -> t c p", p=128)).then_inc(s_str, 16)
            sp.dma_start(CRAW[:, 3, :], A["ffn_conv_b"][L].rearrange("(t p) -> t p", p=128)).then_inc(s_str, 16)

        def tail_stores(sp, L):
            sp.wait_ge(free, U_F[L] + fu(NIT - 1) + 14)
            for j in range(4):
                for o, r in ((O["conv_p"][L, 0], slice(18 * j, 18 * j + 2)),
                             (O["conv_s"][L].rearrange("s r c -> (s r) c"), slice(18 * j + 2, 18 * j + 18))):
                    sp.dma_start(o.rearrange("r (h n two c) -> r h n two c", h=2, two=2, c=128)[:, j // 2, :, j % 2, :],
                                 TLR[r, :, :]).then_inc(s_tout, 16)

        def ffn_sp(sp, L):
            t0 = T_F[L]

            def step(i0, i):
                for q in range(2):
                    p0 = t0 // 2 + 2 * i0 + q
                    sp.wait_ge(lo_done, 2 * p0 - 2 + 4 * i)
                    src = A["ffn_w_up"][L].rearrange("(k p) n -> p k n", p=128)
                    sp.dma_start(WRAW[:, p0 % 2, :, :], src[:, :, bass.ds(q * DFF + 256 * i0 + 256 * i, 256)])\
                        .then_inc(s_raw[p0 % 2], 16)
                n = NIT * L + i0
                if n:
                    sp.wait_ge(dlo, 4 * n + 4 * i)
                sp.dma_start(DRAW[:, :, :], A["ffn_w_down"][L].rearrange("(t p) n -> p t n", p=128)
                             [:, bass.ds(2 * i0 + 2 * i, 2), :]).then_inc(s_draw, 16)
            step(0, 0)
            with sp.Fori(0, NIT - 1) as i:
                step(1, i)

        def later_piece(sp, p):
            w, c = later[p]
            sp.wait_ge(lo_done, 2 * p - 2)
            sp.dma_start(WRAW[:, p % 2, :, :], w.rearrange("(k p) n -> p k n", p=128)[:, :, c:c + 256])\
                .then_inc(s_raw[p % 2], 16)

        def att_sp(sp):
            for p in (T_KV // 2, T_AQ // 2):
                later_piece(sp, p)
            tail_stores(sp, 0)
            sp.wait_ge(free, U_KV)
            sp.wait_ge(s_tout, 128)
            for dup in range(2):
                for g in range(KVH):
                    sp.dma_start(KCR[:, :, g, dup, :], A["cache_k"][:, :, g, :].rearrange("s k d -> k s d")).then_inc(s_cache, 16)
                    sp.dma_start(VCD[:, :, g, dup, :], A["cache_v"][:, :, g, :].rearrange("s k d -> k s d")).then_inc(s_cache, 16)
            later_piece(sp, T_AQ // 2 + 1)
            sp.wait_ge(free, U_KT)
            for s in range(NS):
                r = slice(SL * s, SL * s + SL)
                sp.dma_start(VN[:, s], V4[r]).then_inc(s_vn, 16)
                sp.dma_start(O["k_s"][s, WIN - SL:WIN], KD[r, TT - 1, :, 0, :]).then_inc(s_out, 16)
                sp.dma_start(O["v_s"][s, WIN - SL:WIN], V4[r, :, 0, :]).then_inc(s_out, 16)
            sp.dma_start(O["k_p"][0], KD[:, TT - 2, :, 0, :]).then_inc(s_out, 16)
            sp.dma_start(O["v_p"][0], VZ[:, TT - 2, :, 0:HD]).then_inc(s_out, 16)
            for p in range(T_AQ // 2 + 2, T_AO // 2 + 4):
                later_piece(sp, p)
            sp.wait_ge(a_o, NATT)
            sp.wait_ge(s_out, 16 * N_OUT)
            conv_loads(sp, 1)

        def att_pool(pool):
            pool.wait_ge(free, U_KV)
            pool.wait_ge(s_tout, 128)
            pool.memset(QZ[:, :, :, :, :, :], 0.0).then_inc(azero, 1)
            pool.memset(VZ[:, :, :, HD:2 * HD], 0.0).then_inc(azero, 1)
            pool.memset(KMI[:, :], MASKED).then_inc(azero, 1)
            pool.memset(QMI[:, :], 1.0).then_inc(azero, 1)
            pool.wait_ge(azero, 7)
            q2 = QMI[:, :].rearrange("p (e q) -> p e q", e=2)
            pool.affine_select(out=q2, in_=q2, compare_op=ALU.is_equal, fill=0.0, base=0,
                               pattern=[[-1, 2], [0, CH]], channel_multiplier=1).then_inc(azero, 1)
            k2 = KMI[:, :].rearrange("p (b k) -> p b k", k=CH)
            pool.affine_select(out=k2, in_=k2, compare_op=ALU.is_equal, fill=0.0, base=3,
                               pattern=[[-1, 4], [0, CH]], channel_multiplier=-3).then_inc(azero, 1)

        N_OUT = 2 + 2 * NS + 2
        KV_UNITS = [0, 3, 4, 5]

        def att_pe(pe):
            pe.wait_ge(xl_done, 3 * KT)
            tm_unit(pe, T_KV, U_KV, TMU[0])
            stat_cols(pe, U_KV + 1, 2)
            stat_rows(pe, U_KV + 2)
            for j in range(1, 4):
                tm_unit(pe, T_KV, U_KV + KV_UNITS[j], TMU[j])
            pe.wait_ge(free, U_KT)
            for g in range(KVH):
                u = U_KT + g
                pe.wait_ge(free, u - 3)
                for t in range(TT):
                    mm = pe.transpose(PS[:, 2 * (u % 4) + t // 4, 128 * (t % 4):128 * (t % 4) + 128],
                                      KD[:, t, g, :, :].rearrange("p a d -> p (a d)"), ident[:, :])
                mm.then_inc(full, 1)
            fm_tile(pe, T_AQ, U_Q, fresh=3 * KT)
            for j in range(1, 4):
                fm_tile(pe, T_AQ + j, U_Q + j)
            for j in range(4, 8):
                fm_tile(pe, T_AQ + j, U_Q + j)
            pe.wait_ge(s_cache, 16 * 8)
            for g in range(KVH):
                u = U_KC + g
                pe.wait_ge(free, u - 3)
                for s in range(NS):
                    mm = pe.transpose(PS[:, 2 * (u % 4) + s // 4, 128 * (s % 4):128 * (s % 4) + 128],
                                      KCR[:, s, g, :, :].rearrange("p a d -> p (a d)"), ident[:, :])
                mm.then_inc(full, 1)
            pe.wait_ge(free, U_AO)
            pe.wait_ge(azero, 9)

            def scores(n):
                if n >= 2:
                    pe.wait_ge(a_ex, n - 1)
                b = n % 2
                if n < NATT - NS:
                    t, m = n // KT, n % KT
                    g = m // 4
                    c = slice(128 * t, 128 * t + 128)
                    w = slice(0 if t else 128, 256)
                    for a in range(2):
                        h = slice(HD * a, HD * a + HD)
                        o = PS[:, 2 * b + a, w]
                        pe.matmul(o, QF[h, m, c], KTD[h, g, 128 * (t - 1) + w.start:128 * t + 128], start=True,
                                  stop=False, tile_position=(HD * a, 0))
                        mm = pe.matmul(o, QMI[:, :], KMI[:, w], start=False, stop=True)
                else:
                    s = n - (NATT - NS)
                    if s == 0:
                        pe.wait_ge(qz, 4)
                    for g in range(KVH):
                        mm = pe.matmul(PS[:, 2 * b + g, 0:WIN + SL],
                                       QZ[:, s, g, :, :, :].rearrange("p e m t -> p (e m t)"), KCT[:, g, s, :],
                                       start=True, stop=True)
                mm.then_inc(a_sc, 1)

            def transposes(n):
                pe.wait_ge(a_p, n + 1)
                if n >= 2:
                    pe.wait_ge(a_pt, n - 1)
                for a in range(2):
                    for x in range(2):
                        if n < KT and x == 0:
                            continue
                        k = 128 if x == 0 or n < NATT - NS else SL
                        mm = pe.transpose(PS[0:k, 4 + n % 2, 256 * a + 128 * x:256 * a + 128 * x + 128],
                                          P[:, n % 2, 256 * a + 128 * x:256 * a + 128 * x + k], ident[:, :])
                mm.then_inc(a_tr, 1)

            def values(n):
                pe.wait_ge(a_pt, n + 1)
                if n >= 2:
                    pe.wait_ge(a_ol, n - 1)
                b = 6 + n % 2
                if n < NATT - NS:
                    t, m = n // KT, n % KT
                    ops = [(a, x) for a in range(2) for x in range(2) if t or x]
                    for j, (a, x) in enumerate(ops):
                        mm = pe.matmul(PS[:, b, 0:128], VZ[:, t - 1 + x, m // 4, HD * a:HD * a + 128],
                                       PT[:, n % 2, 256 * a + 128 * x:256 * a + 128 * x + 128],
                                       start=(j == 0), stop=(j == len(ops) - 1))
                else:
                    s = n - (NATT - NS)
                    if s == 0:
                        pe.wait_ge(s_vn, 16 * NS)
                    for g in range(KVH):
                        o = PS[:, b, 128 * g:128 * g + 128]
                        pe.matmul(o, VCD[:, s, g, :, :].rearrange("p e d -> p (e d)"),
                                  PT[:, n % 2, 256 * g:256 * g + 128], start=True, stop=False)
                        mm = pe.matmul(o, VN[:, s, g, :, :].rearrange("p e d -> p (e d)"),
                                       PT[0:SL, n % 2, 256 * g + 128:256 * g + 256], start=False, stop=True)
                mm.then_inc(a_o, 1)

            for n in range(NATT + 3):
                if n < NATT:
                    scores(n)
                if 2 <= n < NATT + 2:
                    transposes(n - 2)
                if n >= 3:
                    values(n - 3)
            pe.wait_ge(a_ol, NATT)
            with pe.Fori(0, 2) as i:
                for j in range(4):
                    fm_tile(pe, T_AO + j, U_AO + j, i)

        def qf_view(i, j):
            return QF[:, bass.ds(4 * i + j, 1), :].rearrange("p a t -> p (a t)")

        def heads_out(n, a):
            b = 6 + n % 2
            if n < NATT - NS:
                t, m = n // KT, n % KT
                return [PS[:, b, 0:128]] + [x[:, m, 128 * t:128 * t + 128] for x in (XH, XL)]
            s = n - (NATT - NS)
            h = slice(HD * a, HD * a + HD)
            c = SEQ + SL * s
            return [PS[h, b, 0:256].rearrange("p (g e m t) -> p g e m t", g=KVH, e=2, m=4)[:, :, a, :, :]] + \
                [x[h, :, c:c + SL].rearrange("p (g m) t -> p g m t", g=KVH) for x in (XH, XL)]

        def parts(n):
            return range(1 if n < NATT - NS else 2)

        def att_dve(v):
            invert(v, RC[2], True)
            v.wait_ge(rstd, RC[2] + 2)
            v.wait_ge(azero, 5)
            for j, groups in enumerate(TMU):
                u = U_KV + KV_UNITS[j]
                v.wait_ge(full, u + 1)
                for f, t in enumerate(groups):
                    k = PS[:, 2 * (u % 4) + f, 0:KVH * HD].rearrange("p (g d) -> p g d", g=KVH)
                    vv = PS[:, 2 * (u % 4) + f, KVH * HD:256].rearrange("p (g d) -> p g d", g=KVH)
                    for dup in range(2):
                        v.tensor_scalar(KD[:, t, :, dup, :], k, RT[:, t:t + 1], None, ALU.mult)
                        o = V4[:, :, dup, :] if t == TT - 1 else VZ[:, t, :, 2 * HD * dup:2 * HD * dup + HD]
                        mm = v.tensor_scalar(o, vv, RT[:, t:t + 1], None, ALU.mult)
                mm.then_inc(free, 3 if j == 0 else 1)
            for k in range(KT):
                rest_x(v, k, V_MIX + KT, XF[0] + 2 * KT)
            for n in (T_AQ + 2, T_AQ + 3):
                rest_tile(v, n)
            for g in range(KVH):
                u = U_KT + g
                v.wait_ge(full, u + 1)
                v.tensor_copy(KTD[:, g, :], PS[:, 2 * (u % 4), :])
                v.tensor_copy(KCT[:, g, :, WIN:WIN + SL], PS[:, 2 * (u % 4) + 1, 0:NS * SL]
                              .rearrange("p (s t) -> p s t", s=NS)).then_inc(free, 1)
            v.wait_ge(s_sink, 16)
            v.tensor_tensor(SKT[:, :], SKB[:, :], HB[:, :], ALU.mult).then_inc(sink_v, 1)
            v.wait_ge(sink_v, 1)
            v.tensor_reduce(SKR[:, :], SKT[:, :].rearrange("p (g h) -> p g h", g=KVH), AX.X, ALU.add).then_inc(sink_v, 1)
            with v.Fori(0, 2) as i:
                for j in range(4):
                    v.wait_ge(full, U_Q + j + 1 + 4 * i)
                    v.scalar_tensor_tensor(out=halves(qf_view(i, j)), in0=unit(U_Q + j), scalar=HD ** -0.5,
                                           in1=halves(RB[:, :]), op0=ALU.mult, op1=ALU.mult).then_inc(free, 1)
                    rest_tile(v, T_AQ + 4 + j, i)
            v.wait_ge(free, U_KC)
            for g in range(KVH):
                for e in range(2):
                    h = slice(HD * e, HD * e + HD)
                    v.tensor_copy(QZ[h, :, g, e, :, :].rearrange("p s m t -> p m s t"),
                                  QF[h, 4 * g:4 * g + 4, SEQ:T].rearrange("p m (s t) -> p m s t", s=NS)).then_inc(qz, 1)
            for g in range(KVH):
                u = U_KC + g
                v.wait_ge(full, u + 1)
                v.tensor_copy(KCT[:, g, :, 0:WIN].rearrange("p (b s) k -> p b s k", b=2),
                              PS[:, 2 * (u % 4):2 * (u % 4) + 2, :].rearrange("p b (s k) -> p b s k", k=WIN))\
                    .then_inc(free, 1)

            def maxima(n):
                v.wait_ge(a_sc, n + 1)
                b = n % 2
                sc = PS[:, 2 * b:2 * b + 2, 0:256]
                if n < KT:
                    sc = sc[:, :, 128:256]
                elif n >= NATT - NS:
                    sc = sc[:, :, 0:WIN + SL]
                m = n % KT
                sink = SKB[:, 2 * m:2 * m + 2] if n < NATT - NS else SKR[:, :]
                v.tensor_reduce(NM[:, b, :], sc, AX.X, ALU.max).then_inc(a_chain, 1)
                v.wait_ge(a_chain, 2 * n + 1)
                v.tensor_tensor(NM[:, b, :], NM[:, b, :], sink, ALU.max).then_inc(a_chain, 1)
                v.wait_ge(a_chain, 2 * n + 2)
                v.tensor_tensor(SE[:, b, :], sink, NM[:, b, :], ALU.subtract)
                v.tensor_scalar(NM[:, b, :], NM[:, b, :], -1.0, None, ALU.mult).then_inc(a_nm, 1)

            def normalise(n):
                b = n % 2
                v.wait_ge(a_ex, n + 1)
                v.tensor_tensor(ES[:, b, :], ES[:, b, :], SE[:, b, :], ALU.add).then_inc(a_sum, 1)
                v.wait_ge(a_sum, 2 * n + 1)
                v.reciprocal(ES[:, b, :], ES[:, b, :]).then_inc(a_sum, 1)
                v.wait_ge(a_sum, 2 * n + 2)
                for a in range(2):
                    w = prob_cols(n, a)
                    mm = v.tensor_scalar(P[:, b, w], P[:, b, w], ES[:, b, a:a + 1], None, ALU.mult)
                mm.then_inc(a_p, 1)

            def rest_out(n):
                v.wait_ge(a_oh, n + 1)
                for a in parts(n):
                    i_, oh, ol = heads_out(n, a)
                    mm = v.tensor_tensor(ol, i_, f32(oh), ALU.subtract)
                mm.then_inc(a_ol, 1)

            for n in range(NATT + 3):
                if n < NATT:
                    maxima(n)
                if 1 <= n <= NATT:
                    normalise(n - 1)
                if n >= 3:
                    rest_out(n - 3)
            with v.Fori(0, 2) as i:
                for j in range(4):
                    v.wait_ge(full, U_AO + j + 1 + 4 * i)
                    xm = halves(X[:, bass.ds(4 * i + j, 1), :].rearrange("p a t -> p (a t)"))
                    v.tensor_tensor(xm, xm, unit(U_AO + j), ALU.add).then_inc(free, 1)
                    rest_tile(v, T_AO + 4 + j, i)
            for k in range(KT):
                rest_x(v, k, V_FFN + KT, XF[1])

        def prob_cols(n, a):
            if n < KT:
                return slice(256 * a + 128, 256 * a + 256)
            return slice(256 * a, 256 * a + (256 if n < NATT - NS else WIN + SL))

        def att_act(act):
            roots(act, U_KV + 1, 2, True)
            act.wait_ge(full, U_KV + 6)
            for k in range(KT):
                round_x(act, k, V_MIX + KT)
            for n in (T_AQ + 2, T_AQ + 3):
                round_tile(act, n)
            with act.Fori(0, 2) as i:
                for j in range(4):
                    act.wait_ge(full, U_Q + j + 1 + 4 * i)
                    round_tile(act, T_AQ + 4 + j, i)

            def exponentials(n):
                b = n % 2
                act.wait_ge(a_nm, n + 1)
                if n >= 2:
                    act.wait_ge(a_tr, n - 1)
                for a in range(2):
                    w = prob_cols(n, a)
                    act.activation(P[:, b, w], PS[:, 2 * b + a, w.start % 256:w.start % 256 + w.stop - w.start], ACT.Exp, bias=NM[:, b, a:a + 1], accum_out=ES[:, b, a:a + 1])
                act.activation(SE[:, b, :], SE[:, b, :], ACT.Exp).then_inc(a_ex, 1)

            def to_sbuf(n):
                act.wait_ge(a_tr, n + 1)
                if n >= 2:
                    act.wait_ge(a_o, n - 1)
                b = n % 2
                if n < NATT - NS:
                    o, i_ = PT[:, b, :], PS[:, 4 + b, :]
                    if n < KT:
                        o, i_ = [x.rearrange("p (a k) -> p a k", a=2)[:, :, 128:256] for x in (o, i_)]
                    act.activation(o, i_, ACT.Copy).then_inc(a_pt, 1)
                else:
                    o, i_ = [x.rearrange("p (a k) -> p a k", a=2) for x in (PT[:, b, :], PS[:, 4 + b, :])]
                    act.activation(o[:, :, 0:128], i_[:, :, 0:128], ACT.Copy)
                    act.activation(o[0:SL, :, 128:256], i_[0:SL, :, 128:256], ACT.Copy).then_inc(a_pt, 1)

            def round_out(n):
                act.wait_ge(a_o, n + 1)
                for a in parts(n):
                    i_, oh, _ = heads_out(n, a)
                    mm = act.activation(oh, i_, ACT.Copy)
                mm.then_inc(a_oh, 1)

            act.wait_ge(free, U_AO)
            for n in range(NATT + 3):
                if 2 <= n < NATT + 2:
                    to_sbuf(n - 2)
                if n < NATT:
                    exponentials(n)
                if n >= 3:
                    round_out(n - 3)
            with act.Fori(0, 2) as i:
                for j in range(4):
                    act.wait_ge(full, U_AO + j + 1 + 4 * i)
                    round_tile(act, T_AO + 4 + j, i)
                    act.wait_ge(free, U_AO + j + 1 + 4 * i)
                    square_x(act, j, 3, 4 * i + j, i)
            for k in range(KT):
                round_x(act, k, V_FFN + KT)

        Y_UNITS = [0, 1, 2, 4, 5]

        def final_pe(pe):
            def group(t):
                u = U_Y + Y_UNITS[t]
                pe.wait_ge(free, u - 3)
                for k in range(KT):
                    if t == 0:
                        pe.wait_ge(free, U_Y - KT + k + 1)
                    mm = pe.transpose(PS[:, 2 * (u % 4) + k // 4, 128 * (k % 4):128 * (k % 4) + 128],
                                      X[:, k, 128 * t:128 * t + 128], ident[:, :])
                mm.then_inc(full, 1)

            for t in range(3):
                group(t)
            pe.wait_ge(ss_done, (KT + 1) * 5)
            stat_rows(pe, U_Y + 3)
            group(3)
            group(4)

        def final_act(act):
            act.wait_ge(full, U_Y + 4)
            act.activation(RT[:, :], PS[:, 2 * ((U_Y + 3) % 4), 0:TT], ACT.Sqrt, bias=eps[:, 0:1],
                           scale=1.0 / D).then_inc(rt_sq, 1)

        def final_dve(v):
            v.wait_ge(rt_sq, RC[4] + 1)
            v.reciprocal(RT[:, :], RT[:, :]).then_inc(rstd, 1)
            v.wait_ge(rstd, RC[4] + 1)
            v.wait_ge(s_nfb, 16)
            for t in range(TT):
                u = U_Y + Y_UNITS[t]
                v.wait_ge(full, u + 1)
                v.scalar_tensor_tensor(out=YO[:, t, :], in0=PS[:, 2 * (u % 4):2 * (u % 4) + 2, :].rearrange("p b c -> p (b c)"),
                                       scalar=RT[:, t:t + 1], in1=NFB[:, :], op0=ALU.mult, op1=ALU.mult)\
                    .then_inc(free, 2 if t == 2 else 1)

        def final_sp(sp):
            yp = O["y_p"][0].rearrange("(t p) d -> p t d", p=128)
            ys = O["y_s"].rearrange("s l d -> (s l) d")
            sp.wait_ge(full, U_F[1] + fu(NIT - 1) + 12)
            sp.dma_start(NFB[:, :], A["norm_final"].rearrange("(o n) -> o n", o=1).to_broadcast([128, D])).then_inc(s_nfb, 16)
            tail_stores(sp, 1)
            for t in range(TT):
                sp.wait_ge(free, U_Y + Y_UNITS[t] + 1)
                sp.dma_start(yp[:, t, :] if t < TT - 1 else ys, YO[:, t, :]).then_inc(s_y, 16)
            sp.wait_ge(s_y, 16 * TT)
            sp.wait_ge(s_tout, 2 * 128)
            sp.wait_ge(s_out, 16 * N_OUT)


        def front_sp(sp):
            xp = A["x_prompt"][0].rearrange("(t p) d -> p t d", p=128)
            xs = A["x_sample"].rearrange("s l d -> (s l) d")
            vecs = ((0, A["norm_mix"].rearrange("l (k p) -> (l k) p", p=128)),
                    (16, A["norm_ffn"].rearrange("l (k p) -> (l k) p", p=128)),
                    (32, A["norm_kv"].rearrange("(k p) -> k p", p=128)),
                    (40, A["norm_final"].rearrange("(k p) -> k p", p=128)),
                    (48, A["gla_g_onorm"][0].rearrange("(k p) -> k p", p=128)),
                    (50, A["gla_b_g2"][0].rearrange("(k p) -> k p", p=128)))
            for t, (r, v) in enumerate(vecs):
                if t < TT:
                    sp.dma_start(XIN[:, t, :], xp[:, t, :] if t < TT - 1 else xs).then_inc(s_xin, 16)
                sp.dma_start(NRAW[r:r + v.shape[0], :], v).then_inc(s_const, 16)
            for p, (w, c) in enumerate(pieces[:2]):
                sp.dma_start(WRAW[:, p, :, :], w.rearrange("(k p) n -> p k n", p=128)[:, :, c:c + 256])\
                    .then_inc(s_raw[p], 16)
            sp.dma_start(SKB[:, :], A["att_sinks"].to_broadcast([128, NH])).then_inc(s_sink, 16)
            for o, c in (("k_s", "cache_k"), ("v_s", "cache_v")):
                sp.dma_start(O[o][:, 0:WIN - SL], A[c][:, SL:WIN]).then_inc(s_out, 16)
            sp.wait_ge(s_setup, 1)
            sp.dma_start(G2[128 - RANK:128, :], A["gla_w_g2"][0]).then_inc(s_g2, 16)
            sp.wait_ge(free, U_X + KT)
            sp.dma_start(XSP, X[:, :, :]).then_inc(s_spill, 16)

            def piece(p):
                w, c = pieces[p]
                sp.wait_ge(lo_done, 2 * p - 2)
                sp.dma_start(WRAW[:, p % 2, :, :], w.rearrange("(k p) n -> p k n", p=128)[:, :, c:c + 256])\
                    .then_inc(s_raw[p % 2], 16)

            for p in range(2, T_WO // 2 + 2):
                piece(p)
            for h in range(H):
                if h == 0:
                    sp.wait_ge(full, U_Z + 4)
                else:
                    sp.wait_ge(st_done, 8 * (h - 1) + 4)
                    sp.dma_start(O["gla_s"][0, :, h - 1].rearrange("s p d -> p s d"), S0[:, :, :]).then_inc(s_sout, 16)
                    sp.wait_ge(s_sout, 16 * h)
                sp.dma_start(S0[:, :, :], A["state_gla"][0, :, h].rearrange("s p d -> p s d")).then_inc(s_s0, 16)
                if h:
                    sp.wait_ge(st_done, 8 * h)
                    sp.dma_start(O["gla_p"][0, 0, h - 1], ST[:, :]).then_inc(s_pout, 16)
            sp.wait_ge(st_done, 8 * H)
            sp.dma_start(O["gla_s"][0, :, H - 1].rearrange("s p d -> p s d"), S0[:, :, :]).then_inc(s_sout, 16)
            sp.dma_start(O["gla_p"][0, 0, H - 1], ST[:, :]).then_inc(s_pout, 16)
            sp.wait_ge(att, STEPS)
            sp.dma_start(X[:, :, :], XSP).then_inc(s_xback, 16)
            for p in range(T_WO // 2 + 2, T_WO // 2 + 4):
                piece(p)
            sp.wait_ge(full, U_WO)
            conv_loads(sp, 0)
            sp.wait_ge(s_sout, 16 * H)
            sp.wait_ge(s_pout, 16 * H)

        def front_pool(pool):
            pool.memset(G2[:, :], 0.0).then_inc(s_setup, 1)
            pool.memset(ident[:, :], 0.0).then_inc(s_setup, 1)
            pool.memset(ones[:, :], 1.0).then_inc(s_setup, 1)
            pool.memset(EPSC[:, :], EPS).then_inc(s_setup, 1)
            pool.memset(EV[:, :], 1.0).then_inc(s_setup, 1)
            pool.wait_ge(s_setup, 5)
            pool.affine_select(out=ident[:, :], in_=ident[:, :], compare_op=ALU.not_equal, fill=1.0, base=0,
                               pattern=[[-1, 128]], channel_multiplier=1).then_inc(s_setup, 1)
            pool.affine_select(out=EV[:, :], in_=EV[:, :], compare_op=ALU.is_ge, fill=0.0, base=0,
                               pattern=[[-2 * SL, 4]], channel_multiplier=1).then_inc(s_setup, 1)
            pool.wait_ge(s_setup, 7)
            pool.affine_select(out=EV[:, :], in_=EV[:, :], compare_op=ALU.is_ge, fill=0.0, base=SL - 1,
                               pattern=[[2 * SL, 4]], channel_multiplier=-1).then_inc(s_setup, 1)
            clear_sums(pool, 0)
            for k in range(KT):
                add_squares(pool, k, 0)
            pool.memset(HB[:, :], 1.0).then_inc(azero, 1)
            pool.wait_ge(azero, 1)
            bands = [[0, KVH], [-SL, 4], [-HD, 2]]
            pool.affine_select(out=HB[:, :], in_=HB[:, :], compare_op=ALU.is_ge, fill=0.0, base=0,
                               pattern=bands, channel_multiplier=1).then_inc(azero, 1)
            pool.wait_ge(azero, 2)
            pool.affine_select(out=HB[:, :], in_=HB[:, :], compare_op=ALU.is_ge, fill=0.0, base=SL - 1,
                               pattern=[[0, KVH], [SL, 4], [HD, 2]], channel_multiplier=-1).then_inc(azero, 1)
            pool.wait_ge(s_spill, 16)
            pool.wait_ge(xl_done, KT)
            pool.memset(MASK[:, :, :], 0.0).then_inc(s_mask, 1)
            pool.wait_ge(s_mask, 1)
            n = 1
            m0 = MASK[:, 0, :].rearrange("p (b r) -> p b r", r=BLK)
            views = [(m0, 128 // BLK, BLK)]
            for l in range(1, 4):
                hf = BLK << (l - 1)
                views.append((MASK[:, l, :].rearrange("p (s two r) -> p s two r", two=2, r=hf)[:, :, 1, :], 64 // hf, hf))
            for v, _, _ in views:
                pool.memset(v, 1.0).then_inc(s_mask, 1)
                n += 1
            pool.wait_ge(s_mask, n)
            for l, (v, ns, w) in enumerate(views):
                sup = w if l == 0 else 2 * w
                pool.affine_select(out=v, in_=v, compare_op=ALU.is_ge, fill=0.0, base=0,
                                   pattern=[[-sup, ns], [0, w]], channel_multiplier=1).then_inc(s_mask, 1)
                n += 1
            pool.wait_ge(s_mask, n)
            pool.affine_select(out=m0, in_=m0, compare_op=ALU.is_ge, fill=0.0, base=0,
                               pattern=[[BLK, 128 // BLK], [1, BLK]], channel_multiplier=-1).then_inc(s_mask, 1)
            for l, (v, ns, w) in list(enumerate(views))[1:]:
                pool.affine_select(out=v, in_=v, compare_op=ALU.is_ge, fill=0.0, base=w - 1,
                                   pattern=[[2 * w, ns], [0, w]], channel_multiplier=-1).then_inc(s_mask, 1)
            pool.wait_ge(full, U_Z + 4)
            pool.memset(QM[:, :], 0.0).then_inc(zset, 1)
            pool.wait_ge(full, U_OT)
            for s in range(2):
                pool.memset(SET[:, s, 2 * T:2 * T + 6 * SEQ], 0.0).then_inc(zset, 1)
            clear_sums(pool, 1)
            with pool.Fori(0, 2) as i:
                for k in range(4):
                    add_squares(pool, k, 1, i)

        NMASK = 1 + 4 + 4 + 4

        def kq_view(i, j):
            return QK[:, bass.ds(4 * i + j, 1), :].rearrange("p a t -> p (a t)")

        def front_pe(pe):
            pe.wait_ge(s_setup, 8)
            pe.wait_ge(s_const, 16 * 6)
            pe.transpose(PS[:, 0, 0:NVEC], NRAW[:, :], ident[0:NVEC, 0:NVEC]).then_inc(full, 1)
            pe.wait_ge(s_xin, 16 * TT)
            for k in range(KT):
                u = U_X + k
                if u >= 4:
                    pe.wait_ge(free, u - 3)
                for t in range(TT):
                    mm = pe.transpose(PS[:, 2 * (u % 4) + t // 4, 128 * (t % 4):128 * (t % 4) + 128],
                                      XIN[:, t, 128 * k:128 * k + 128], ident[:, :])
                mm.then_inc(full, 1)
            fm_tile(pe, T_GL + 1, U_GL, fresh=0)
            stat_cols(pe, U_GL + 1, 0)
            stat_rows(pe, U_GL + 2)
            with pe.Fori(0, 2) as i:
                for j in range(4):
                    fm_tile(pe, T_KQ + j, U_KQ + j, i)
            pe.wait_ge(s_g2, 16)
            for h in range(H):
                u = U_Z + h
                pe.wait_ge(free, u - 3)
                for f in range(2):
                    mm = pe.matmul(PS[:, 2 * (u % 4) + f, 0:HALF], G2[:, DK * h:DK * h + DK],
                                   GLS[:, f * HALF:(f + 1) * HALF], start=True, stop=True)
                mm.then_inc(full, 1)
            for t0, u0 in ((T_V, U_V), (T_R, U_R)):
                with pe.Fori(0, 2) as i:
                    for q in range(2):
                        for j, groups in enumerate(TMU):
                            tm_unit(pe, t0 + 2 * q, u0 + 4 * q + j, groups, i)
            gla_pe(pe)
            pe.wait_ge(att, STEPS)
            pe.wait_ge(osq, STEPS)
            pe.wait_ge(st_done, 8 * H)
            for g in range(TT):
                u = U_OT + g
                if g == 4:
                    pe.wait_ge(free, u - 3)
                pe.wait_ge(ogn, g + 1)
                for kt in range(KT):
                    mm = pe.transpose(PS[:, 2 * (u % 4) + kt // 4, 128 * (kt % 4):128 * (kt % 4) + 128],
                                      RS[:, g, 128 * kt:128 * kt + 128], ident[:, :])
                mm.then_inc(full, 1)
            pe.wait_ge(free, U_OT + TT)
            with pe.Fori(0, 2) as i:
                for j in range(4):
                    fm_tile(pe, T_WO + j, U_WO + j, i)

        def front_dve(v):
            v.wait_ge(full, 1)
            v.tensor_copy(NW[:, :], PS[:, 0, 0:NVEC]).then_inc(free, 1)
            v.wait_ge(free, 1)
            for k in range(KT):
                u = U_X + k
                v.wait_ge(full, u + 1)
                v.tensor_copy(X[:, k, 0:512], PS[:, 2 * (u % 4), :])
                v.tensor_copy(X[:, k, 512:T], PS[:, 2 * (u % 4) + 1, 0:T - 512]).then_inc(free, 1)
                if k:
                    rest_x(v, k - 1, V_MIX, 0)
            rest_x(v, KT - 1, V_MIX, 0)
            for n in range(4):
                rest_tile(v, n)
            v.wait_ge(s_setup, 8)
            v.tensor_reduce(EO[:, 0:1], EV[:, :], AX.X, ALU.add).then_inc(dve, 1)
            v.wait_ge(dve, 1)
            v.tensor_scalar(EO[:, 1:2], EO[:, 0:1], -1.0, 1.0, ALU.mult, ALU.add).then_inc(dve, 1)
            invert(v, 0, True)
            v.wait_ge(rstd, 2)
            v.tensor_tensor(halves(GLS[:, :]), unit(U_GL), halves(RB[:, :]), ALU.mult).then_inc(free, 3)
            for n in (4, 5):
                rest_tile(v, n)
            with v.Fori(0, 2) as i:
                for j in range(4):
                    v.wait_ge(full, U_KQ + j + 1 + 4 * i)
                    v.tensor_tensor(halves(kq_view(i, j)), unit(U_KQ + j), halves(RB[:, :]), ALU.mult)\
                        .then_inc(free, 1)
                    rest_tile(v, T_KQ + 4 + j, i)
            v.wait_ge(s_spill, 16)
            v.wait_ge(xh_done, KT)
            v.wait_ge(sq_done, KT)
            v.memset(M16[:, :], 1.0).then_inc(dve, 1)
            v.memset(M128[:, :], 1.0).then_inc(dve, 1)
            v.wait_ge(dve, 4)
            v.memset(M16[:, 0:T:BLK], 0.0).then_inc(dve, 1)
            v.memset(M128[:, 0:SEQ:128], 0.0).then_inc(dve, 1)
            v.memset(M128[:, SEQ:T:SL], 0.0).then_inc(dve, 1)
            for h in range(H):
                v.wait_ge(full, U_Z + h + 1)
                v.wait_ge(s_mn, h + 1)
                v.tensor_scalar(halves(LA[:, h, :]), unit(U_Z + h), NW[:, V_BG + h:V_BG + h + 1], 0.0,
                                ALU.add, ALU.min).then_inc(free, 1)
            with v.Fori(0, 2) as i:
                for q in range(2):
                    for j, groups in enumerate(TMU):
                        u = U_V + 4 * q + j
                        v.wait_ge(full, u + 1 + 8 * i)
                        for f, t in enumerate(groups):
                            mm = v.tensor_scalar(V[:, t, bass.ds(256 * q + 512 * i, 256)],
                                                 PS[:, 2 * (u % 4) + f, 0:256], RT[:, t:t + 1], None, ALU.mult)
                        mm.then_inc(free, 1)
                    for n in range(2):
                        rest_tile(v, T_V + 4 + 2 * q + n, i)
            v.wait_ge(s_mn, H + 2)
            v.wait_ge(free, U_V)
            v.tensor_tensor(LA[:, :, :], LA[:, :, :], AB[:, :, :], ALU.subtract).then_inc(s_la, 1)
            v.wait_ge(s_la, 1)
            with v.Fori(0, 2) as i:
                for n in range(4):
                    rest_tile(v, T_R + 4 + n, i)
            gla_dve(v)
            v.wait_ge(rt_h, 1)
            v.reciprocal(RH[:, :], RH[:, :]).then_inc(rt_h, 1)
            v.wait_ge(rt_h, 2)
            v.tensor_scalar(RH[:, :], RH[:, :], DK ** -0.5, None, ALU.mult).then_inc(rt_h, 1)
            v.wait_ge(rt_h, 3)
            v.wait_ge(og, STEPS)
            for g in range(TT):
                for h in range(H):
                    mm = v.tensor_scalar(RS[:, g, DV * h:DV * h + DV], RS[:, g, DV * h:DV * h + DV],
                                         RH[:, TT * h + g:TT * h + g + 1], None, ALU.mult)
                mm.then_inc(ogn, 1)
            for g in range(TT):
                u = U_OT + g
                v.wait_ge(xh_done, KT + g + 1)
                for e in range(2):
                    i_, oh, ol = ot_views(u, g, e)
                    mm = v.scalar_tensor_tensor(out=ol, in0=i_, scalar=NW[:, V_ON + e:V_ON + e + 1], in1=f32(oh),
                                                op0=ALU.mult, op1=ALU.subtract)
                mm.then_inc(free, 1)
            v.wait_ge(s_xback, 16)
            with v.Fori(0, 2) as i:
                for j in range(4):
                    v.wait_ge(full, U_WO + j + 1 + 4 * i)
                    xm = halves(X[:, bass.ds(4 * i + j, 1), :].rearrange("p a t -> p (a t)"))
                    v.tensor_tensor(xm, xm, unit(U_WO + j), ALU.add).then_inc(free, 1)
                    rest_tile(v, T_WO + 4 + j, i)
            for k in range(KT):
                rest_x(v, k, V_FFN, XF[0])

        def ot_views(u, g, e):
            b = 2 * (u % 4)
            i_ = PS[:, b:b + 2, :].rearrange("p b (c e q) -> p b c e q", c=2, e=2)[:, :, :, e, :]
            o_ = [x[:, :, 128 * g:128 * g + 128].rearrange("p (b c e) q -> p b c e q", b=2, c=2)[:, :, :, e, :]
                  for x in (XH, XL)]
            return i_, o_[0], o_[1]

        def front_act(act):
            for k in range(KT):
                act.wait_ge(free, U_X + k + 1)
                round_x(act, k, V_MIX)
                if k % 2:
                    round_tile(act, k // 2)
            for k in range(KT):
                square_x(act, k, 0)
            roots(act, U_GL + 1, 0, True)
            act.wait_ge(full, U_GL + 1)
            for n in (4, 5):
                round_tile(act, n)
            with act.Fori(0, 2) as i:
                for j in range(4):
                    act.wait_ge(full, U_KQ + j + 1 + 4 * i)
                    round_tile(act, T_KQ + 4 + j, i)
            for h in range(H):
                act.wait_ge(full, U_Z + h + 1)
                act.activation(halves(AB[:, h, :]), unit(U_Z + h), ACT.Abs, bias=NW[:, V_BG + h:V_BG + h + 1])\
                    .then_inc(s_mn, 1)
            act.wait_ge(s_mn, H)
            act.activation(AB[:, :, :], AB[:, :, :], ACT.Exp, scale=-1.0).then_inc(s_mn, 1)
            act.wait_ge(s_mn, H + 1)
            act.activation(AB[:, :, :], AB[:, :, :], ACT.Ln, bias=1.0).then_inc(s_mn, 1)
            with act.Fori(0, 2) as i:
                for q in range(2):
                    act.wait_ge(full, U_V + 4 * q + 4 + 8 * i)
                    for n in range(2):
                        round_tile(act, T_V + 4 + 2 * q + n, i)
            act.wait_ge(free, U_R)
            act.wait_ge(s_la, 1)
            with act.Fori(0, 2) as i:
                for q in range(2):
                    for j, groups in enumerate(TMU):
                        u = U_R + 4 * q + j
                        act.wait_ge(full, u + 1 + 8 * i)
                        for f, t in enumerate(groups):
                            mm = act.activation(RS[:, t, bass.ds(256 * q + 512 * i, 256)],
                                                PS[:, 2 * (u % 4) + f, 0:256], ACT.Silu, scale=RT[:, t:t + 1])
                        mm.then_inc(free, 1)
                    for n in range(2):
                        round_tile(act, T_R + 4 + 2 * q + n, i)
            gla_act(act)
            act.wait_ge(osq, STEPS)
            act.activation(RH[:, :], SSH[:, :], ACT.Sqrt, scale=1.0 / (DV * DK), bias=eps[:, 0:1]).then_inc(rt_h, 1)
            for g in range(TT):
                u = U_OT + g
                act.wait_ge(full, u + 1)
                for e in range(2):
                    i_, oh, _ = ot_views(u, g, e)
                    mm = act.activation(oh, i_, ACT.Copy, scale=NW[:, V_ON + e:V_ON + e + 1])
                mm.then_inc(xh_done, 1)
            with act.Fori(0, 2) as i:
                for j in range(4):
                    act.wait_ge(full, U_WO + j + 1 + 4 * i)
                    round_tile(act, T_WO + 4 + j, i)
                    act.wait_ge(free, U_WO + j + 1 + 4 * i)
                    square_x(act, j, 1, 4 * i + j, i)
            for k in range(KT):
                round_x(act, k, V_FFN)

        def gla_pe(pe):
            pe.wait_ge(free, U_OT)
            pe.wait_ge(s_mask, NMASK)

            def scores(n):
                h, g = n // TT, GO[n % TT]
                s = h % 2
                if n % TT == 0:
                    pe.wait_ge(prep, 2 * h + 1)
                if n >= 2:
                    pe.wait_ge(kt_done, n - 1)
                pe.transpose(PS[:, 6 + n % 2, 0:128], kr(s)[:, 128 * g:128 * g + 128], ident[:, :])\
                    .then_inc(tr_full, 1)
                if n >= 2:
                    pe.wait_ge(att, n - 1)
                c = slice(128 * g, 128 * g + 128)
                mm = pe.matmul(PS[:, n % 2, 0:128], kd(s)[:, c], qd(s)[:, c], start=True, stop=True)
                if g < TT - 1:
                    for l in range(1, 4):
                        mm = pe.matmul(PS[:, n % 2, 128 * l:128 * l + 128], kl(s, l)[:, c], ql(s, l)[:, c],
                                       start=True, stop=True)
                mm.then_inc(sc_full, 1)

            def outputs(n):
                h, j = n // TT, n % TT
                g = GO[j]
                s = h % 2
                pe.wait_ge(att, n + 1)
                if n >= 2:
                    pe.wait_ge(og, n - 1)
                o = PS[:, 2 + n % 2, 0:DV]
                vv = V[:, g, DV * h:DV * h + DV]
                mm = pe.matmul(o, AT[:, n % 2, :], vv, start=True, stop=(j == 1))
                if j == 0:
                    pe.wait_ge(prep, 2 * h + 2)
                    pe.wait_ge(s_s0, 16 * (h + 1))
                    for q in range(NS):
                        mm = pe.matmul(o, QM[:, 128 * q:128 * q + 128], S0[:, q, :], start=False, stop=(q == NS - 1))
                elif j >= 2:
                    pe.wait_ge(st_done, 8 * h + 4 + j - 1)
                    mm = pe.matmul(o, QI[:, s, 128 * g:128 * g + 128], ST[:, :], start=False, stop=True)
                mm.then_inc(o_full, 1)
                pe.wait_ge(kt_done, n + 1)
                for x in range(4 if j == 0 else 1):
                    cnt = 8 * h + x if j == 0 else 8 * h + 4 + j - 1
                    if cnt >= 2:
                        pe.wait_ge(st_done, cnt - 1)
                    b = 4 + cnt % 2
                    if j:
                        mm = pe.matmul(PS[:, b, 0:DV], KTK[:, 2 * (n % 2), :], vv, start=True, stop=True)
                    else:
                        for e in range(2):
                            r = slice(32 * x, 32 * x + 32)
                            mm = pe.matmul(PS[:, b, DV * e:DV * e + DV], KTK[r, 2 * (n % 2) + e, :],
                                           V[r, g, DV * h:DV * h + DV], start=True, stop=True,
                                           tile_position=(32 * x, 0))
                    mm.then_inc(st_full, 1)

            for n in range(STEPS + 1):
                if n < STEPS:
                    scores(n)
                if n:
                    outputs(n - 1)

        def span(ap, l, odd):
            hf = BLK << (l - 1)
            return ap.rearrange("p (s two r) -> p s two r", two=2, r=hf)[:, :, odd, :]

        def gla_dve(v):
            def exponents(h):
                s = h % 2
                if h >= 1:
                    v.wait_ge(exps, h)
                if h >= 2:
                    v.wait_ge(o_full, TT * (h - 1))
                    v.wait_ge(st_full, 8 * (h - 1))
                v.tensor_tensor_scan(B16[:, :], M16[:, :], LA[:, h, :], 0.0, ALU.mult, ALU.add).then_inc(cum, 1)
                v.tensor_tensor_scan(B128[:, :], M128[:, :], LA[:, h, :], 0.0, ALU.mult, ALU.add).then_inc(cum, 1)
                v.wait_ge(cum, 2 * h + 2)
                b = B128[:, 0:SEQ]
                for l in range(1, 4):
                    hf = BLK << (l - 1)
                    even, odd = span(b, l, 0), span(b, l, 1)
                    ref = even[:, :, hf - 1:hf].to_broadcast([128, SEQ // (2 * hf), hf])
                    v.tensor_tensor(span(ql(s, l), l, 1), odd, ref, ALU.subtract)
                    v.tensor_tensor(span(kl(s, l), l, 0), ref, even, ALU.subtract)
                bg = b.rearrange("p (g t) -> p g t", t=128)
                v.tensor_tensor(kr(s)[:, 0:SEQ].rearrange("p (g t) -> p g t", t=128),
                                bg[:, :, 127:128].to_broadcast([128, TT - 1, 128]), bg, ALU.subtract)
                bs = B16[:, SEQ:T].rearrange("p (s t) -> p s t", t=SL)
                v.tensor_tensor(kr(s)[:, SEQ:T].rearrange("p (s t) -> p s t", t=SL),
                                bs[:, :, SL - 1:SL].to_broadcast([128, NS, SL]), bs, ALU.subtract).then_inc(args, 1)

            def operands(h):
                s = h % 2
                q, k = QK[:, H + h, :], QK[:, h, :]
                v.wait_ge(exps, h + 1)
                v.tensor_tensor(kd(s), kd(s), k, ALU.mult)
                v.tensor_tensor(kr(s), kr(s), k, ALU.mult)
                v.tensor_tensor(QI[:, s, :], QI[:, s, :], q[:, 0:SEQ], ALU.mult)
                for l in range(1, 4):
                    v.tensor_tensor(span(ql(s, l), l, 1), span(ql(s, l), l, 1), span(q[:, 0:SEQ], l, 1), ALU.mult)
                    v.tensor_tensor(span(kl(s, l), l, 0), span(kl(s, l), l, 0), span(k[:, 0:SEQ], l, 0), ALU.mult)
                v.tensor_tensor(qd(s), qd(s), q, ALU.mult).then_inc(prep, 1)
                v.wait_ge(prep, 2 * h + 1)
                if h:
                    v.wait_ge(o_full, TT * (h - 1) + 1)
                qs = qd(s)[:, SEQ:T].rearrange("p (s t) -> p s t", t=SL)
                n = NS - 1
                v.tensor_copy(QM[:, 0:n * (128 + SL)].rearrange("p (s c) -> p s c", s=n)[:, :, 0:SL], qs[:, 0:n, :])
                v.tensor_copy(QM[:, n * (128 + SL):n * (128 + SL) + SL], qs[:, n, :]).then_inc(prep, 1)

            def mask(n):
                g = GO[n % TT]
                v.wait_ge(sc_full, n + 1)
                if n >= 2:
                    v.wait_ge(o_full, n - 1)
                if g == TT - 1:
                    v.tensor_tensor(AT[:, n % 2, :], PS[:, n % 2, 0:128], MASK[:, 0, :], ALU.mult).then_inc(att, 1)
                    return
                if n >= 1:
                    v.wait_ge(att, n)
                v.tensor_tensor(MPR[:, :], PS[:, n % 2, :], MASK[:, :, :].rearrange("p l q -> p (l q)"), ALU.mult)\
                    .then_inc(prod, 1)
                v.wait_ge(prod, 4 * (n // TT) + n % TT)
                v.tensor_reduce(AT[:, n % 2, :], MPR[:, :].rearrange("p (l q) -> p q l", l=4), AX.X, ALU.add)\
                    .then_inc(att, 1)

            def after(n):
                h, j = n // TT, n % TT
                g = GO[j]
                v.wait_ge(osq, n + 1)
                r = RS[:, g, DV * h:DV * h + DV]
                v.tensor_tensor(r, PS[:, 2 + n % 2, 0:DV], r, ALU.mult).then_inc(og, 1)
                for x in range(4 if j == 0 else 1):
                    cnt = 8 * h + x if j == 0 else 8 * h + 4 + j - 1
                    v.wait_ge(st_full, cnt + 1)
                    b = 4 + cnt % 2
                    if j == 0:
                        for e in range(2):
                            q = 2 * x + e
                            mm = v.scalar_tensor_tensor(out=S0[:, q, :], in0=S0[:, q, :],
                                                        scalar=DEC[:, h % 2, 4 + q:5 + q],
                                                        in1=PS[:, b, DV * e:DV * e + DV], op0=ALU.mult, op1=ALU.add)
                        mm.then_inc(st_done, 1)
                    elif j == 1:
                        if h:
                            v.wait_ge(s_pout, 16 * h)
                        v.tensor_copy(ST[:, :], PS[:, b, 0:DV]).then_inc(st_done, 1)
                    else:
                        v.wait_ge(st_done, cnt)
                        v.scalar_tensor_tensor(out=ST[:, :], in0=ST[:, :], scalar=DEC[:, h % 2, j - 1:j],
                                               in1=PS[:, b, 0:DV], op0=ALU.mult, op1=ALU.add).then_inc(st_done, 1)

            v.wait_ge(dve, 7)
            v.wait_ge(zset, 3)
            exponents(0)
            operands(0)
            for n in range(STEPS + 1):
                if n < STEPS:
                    mask(n)
                if n:
                    after(n - 1)
                h = n // TT
                if n % TT == 0 and h + 1 < H:
                    exponents(h + 1)
                if n % TT == 3 and h + 1 < H:
                    operands(h + 1)

        def gla_act(act):
            def exponentials(h):
                s = h % 2
                c = 1.0 / GATE
                act.wait_ge(args, h + 1)
                if h >= 2:
                    act.wait_ge(st_done, 8 * (h - 1))
                act.activation(kd(s), B16[:, :], ACT.Exp, scale=-c)
                act.activation(kr(s), kr(s), ACT.Exp, scale=c)
                act.activation(QI[:, s, :], B128[:, 0:SEQ], ACT.Exp, scale=c)
                for l in range(1, 4):
                    act.activation(span(ql(s, l), l, 1), span(ql(s, l), l, 1), ACT.Exp, scale=c)
                    act.activation(span(kl(s, l), l, 0), span(kl(s, l), l, 0), ACT.Exp, scale=c)
                act.activation(DEC[:, s, 0:4], B128[:, 127:SEQ:128], ACT.Exp, scale=c)
                act.activation(DEC[:, s, 4:12], B16[:, SEQ + SL - 1:T:SL], ACT.Exp, scale=c)
                act.activation(qd(s), B16[:, :], ACT.Exp, scale=c).then_inc(exps, 1)

            exponentials(0)
            for n in range(STEPS + 1):
                if n < STEPS:
                    act.wait_ge(tr_full, n + 1)
                    if n >= 2:
                        act.wait_ge(st_full, stc(n - 2))
                    if GO[n % TT] == TT - 1:
                        act.activation(KTK[:, 2 * (n % 2), :], PS[:, 6 + n % 2, 0:128], ACT.Copy, scale=EO[:, 0:1])
                        act.activation(KTK[:, 2 * (n % 2) + 1, :], PS[:, 6 + n % 2, 0:128], ACT.Copy,
                                       scale=EO[:, 1:2]).then_inc(kt_done, 1)
                    else:
                        act.activation(KTK[:, 2 * (n % 2), :], PS[:, 6 + n % 2, 0:128], ACT.Copy).then_inc(kt_done, 1)
                if n:
                    m = n - 1
                    act.wait_ge(o_full, m + 1)
                    if m:
                        act.wait_ge(osq, m)
                    c = TT * (m // TT) + GO[m % TT]
                    act.activation(JNK[:, :], PS[:, 2 + m % 2, 0:DV], ACT.Square, accum_out=SSH[:, c:c + 1])\
                        .then_inc(osq, 1)
                if n % TT == 1 and n // TT + 1 < H:
                    exponentials(n // TT + 1)

        def stc(n):
            return 8 * (n // TT) + 4 + n % TT

        block = ctx.enter_context(nc.Block())

        @block.sync
        def _(sp):
            front_sp(sp)
            ffn_sp(sp, 0)
            att_sp(sp)
            ffn_sp(sp, 1)
            final_sp(sp)

        @block.gpsimd
        def _(pool):
            front_pool(pool)
            ffn_pool(pool, 0)
            clear_sums(pool, 2)
            for k in range(KT):
                add_squares(pool, k, 2)
            att_pool(pool)
            clear_sums(pool, 3)
            with pool.Fori(0, 2) as i:
                for k in range(4):
                    add_squares(pool, k, 3, i)
            ffn_pool(pool, 1)
            clear_sums(pool, 4)
            for k in range(KT):
                add_squares(pool, k, 4)

        @block.scalar
        def _(act):
            front_act(act)
            ffn_act(act, 0, False, V_KV, 2)
            att_act(act)
            ffn_act(act, 1, True, None, 4)
            final_act(act)

        @block.vector
        def _(v):
            front_dve(v)
            ffn_dve(v, 0, False, V_KV, XF[0] + KT)
            att_dve(v)
            ffn_dve(v, 1, True, None, 0)
            final_dve(v)

        @block.tensor
        def _(pe):
            front_pe(pe)
            ffn_pe(pe, 0)
            att_pe(pe)
            ffn_pe(pe, 1)
            final_pe(pe)


INPUTS = ("x_prompt", "x_sample", "state_gla", "cache_k", "cache_v", "state_ffn_conv", "norm_mix", "norm_ffn",
          "norm_kv", "norm_final", "gla_w_in", "gla_w_g2", "gla_b_g2", "gla_g_onorm", "gla_w_out", "w_kv", "att_w_q",
          "att_sinks", "att_w_o", "ffn_w_up", "ffn_conv_w", "ffn_conv_b", "ffn_w_down")
OUTPUTS = (("y_p", (1, SEQ, D)), ("y_s", (NS, SL, D)), ("gla_p", (1, 1, H, DK, DV)), ("k_p", (1, WIN, KVH, HD)),
           ("v_p", (1, WIN, KVH, HD)), ("conv_p", (2, 1, 2, 2 * DFF)), ("gla_s", (1, NS, H, DK, DV)),
           ("k_s", (NS, WIN, KVH, HD)), ("v_s", (NS, WIN, KVH, HD)), ("conv_s", (2, NS, 2, 2 * DFF)))


def kernel(**inputs):
    import numpy as np
    import concourse.bacc as bacc
    from concourse.bass_utils import run_bass_kernel_spmd

    nc = bacc.Bacc("TRN2", target_bir_lowering=False, num_devices=1)
    arrays, A, O = {}, {}, {}
    for name in INPUTS:
        a = np.ascontiguousarray(inputs[name])
        arrays[f"in_{name}_dram"] = a
        A[name] = nc.dram_tensor(f"in_{name}_dram", a.shape, mybir.dt.from_np(a.dtype), kind="ExternalInput").ap()
    for i, (name, shape) in enumerate(OUTPUTS):
        O[name] = nc.dram_tensor(f"out_{i}_dram", shape, F32, kind="ExternalOutput").ap()
    build(nc, A, O)
    r = run_bass_kernel_spmd(nc, [arrays], core_ids=[0])
    return tuple(r.results[0][f"out_{i}_dram"] for i in range(len(OUTPUTS)))
```

```python
from contextlib import ExitStack

import concourse.bass as bass
from concourse import mybir

ALU = mybir.AluOpType
ACT = mybir.ActivationFunctionType
AX = mybir.AxisListType
F32 = mybir.dt.float32
F32R = mybir.dt.float32r
BF16 = mybir.dt.bfloat16

D = 1024
SEQ = 512
NS, SL = 8, 16
T = SEQ + NS * SL
KT = D // 128
TT = T // 128
HALF = T // 2
H, DK, DV, RANK = 4, 128, 256, 16
BLK = 16
GATE = 16.0
DFF = 2816
FT = DFF // 128
NIT = FT // 2
CW = SEQ + 2 + NS * (SL + 2)
CC = CW - 2
NH, HD, KVH, WIN, CH = 16, 64, 2, 128, 64
EPS = 1e-6


def build(nc, A, O):
    ctx = ExitStack()
    with ctx:
        top = [16512]

        def at(name, shape, dt, offset):
            return nc.alloc_sbuf_tensor_at(name, shape, dt, offset=offset)

        def size(shape, dt):
            n = 2 if dt == BF16 else 4
            for s in shape[1:]:
                n *= s
            return (n + 31) // 32 * 32

        def sb(name, shape, dt=F32):
            o = top[0]
            top[0] += size(shape, dt)
            return at(name, shape, dt, o)

        def area(n):
            o = top[0]
            top[0] += (n + 31) // 32 * 32
            return o

        def sem(name):
            return ctx.enter_context(nc.semaphore(name))

        x_area, xs_area = area(4 * KT * T), area(8 * KT * T)
        X = at("x_res", [128, KT, T], F32, x_area)
        XH = at("x_hi", [128, KT, T], F32R, xs_area)
        XL = at("x_lo", [128, KT, T], F32R, xs_area + 4 * KT * T)
        WRAW = sb("w_raw", [128, 2, KT, 256])
        DRAW_AREA = top[0]
        DRAW = sb("d_raw", [128, 2, D])
        WH = sb("w_hi", [128, 4, KT, 128], F32R)
        WL = sb("w_lo", [128, 4, KT, 128], F32R)
        d_area = area(4 * 4 * D)
        DH = at("d_hi", [128, 2, D], F32R, d_area)
        DL = at("d_lo", [128, 2, D], F32R, d_area + 8 * D)
        e_area = area(12 * KT * T)
        ident = sb("ident", [128, 128])
        ones = sb("ones", [128, 128])
        RB = sb("rstd_cols", [128, T])
        RT = sb("rstd_rows", [128, TT])
        SS = sb("sum_sq", [128, T])
        NVEC = 54
        NW = sb("vectors", [128, NVEC])
        CWT = sb("conv_taps", [128, 4, 2 * FT])
        k_area = top[0]
        KTK = sb("keys_rows", [128, 4, 128])
        m_area = area(2048)
        MPR = at("masked_scores", [128, 512], F32, m_area)
        AT = sb("scores", [128, 2, 128])
        ST = sb("gla_state", [128, DV])
        DEC = sb("decay", [128, 2, 12])
        JNK = sb("unused_out", [128, DV], BF16)
        SSH = sb("head_sq", [128, 20])
        RH = sb("head_rstd", [128, 20])
        EO = sb("even_odd", [128, 2])
        HB = sb("head_bands", [128, NH])
        SKB = sb("sinks_by_head", [128, NH])
        SKT = sb("sinks_banded", [128, NH])
        SKP = sb("sinks_pairs", [128, NH // 2])
        SKR = sb("sinks_rows", [128, KVH])
        NM = sb("neg_max", [128, 2, 2])
        SE = sb("sink_exp", [128, 2, 2])
        ES = sb("exp_sum", [128, 2, 2])
        assert top[0] <= 229344, top[0]

        QK = at("kq_cols", [128, 2 * H, T], F32, e_area)
        V = at("v_rows", [128, TT, H * DV], F32, e_area + 4 * KT * T)
        RS = at("r_rows", [128, TT, H * DV], F32, e_area + 8 * KT * T)
        XIN = at("x_in", [128, TT, D], F32, e_area + 4 * KT * T)
        AB = at("gate_tail", [128, H, T], F32, e_area + 8 * KT * T)
        NRAW = at("vectors_raw", [NVEC, 128], F32, e_area)
        SQ = at("squares", [128, 2, T], F32, e_area + 12 * KT * T - 8 * T)
        GLS = at("gate_low", [128, T], F32, d_area)
        G2 = at("gate_up", [128, H * DK], F32, d_area + 4 * T)
        QI = at("q_inter", [128, 2, SEQ], F32, d_area)
        QM = at("q_by_seq", [128, NS * 128], F32, d_area + 4096)
        S0 = at("seq_states", [128, NS, DV], F32, d_area + 8192)
        LA = at("log_gate", [128, H, T], F32, x_area)
        M16 = at("carry16", [128, T], BF16, x_area + 4 * H * T)
        M128 = at("carry128", [128, T], BF16, x_area + 4 * H * T + 2 * T)
        B16 = at("cum16", [128, T], F32, x_area + 4 * H * T + 4 * T)
        B128 = at("cum128", [128, T], F32, x_area + 4 * H * T + 8 * T)
        MASK = at("score_mask", [128, 4, 128], F32, x_area + 4 * H * T + 12 * T)
        SET = [at("gla_operands0", [128, 3 * T], F32, DRAW_AREA),
               at("gla_operands1", [128, 3 * T], F32, xs_area + 8 * 6 * SEQ)]
        SETL = at("gla_level_operands", [128, 2, 6 * SEQ], F32, xs_area)

        def qd(s): return SET[s][:, 0:T]
        def kd(s): return SET[s][:, T:2 * T]
        def kr(s): return SET[s][:, 2 * T:3 * T]
        def ql(s, l): return SETL[:, s, (l - 1) * SEQ:l * SEQ]
        def kl(s, l): return SETL[:, s, (l + 2) * SEQ:(l + 3) * SEQ]

        fo = [e_area]

        def fb(name, shape, dt=F32):
            o = fo[0]
            fo[0] += size(shape, dt)
            assert fo[0] <= e_area + 12 * KT * T - 8 * T
            return at(name, shape, dt, o)

        UB = fb("up_rows", [128, 4, CW])
        CB = fb("conv_out", [128, 4, CC])
        Y = fb("gated", [128, 2, T])
        YH = fb("gated_hi", [128, 2, T], F32R)
        YL = fb("gated_lo", [128, 2, T], F32R)
        TLC = fb("tail_cols", [128, NIT, 4, 18])
        TLR = fb("tail_rows", [72, NIT, 128])
        STR = fb("conv_state", [64, NIT, 128])
        STC = fb("conv_state_cols", [128, NIT, 64])
        CRAW = fb("taps_raw", [2 * FT, 4, 128])

        KCR = at("cache_k_rows", [128, NS, KVH, 2, HD], F32, e_area)
        P = at("probs", [128, 2, 512], F32, e_area)
        PT = at("probs_cols", [128, 2, 512], F32, e_area + 4096)
        KTD = at("keys_cols", [128, KVH, SEQ], F32, e_area + 8192)
        VZ = at("v_0_v", [128, TT - 1, KVH, 3 * HD], F32, e_area + 12288)
        QZ = at("q_0_q", [128, NS, KVH, 2, 4, SL], F32, e_area + 18432)
        KCT = at("seq_keys_cols", [128, KVH, NS, WIN + SL], F32, e_area + 26624)
        QF = at("q_cols", [128, KT // 2, T // CH, 2, CH], F32, e_area + 35840)
        KD = at("keys_twice", [128, TT, KVH, 2, HD], F32, d_area)
        V4 = at("v_new_rows", [128, KVH, 2, HD], F32, d_area + 5120)
        VN = at("v_new", [SL, NS, KVH, 2, HD], F32, d_area + 6144)
        VCD = at("cache_v", [128, NS, KVH, 2, HD], F32, DRAW_AREA)
        VS = at("v_0_v_shifted", [128, TT - 1, KVH, 3 * HD], F32, k_area)
        NFB = at("norm_final_rows", [128, D], F32, xs_area + 4 * KT * T)
        YO = at("y_rows", [128, TT, D], F32, xs_area)

        PS = ctx.enter_context(nc.psum_tensor("ps", [128, 8, 512], F32))
        XSP = nc.dram_tensor("x_spill", [128, KT, T], F32, kind="Internal").ap()

        s_const = sem("s_const")
        s_xin = sem("s_xin")
        s_raw = [sem("s_raw0"), sem("s_raw1")]
        s_draw = sem("s_draw")
        s_setup = sem("s_setup")
        full = sem("full")
        free = sem("free")
        hi_done = sem("hi_done")
        lo_done = sem("lo_done")
        dhi = sem("dhi")
        dlo = sem("dlo")
        xh_done = sem("xh_done")
        xl_done = sem("xl_done")
        sq_done = sem("sq_done")
        ss_done = sem("ss_done")
        rt_sq = sem("rt_sq")
        rstd = sem("rstd")
        s_spill = sem("s_spill")
        s_g2 = sem("s_g2")
        s_mask = sem("s_mask")
        rt_h = sem("rt_h")
        cum = sem("cum")
        prod = sem("prod")
        s_xback = sem("s_xback")
        dve = sem("dve")
        s_mn = sem("s_mn")
        s_la = sem("s_la")
        argk = sem("argk")
        argl = sem("argl")
        argp = sem("argp")
        exps = sem("exps")
        expl = sem("expl")
        prep = sem("prep")
        prepp = sem("prepp")
        prepl = sem("prepl")
        preplp = sem("preplp")
        zset = sem("zset")
        tr_full = sem("tr_full")
        kt_done = sem("kt_done")
        sc_full = sem("sc_full")
        att = sem("att")
        o_full = sem("o_full")
        osq = sem("osq")
        og = sem("og")
        st_full = sem("st_full")
        st_done = sem("st_done")
        s_s0 = sem("s_s0")
        s_sout = sem("s_sout")
        s_pout = sem("s_pout")
        ogh = sem("ogh")
        ogn = sem("ogn")
        t0_done = sem("t0_done")
        conv = sem("conv")
        silu = sem("silu")
        y_done = sem("y_done")
        yh = sem("yh")
        yl = sem("yl")
        st_c = sem("st_c")
        tl_g = sem("tl_g")
        s_str = sem("s_str")
        s_tout = sem("s_tout")
        s_out = sem("s_out")
        s_sink = sem("s_sink")
        s_cache = sem("s_cache")
        s_vs = sem("s_vs")
        s_vn = sem("s_vn")
        s_nfb = sem("s_nfb")
        s_y = sem("s_y")
        azero = sem("azero")
        sink_v = sem("sink_v")
        qz = sem("qz")
        a_sc = sem("a_sc")
        a_chain = sem("a_chain")
        a_sum = sem("a_sum")
        a_nm = sem("a_nm")
        a_ex = sem("a_ex")
        a_p = sem("a_p")
        a_tr = sem("a_tr")
        a_pt = sem("a_pt")
        a_o = sem("a_o")
        a_oh = sem("a_oh")
        a_ol = sem("a_ol")

        T_GL, T_KQ, T_V, T_R, T_WO = 0, 2, 10, 18, 26
        T_F = [34, 96]
        T_KV, T_AQ, T_AO = 78, 80, 88
        w_in = A["gla_w_in"][0]
        pieces = [(w_in, 2 * H * DK + 2 * H * DV + RANK - 256)]
        pieces += [(w_in, H * DK + 256 * n) for n in range(2)] + [(w_in, 256 * n) for n in range(2)]
        pieces += [(w_in, 2 * H * DK + 256 * n) for n in range(8)]
        pieces += [(A["gla_w_out"][0], 256 * n) for n in range(4)]
        later = {T_KV // 2: (A["w_kv"], 0)}
        later.update({T_AQ // 2 + n: (A["att_w_q"][0], 256 * n) for n in range(4)})
        later.update({T_AO // 2 + n: (A["att_w_o"][0], 256 * n) for n in range(4)})
        U_C, U_X, U_GL, U_KQ, U_Z, U_V, U_R = 0, 1, 9, 12, 20, 24, 40
        U_OT, U_WO = 56, 61
        FFN_UNITS = 6 + 12 * (NIT - 1) + 2 + KT
        U_KV = 69 + FFN_UNITS
        U_KT, U_Q, U_KC = U_KV + 6, U_KV + 8, U_KV + 16
        U_AO = U_KC + 2
        U_F = [69, U_AO + KT]
        U_Y = U_F[1] + FFN_UNITS
        XF = [KT + TT, KT + TT + 3 * KT]
        XLF = [KT, 4 * KT]
        NORM_F = [1, 3]
        RC = [0, 2, 3, 5, 6]
        STATS_READ = [0, U_GL + 3, U_F[0] + 3, U_KV + 3, U_F[1] + 3]
        GO = [TT - 1] + list(range(TT - 1))
        STEPS = H * TT
        TMU = [[0], [1], [2, 3], [4]]
        NATT = (TT - 1) * KT + NS
        V_MIX, V_FFN, V_KV, V_FIN, V_ON, V_BG = 0, 16, 32, 40, 48, 50

        def unit(u, n=HALF):
            return PS[:, 2 * (u % 4):2 * (u % 4) + 2, 0:n]

        def halves(ap):
            return ap.rearrange("p (a b) -> p a b", a=2)

        def f32(ap):
            return ap.bitcast(F32)

        def round_tile(act, n0, i=0):
            p0 = n0 // 2
            act.wait_ge(s_raw[p0 % 2], 16 * (p0 // 2 + 1) + 16 * i)
            half = (n0 % 2) * 128
            act.activation(WH[:, n0 % 4, :, :], WRAW[:, p0 % 2, :, half:half + 128],
                           ACT.Copy).then_inc(hi_done, 1)

        def rest_tile(v, n0, i=0):
            p0 = n0 // 2
            half = (n0 % 2) * 128
            v.wait_ge(hi_done, n0 + 1 + 4 * i)
            v.tensor_tensor(WL[:, n0 % 4, :, :], WRAW[:, p0 % 2, :, half:half + 128],
                            f32(WH[:, n0 % 4, :, :]), ALU.subtract).then_inc(lo_done, 1)

        def fm_tile(pe, n0, u0, i=0, wstep=4, ustep=4, fresh=None, beside=None):
            pe.wait_ge(lo_done, n0 + 1 + wstep * i)
            if u0 >= 4:
                pe.wait_ge(free, u0 - 3 + ustep * i)
            for k in range(KT):
                if fresh is not None:
                    pe.wait_ge(xl_done, fresh + k + 1)
                for a, (w, x) in enumerate(((WH, XH), (WH, XL), (WL, XH))):
                    for f in range(2):
                        mm = pe.matmul(PS[:, 2 * (u0 % 4) + f, 0:HALF], w[:, n0 % 4, k, :],
                                       x[:, k, f * HALF:(f + 1) * HALF],
                                       start=(k == 0 and a == 0), stop=(k == KT - 1 and a == 2))
            if beside is not None:
                mm = beside()
            mm.then_inc(full, 1)

        def fm_tile_halves(pe, n0, u0, split):
            pe.wait_ge(lo_done, n0 + 1)
            for f in range(2):
                pe.wait_ge(free, split[f])
                for k in range(KT):
                    for a, (w, x) in enumerate(((WH, XH), (WH, XL), (WL, XH))):
                        mm = pe.matmul(PS[:, 2 * (u0 % 4) + f, 0:HALF], w[:, n0 % 4, k, :],
                                       x[:, k, f * HALF:(f + 1) * HALF],
                                       start=(k == 0 and a == 0), stop=(k == KT - 1 and a == 2))
            mm.then_inc(full, 1)

        def tm_unit(pe, n0, u0, groups, i=0):
            pe.wait_ge(lo_done, n0 + 2 + 4 * i)
            pe.wait_ge(free, u0 - 3 + 8 * i)
            for f, t in enumerate(groups):
                for k in range(KT):
                    for a, (x, w) in enumerate(((XH, WH), (XH, WL), (XL, WH))):
                        mm = pe.matmul(PS[:, 2 * (u0 % 4) + f, 0:256], x[:, k, 128 * t:128 * t + 128],
                                       w[:, n0 % 4:n0 % 4 + 2, k, :],
                                       start=(k == 0 and a == 0), stop=(k == KT - 1 and a == 2))
            mm.then_inc(full, 1)

        def stat_cols(pe, u, norm):
            pe.wait_ge(ss_done, (KT + 1) * (norm + 1))
            pe.wait_ge(free, u - 3)
            for f in range(2):
                mm = pe.matmul(PS[:, 2 * (u % 4) + f, 0:HALF], ones[:, :], SS[:, f * HALF:(f + 1) * HALF],
                               start=True, stop=True)
            mm.then_inc(full, 1)

        def stat_rows(pe, u):
            pe.wait_ge(free, u - 3)
            for t in range(TT):
                mm = pe.matmul(PS[:, 2 * (u % 4), t:t + 1], SS[:, 128 * t:128 * t + 128], ones[:, 0:1],
                               start=True, stop=True)
            mm.then_inc(full, 1)

        def roots(act, u, norm, rows):
            act.wait_ge(full, u + 1)
            act.activation(halves(RB[:, :]), unit(u), ACT.Sqrt, bias=eps[:, 0:1], scale=1.0 / D).then_inc(rt_sq, 1)
            if rows:
                act.wait_ge(full, u + 2)
                act.activation(RT[:, :], PS[:, 2 * ((u + 1) % 4), 0:TT], ACT.Sqrt, bias=eps[:, 0:1],
                               scale=1.0 / D).then_inc(rt_sq, 1)

        eps = EPSC = sb("eps", [128, 2])
        EV = sb("bands", [128, 4])
        assert top[0] <= 229344, top[0]

        def invert(v, count, rows):
            v.wait_ge(rt_sq, count + 1)
            v.reciprocal(RB[:, :], RB[:, :]).then_inc(rstd, 1)
            if rows:
                v.wait_ge(rt_sq, count + 2)
                v.reciprocal(RT[:, :], RT[:, :]).then_inc(rstd, 1)

        def round_x(act, k, vec):
            act.activation(XH[:, k, :], X[:, k, :], ACT.Copy, scale=NW[:, vec + k:vec + k + 1]).then_inc(xh_done, 1)

        def rest_x(v, k, vec, base):
            v.wait_ge(xh_done, base + k + 1)
            v.scalar_tensor_tensor(out=XL[:, k, :], in0=X[:, k, :], scalar=NW[:, vec + k:vec + k + 1],
                                   in1=f32(XH[:, k, :]), op0=ALU.mult, op1=ALU.subtract).then_inc(xl_done, 1)

        def square_x(act, k, norm, k2=None, i=0):
            n = KT * norm + k
            if n >= 2:
                act.wait_ge(ss_done, (KT + 1) * norm + k + 4 * i)
            x = X[:, k, :] if k2 is None else X[:, bass.ds(k2, 1), :].rearrange("p a t -> p (a t)")
            act.activation(SQ[:, k % 2, :], x, ACT.Square).then_inc(sq_done, 1)

        def clear_sums(pool, norm):
            if norm:
                pool.wait_ge(full, STATS_READ[norm])
            pool.memset(SS[:, :], 0.0).then_inc(ss_done, 1)

        def add_squares(pool, k, norm, i=0):
            n = (KT + 1) * norm + k
            pool.wait_ge(sq_done, KT * norm + k + 1 + 4 * i)
            pool.wait_ge(ss_done, n + 1 + 4 * i)
            pool.tensor_tensor(SS[:, :], SS[:, :], SQ[:, k % 2, :], ALU.add).then_inc(ss_done, 1)

        def add_x(v, m, u0, i=0, ustep=12, inc=1):
            v.wait_ge(full, u0 + 1 + ustep * i)
            v.tensor_tensor(halves(X[:, m, :]), halves(X[:, m, :]), unit(u0), ALU.add).then_inc(free, inc)

        def fu(i0):
            return 0 if i0 == 0 else 6 + 12 * (i0 - 1)

        def fpos(first):
            return ([1, 3], None, [4, 5]) if first else ([0, 1], list(range(2, 10)), [10, 11])

        TAILS = (range(6), range(6, NIT))

        def ffn_pe(pe, L):
            t0, u0 = T_F[L], U_F[L]

            def up(js, us, base, i0, i, first):
                for j, u in zip(js, us):
                    fm_tile(pe, t0 + 4 * i0 + j, u0 + base + u, i, 4, 12, fresh=XLF[L] if first and j == 0 else None)
                    if first and j == 0:
                        stat_cols(pe, u0 + 2, NORM_F[L])

            def down(base, us, i0, i):
                for m, u in enumerate(us):
                    w = u0 + base + u
                    if m == 0:
                        pe.wait_ge(yl, 2 * (NIT * L + i0) + 2 + 2 * i)
                    pe.wait_ge(dlo, 4 * (NIT * L + i0) + m // 2 + 1 + 4 * i)
                    pe.wait_ge(free, w - 3 + 12 * i)
                    for k in range(2):
                        for a, (wt, y) in enumerate(((DH, YH), (DH, YL), (DL, YH))):
                            for f in range(2):
                                mm = pe.matmul(PS[:, 2 * (w % 4) + f, 0:HALF], wt[:, k, 128 * m:128 * m + 128],
                                               y[:, k, f * HALF:(f + 1) * HALF],
                                               start=(k == 0 and a == 0), stop=(k == 1 and a == 2))
                    mm.then_inc(full, 1)

            def last_down(base):
                n = NIT * (L + 1)
                for ms, k in ((range(4), 0), (range(4), 1), (range(4, 8), None)):
                    for m in ms:
                        w = u0 + base + m
                        pe.wait_ge(yl, 2 * n - (1 if k == 0 else 0))
                        if k != 1:
                            pe.wait_ge(dlo, 4 * (n - 1) + m // 2 + 1)
                            pe.wait_ge(free, w - 3)
                        for kk in ([k] if k is not None else [0, 1]):
                            for a, (wt, y) in enumerate(((DH, YH), (DH, YL), (DL, YH))):
                                for f in range(2):
                                    mm = pe.matmul(PS[:, 2 * (w % 4) + f, 0:HALF], wt[:, kk, 128 * m:128 * m + 128],
                                                   y[:, kk, f * HALF:(f + 1) * HALF],
                                                   start=(kk == 0 and a == 0), stop=(kk == 1 and a == 2))
                        if k != 0:
                            mm.then_inc(full, 1)

            def step(i0, i, first=False):
                gu, du, vu = fpos(first)
                b = fu(i0)
                up([0, 1], gu, b, i0, i, first)
                if du:
                    down(b, du, i0 - 1, i)
                up([2, 3], vu, b, i0, i, first)

            pe.wait_ge(s_str, 96 * (L + 1))
            pe.wait_ge(free, u0 - 3)
            for n in range(NIT):
                b = 2 * (u0 % 4) + n // 8
                pe.transpose(PS[:, b, 64 * (n % 8):64 * (n % 8) + 64], STR[:, n, :], ident[0:64, 0:64])
            for c in range(4):
                o = 64 * (NIT - 8) + 2 * FT * c
                mm = pe.transpose(PS[:, b, o:o + 2 * FT], CRAW[:, c, :], ident[0:2 * FT, 0:2 * FT])
            mm.then_inc(full, 1)
            step(0, 0, True)
            with pe.Fori(0, NIT - 2) as i:
                step(1, i)
            step(NIT - 1, 0)
            last_down(fu(NIT - 1) + 12)
            pe.wait_ge(tl_g, 2 * NIT * (L + 1))
            for q, ns in enumerate(TAILS):
                u = u0 + FFN_UNITS - 2 + q
                pe.wait_ge(free, u - 3)
                for j, n in enumerate(ns):
                    mm = pe.transpose(PS[0:72, 2 * (u % 4) + j // 4, 128 * (j % 4):128 * (j % 4) + 128],
                                      TLC[:, n, :, :].rearrange("p a b -> p (a b)"), ident[:, :])
                mm.then_inc(full, 1)

        def ffn_dve(v, L, last, nextvec, nextx):
            t0, u0 = T_F[L], U_F[L]

            def evac(j, u, i, i0, first):
                w = u0 + u
                if first and j == 0:
                    invert(v, RC[NORM_F[L]], False)
                    v.wait_ge(rstd, RC[NORM_F[L]] + 1)
                    inc = 2
                else:
                    inc = 1
                v.wait_ge(full, w + 1 + 12 * i)
                if j == 0 and not first:
                    v.wait_ge(tl_g, 2 * (NIT * L + i0) + 2 * i)
                if j == 0:
                    v.tensor_copy(UB[:, :, SEQ + 2:CW].rearrange("p a (s c) -> p a s c", s=NS)[:, :, :, 0:2],
                                  STC[:, bass.ds(i0 + i, 1), :].rearrange("p o (a s r) -> p (o a) s r", a=4, s=NS))
                b = 2 * (w % 4)
                nb = SEQ - HALF
                v.tensor_tensor(UB[:, j, 2:2 + HALF], PS[:, b, 0:HALF], RB[:, 0:HALF], ALU.mult)
                v.tensor_tensor(UB[:, j, 2 + HALF:2 + SEQ], PS[:, b + 1, 0:nb], RB[:, HALF:SEQ], ALU.mult)
                v.tensor_tensor(UB[:, j, SEQ + 2:CW].rearrange("p (s c) -> p s c", s=NS)[:, :, 2:2 + SL],
                                PS[:, b + 1, nb:HALF].rearrange("p (s c) -> p s c", s=NS),
                                RB[:, SEQ:T].rearrange("p (s c) -> p s c", s=NS), ALU.mult).then_inc(free, inc)

            def tile_col(j, i0, i):
                return (FT if j >= 2 else 0) + j % 2 + 2 * i0 + 2 * i

            def conv_taps(j, i0, i):
                c = tile_col(j, i0, i)
                n = 4 * (NIT * L + i0) + j
                v.wait_ge(t0_done, n + 1 + 4 * i)
                v.scalar_tensor_tensor(out=CB[:, j, :], in0=UB[:, j, 1:1 + CC], scalar=CWT[:, 1, bass.ds(c, 1)],
                                       in1=CB[:, j, :], op0=ALU.mult, op1=ALU.add).then_inc(conv, 1)
                v.wait_ge(conv, 2 * n + 1 + 8 * i)
                v.scalar_tensor_tensor(out=CB[:, j, :], in0=UB[:, j, 2:2 + CC], scalar=CWT[:, 2, bass.ds(c, 1)],
                                       in1=CB[:, j, :], op0=ALU.mult, op1=ALU.add).then_inc(conv, 1)

            def gate(j, i0, i):
                n = 2 * (NIT * L + i0) + j
                v.wait_ge(silu, n + 1 + 2 * i)
                v.wait_ge(conv, 8 * (NIT * L + i0) + 2 * (j + 2) + 2 + 8 * i)
                v.tensor_tensor(Y[:, j, 0:SEQ], CB[:, j, 0:SEQ], CB[:, 2 + j, 0:SEQ], ALU.mult)
                a = CB[:, j, SEQ:CC].rearrange("p (s c) -> p s c", s=NS)[:, :, 2:2 + SL]
                b = CB[:, 2 + j, SEQ:CC].rearrange("p (s c) -> p s c", s=NS)[:, :, 2:2 + SL]
                v.tensor_tensor(Y[:, j, SEQ:T].rearrange("p (s c) -> p s c", s=NS), a, b, ALU.mult).then_inc(y_done, 1)

            def rest_y(j, i0, i):
                n = 2 * (NIT * L + i0) + j
                v.wait_ge(yh, n + 1 + 2 * i)
                v.tensor_tensor(YL[:, j, :], Y[:, j, :], f32(YH[:, j, :]), ALU.subtract).then_inc(yl, 1)

            def rest_down(c, i0, i):
                v.wait_ge(dhi, 4 * (NIT * L + i0) + c + 1 + 4 * i)
                v.tensor_tensor(DL[:, :, 256 * c:256 * c + 256], DRAW[:, :, 256 * c:256 * c + 256],
                                f32(DH[:, :, 256 * c:256 * c + 256]), ALU.subtract).then_inc(dlo, 1)

            def step(i0, i, first=False, ahead=True):
                gu, du, vu = fpos(first)
                b = fu(i0)
                for j, u in zip((0, 1), gu):
                    evac(j, b + u, i, i0, first)
                    if ahead:
                        rest_tile(v, t0 + 4 * i0 + j + 4, i)
                    conv_taps(j, i0, i)
                if du:
                    for m, u in enumerate(du):
                        add_x(v, m, u0 + b + u, i)
                        if m % 2:
                            rest_down(m // 2, i0, i)
                else:
                    for c in range(4):
                        rest_down(c, i0, i)
                for j, u in zip((2, 3), vu):
                    evac(j, b + u, i, i0, first)
                    if ahead:
                        rest_tile(v, t0 + 4 * i0 + j + 4, i)
                    if j == 3:
                        rest_y(0, i0, i)
                    conv_taps(j, i0, i)
                    gate(j - 2, i0, i)
                rest_y(1, i0, i)

            v.memset(UB[:, :, 0:2], 0.0)
            v.wait_ge(full, u0 + 1)
            b = 2 * (u0 % 4)
            v.tensor_copy(STC[:, 0:8, :].rearrange("p n c -> p (n c)"), PS[:, b, :])
            v.tensor_copy(STC[:, 8:NIT, :].rearrange("p n c -> p (n c)"), PS[:, b + 1, 0:64 * (NIT - 8)]).then_inc(st_c, 1)
            v.tensor_copy(CWT[:, :, :].rearrange("p c t -> p (c t)"),
                          PS[:, b + 1, 64 * (NIT - 8):64 * (NIT - 8) + 8 * FT]).then_inc(free, 1)
            v.wait_ge(st_c, L + 1)
            step(0, 0, True)
            with v.Fori(0, NIT - 2) as i:
                step(1, i)
            step(NIT - 1, 0, ahead=not last)
            b = fu(NIT - 1) + 12
            for m in range(8):
                add_x(v, m, u0 + b + m)
                if m and nextvec is not None:
                    rest_x(v, m - 1, nextvec, nextx)
            if nextvec is not None:
                rest_x(v, 7, nextvec, nextx)
            for q, ns in enumerate(TAILS):
                u = u0 + FFN_UNITS - 2 + q
                v.wait_ge(full, u + 1)
                o = TLR[:, ns[0]:ns[-1] + 1, :].rearrange("p n c -> p (n c)")
                v.tensor_copy(o[:, 0:512], PS[0:72, 2 * (u % 4), :])
                v.tensor_copy(o[:, 512:128 * len(ns)], PS[0:72, 2 * (u % 4) + 1, 0:128 * len(ns) - 512]).then_inc(free, 1)

        def ffn_act(act, L, last, nextvec, nextnorm):
            t0, u0 = T_F[L], U_F[L]

            def tap0(j, i0, i, w):
                c = (FT if j >= 2 else 0) + j % 2 + 2 * i0 + 2 * i
                act.wait_ge(free, w + 1 + 12 * i)
                act.activation(CB[:, j, :], UB[:, j, 0:CC], ACT.Identity, scale=CWT[:, 0, bass.ds(c, 1)],
                               bias=CWT[:, 3, bass.ds(c, 1)]).then_inc(t0_done, 1)

            def do_silu(j, i0, i):
                act.wait_ge(conv, 8 * (NIT * L + i0) + 2 * j + 2 + 8 * i)
                act.activation(CB[:, j, :], CB[:, j, :], ACT.Silu).then_inc(silu, 1)

            def round_y(j, i0, i):
                act.wait_ge(y_done, 2 * (NIT * L + i0) + j + 1 + 2 * i)
                act.activation(YH[:, j, :], Y[:, j, :], ACT.Copy).then_inc(yh, 1)

            def round_down(c, i0, i):
                act.activation(DH[:, :, 256 * c:256 * c + 256], DRAW[:, :, 256 * c:256 * c + 256],
                               ACT.Copy).then_inc(dhi, 1)

            def step(i0, i, first=False, ahead=True):
                gu, du, vu = fpos(first)
                b = fu(i0)
                n = NIT * L + i0
                for j, u in zip((0, 1), gu):
                    w = u0 + b + u
                    if first and j == 0:
                        roots(act, u0 + 2, NORM_F[L], False)
                    if ahead:
                        act.wait_ge(full, w + 1 + 12 * i)
                        round_tile(act, t0 + 4 * i0 + j + 4, i)
                    if j == 1:
                        do_silu(0, i0, i)
                    tap0(j, i0, i, w)
                do_silu(1, i0, i)
                for c in range(4):
                    if c == 0:
                        act.wait_ge(s_draw, 16 * (n + 1) + 16 * i)
                    if du:
                        act.wait_ge(full, u0 + b + du[2 * c + 1] + 1 + 12 * i)
                    round_down(c, i0, i)
                for j, u in zip((2, 3), vu):
                    w = u0 + b + u
                    if ahead:
                        act.wait_ge(full, w + 1 + 12 * i)
                        round_tile(act, t0 + 4 * i0 + j + 4, i)
                    if j == 3:
                        round_y(0, i0, i)
                    tap0(j, i0, i, w)
                round_y(1, i0, i)

            step(0, 0, True)
            with act.Fori(0, NIT - 2) as i:
                step(1, i)
            step(NIT - 1, 0, ahead=not last)
            b = fu(NIT - 1) + 12
            for m in range(8):
                act.wait_ge(free, u0 + b + m + 1)
                if nextvec is not None:
                    round_x(act, m, nextvec)
                square_x(act, m, nextnorm)

        def ffn_pool(pool, L):
            u0 = U_F[L]

            def gather(jj, w, i0, i):
                pool.wait_ge(free, w + 1 + 12 * i)
                a = slice(2 * jj, 2 * jj + 2)
                to = TLC[:, bass.ds(i0 + i, 1), a, :].rearrange("p o a c -> p (o a) c")
                pool.tensor_tensor(to[:, :, 0:2], UB[:, a, SEQ:SEQ + 2],
                                   ones[:, 0:4].rearrange("p (a r) -> p a r", a=2), ALU.mult)
                pool.tensor_tensor(to[:, :, 2:18].rearrange("p a (s r) -> p a s r", s=NS),
                                   UB[:, a, SEQ + 2:CW].rearrange("p a (s c) -> p a s c", s=NS)[:, :, :, SL:SL + 2],
                                   ones[:, 0:4 * NS].rearrange("p (a s r) -> p a s r", a=2, s=NS), ALU.mult)\
                    .then_inc(tl_g, 1)

            def step(i0, i, first=False):
                gu, du, vu = fpos(first)
                b = fu(i0)
                gather(0, u0 + b + gu[1], i0, i)
                gather(1, u0 + b + vu[1], i0, i)

            step(0, 0, True)
            with pool.Fori(0, NIT - 2) as i:
                step(1, i)
            step(NIT - 1, 0)

        def conv_loads(sp, L):
            for j in range(4):
                src = A["state_ffn_conv"][L].rearrange("s r (h n two c) -> (s r) h n two c", h=2, two=2, c=128)
                sp.dma_start(STR[16 * j:16 * j + 16, :, :], src[:, j // 2, :, j % 2, :]).then_inc(s_str, 16)
            sp.dma_start(CRAW[:, 0:3, :], A["ffn_conv_w"][L].rearrange("c (t p) -> t c p", p=128)).then_inc(s_str, 16)
            sp.dma_start(CRAW[:, 3, :], A["ffn_conv_b"][L].rearrange("(t p) -> t p", p=128)).then_inc(s_str, 16)

        def tail_stores(sp, L):
            sp.wait_ge(free, U_F[L] + FFN_UNITS)
            for j in range(4):
                for o, r in ((O["conv_p"][L, 0], slice(18 * j, 18 * j + 2)),
                             (O["conv_s"][L].rearrange("s r c -> (s r) c"), slice(18 * j + 2, 18 * j + 18))):
                    sp.dma_start(o.rearrange("r (h n two c) -> r h n two c", h=2, two=2, c=128)[:, j // 2, :, j % 2, :],
                                 TLR[r, :, :]).then_inc(s_tout, 16)

        def ffn_sp(sp, L):
            t0 = T_F[L]

            def step(i0, i):
                for q in range(2):
                    p0 = t0 // 2 + 2 * i0 + q
                    sp.wait_ge(lo_done, 2 * p0 - 2 + 4 * i)
                    src = A["ffn_w_up"][L].rearrange("(k p) n -> p k n", p=128)
                    sp.dma_start(WRAW[:, p0 % 2, :, :], src[:, :, bass.ds(q * DFF + 256 * i0 + 256 * i, 256)])\
                        .then_inc(s_raw[p0 % 2], 16)
                n = NIT * L + i0
                if n:
                    sp.wait_ge(dlo, 4 * n + 4 * i)
                sp.dma_start(DRAW[:, :, :], A["ffn_w_down"][L].rearrange("(t p) n -> p t n", p=128)
                             [:, bass.ds(2 * i0 + 2 * i, 2), :]).then_inc(s_draw, 16)
            step(0, 0)
            with sp.Fori(0, NIT - 1) as i:
                step(1, i)

        def later_piece(sp, p):
            w, c = later[p]
            sp.wait_ge(lo_done, 2 * p - 2)
            sp.dma_start(WRAW[:, p % 2, :, :], w.rearrange("(k p) n -> p k n", p=128)[:, :, c:c + 256])\
                .then_inc(s_raw[p % 2], 16)

        def att_sp(sp):
            for p in (T_KV // 2, T_AQ // 2):
                later_piece(sp, p)
            tail_stores(sp, 0)
            sp.wait_ge(free, U_KV)
            sp.wait_ge(s_tout, 128)
            for dup in range(2):
                for g in range(KVH):
                    sp.dma_start(KCR[:, :, g, dup, :], A["cache_k"][:, :, g, :].rearrange("s k d -> k s d")).then_inc(s_cache, 16)
                    sp.dma_start(VCD[:, :, g, dup, :], A["cache_v"][:, :, g, :].rearrange("s k d -> k s d")).then_inc(s_cache, 16)
            later_piece(sp, T_AQ // 2 + 1)
            sp.wait_ge(free, U_KT)
            sp.dma_start(VS[0:CH, :], VZ[CH:128, :]).then_inc(s_vs, 16)
            sp.dma_start(VS[CH:128, 0:TT - 2], VZ[0:CH, 1:TT - 1]).then_inc(s_vs, 16)
            for s in range(NS):
                r = slice(SL * s, SL * s + SL)
                sp.dma_start(VN[:, s], V4[r]).then_inc(s_vn, 16)
                sp.dma_start(O["k_s"][s, WIN - SL:WIN], KD[r, TT - 1, :, 0, :]).then_inc(s_out, 16)
                sp.dma_start(O["v_s"][s, WIN - SL:WIN], V4[r, :, 0, :]).then_inc(s_out, 16)
            sp.dma_start(O["k_p"][0], KD[:, TT - 2, :, 0, :]).then_inc(s_out, 16)
            sp.dma_start(O["v_p"][0], VZ[:, TT - 2, :, 0:HD]).then_inc(s_out, 16)
            for p in range(T_AQ // 2 + 2, T_AO // 2 + 4):
                later_piece(sp, p)
            sp.wait_ge(a_o, NATT)
            sp.wait_ge(s_out, 16 * N_OUT)
            conv_loads(sp, 1)

        def att_pool(pool):
            pool.wait_ge(free, U_KV)
            pool.wait_ge(s_tout, 128)
            pool.memset(QZ[:, :, :, :, :, :], 0.0).then_inc(azero, 1)
            pool.memset(VZ[:, :, :, HD:2 * HD], 0.0).then_inc(azero, 1)

        N_OUT = 2 + 2 * NS + 2
        KV_UNITS = [0, 3, 4, 5]

        def att_pe(pe):
            pe.wait_ge(xl_done, 3 * KT)
            tm_unit(pe, T_KV, U_KV, TMU[0])
            stat_cols(pe, U_KV + 1, 2)
            stat_rows(pe, U_KV + 2)
            for j in range(1, 4):
                tm_unit(pe, T_KV, U_KV + KV_UNITS[j], TMU[j])
            pe.wait_ge(free, U_KT)
            for g in range(KVH):
                u = U_KT + g
                pe.wait_ge(free, u - 3)
                for t in range(TT):
                    mm = pe.transpose(PS[:, 2 * (u % 4) + t // 4, 128 * (t % 4):128 * (t % 4) + 128],
                                      KD[:, t, g, :, :].rearrange("p a d -> p (a d)"), ident[:, :])
                mm.then_inc(full, 1)
            fm_tile(pe, T_AQ, U_Q, fresh=3 * KT)
            for j in range(1, 4):
                fm_tile(pe, T_AQ + j, U_Q + j)
            for j in range(4, 8):
                fm_tile(pe, T_AQ + j, U_Q + j)
            pe.wait_ge(s_cache, 16 * 8)
            for g in range(KVH):
                u = U_KC + g
                pe.wait_ge(free, u - 3)
                for s in range(NS):
                    mm = pe.transpose(PS[:, 2 * (u % 4) + s // 4, 128 * (s % 4):128 * (s % 4) + 128],
                                      KCR[:, s, g, :, :].rearrange("p a d -> p (a d)"), ident[:, :])
                mm.then_inc(full, 1)
            pe.wait_ge(free, U_AO)
            pe.wait_ge(s_vs, 16 * 2)

            def scores(n):
                if n >= 2:
                    pe.wait_ge(a_ex, n - 1)
                b = n % 2
                if n < NATT - NS:
                    c, m, g = step_of(n)
                    k0, nk = window(c)
                    for a in range(2):
                        h = slice(HD * a, HD * a + HD)
                        mm = pe.matmul(PS[:, 2 * b + a, 0:nk], QF[h, m // 2, c, :, :].rearrange("p m q -> p (m q)"),
                                       KTD[h, g, k0:k0 + nk], start=True, stop=True, tile_position=(HD * a, 0))
                else:
                    s = n - (NATT - NS)
                    if s == 0:
                        pe.wait_ge(qz, 16)
                    for g in range(KVH):
                        mm = pe.matmul(PS[:, 2 * b + g, 0:WIN + SL],
                                       QZ[:, s, g, :, :, :].rearrange("p e m t -> p (e m t)"), KCT[:, g, s, :],
                                       start=True, stop=True)
                mm.then_inc(a_sc, 1)

            def transposes(n):
                pe.wait_ge(a_p, n + 1)
                if n >= 2:
                    pe.wait_ge(a_pt, n - 1)
                for a in range(2):
                    for x, k in enumerate(key_parts(n)):
                        mm = pe.transpose(PS[0:k, 4 + n % 2, 256 * a + 128 * x:256 * a + 128 * x + 128],
                                          P[:, n % 2, 256 * a + 128 * x:256 * a + 128 * x + k], ident[:, :])
                mm.then_inc(a_tr, 1)

            def values(n):
                pe.wait_ge(a_pt, n + 1)
                if n >= 2:
                    pe.wait_ge(a_ol, n - 1)
                b = 6 + n % 2
                if n < NATT - NS:
                    c, m, g = step_of(n)
                    ops = [(a, x, k) for a in range(2) for x, k in enumerate(key_parts(n))]
                    for j, (a, x, k) in enumerate(ops):
                        vv = VS if c % 2 and c > 1 else VZ
                        t = max(c // 2 - 1, 0) + x
                        mm = pe.matmul(PS[:, b, 0:128], vv[0:k, t, g, HD * a:HD * a + 128],
                                       PT[0:k, n % 2, 256 * a + 128 * x:256 * a + 128 * x + 128],
                                       start=(j == 0), stop=(j == len(ops) - 1))
                else:
                    s = n - (NATT - NS)
                    if s == 0:
                        pe.wait_ge(s_vn, 16 * NS)
                    for g in range(KVH):
                        o = PS[:, b, 128 * g:128 * g + 128]
                        pe.matmul(o, VCD[:, s, g, :, :].rearrange("p e d -> p (e d)"),
                                  PT[:, n % 2, 256 * g:256 * g + 128], start=True, stop=False)
                        mm = pe.matmul(o, VN[:, s, g, :, :].rearrange("p e d -> p (e d)"),
                                       PT[0:SL, n % 2, 256 * g + 128:256 * g + 256], start=False, stop=True)
                mm.then_inc(a_o, 1)

            for n in range(NATT + 3):
                if n < NATT:
                    scores(n)
                if 2 <= n < NATT + 2:
                    transposes(n - 2)
                if n >= 3:
                    values(n - 3)
            pe.wait_ge(a_ol, NATT)
            with pe.Fori(0, 2) as i:
                for j in range(4):
                    fm_tile(pe, T_AO + j, U_AO + j, i)

        def qf_view(i, j):
            return QF[:, bass.ds(2 * i + j // 2, 1), :, j % 2, :].rearrange("p o (a c) q -> p (o a) c q", a=2)

        def step_of(n):
            c, m = n // 4, 2 * (n % 4)
            return c, m, m // 4

        def window(c):
            return CH * max(c - 2, 0), CH * min(c + 1, 3)

        def key_parts(n):
            if n >= NATT - NS:
                return [WIN, SL]
            nk = window(step_of(n)[0])[1]
            return [nk] if nk <= 128 else [128, nk - 128]

        def heads_out(n, a):
            b = 6 + n % 2
            if n < NATT - NS:
                c, m, _ = step_of(n)
                return [PS[:, b, 0:128].rearrange("p (m q) -> p m q", m=2)] + \
                    [x[:, m:m + 2, CH * c:CH * c + CH] for x in (XH, XL)]
            s = n - (NATT - NS)
            h = slice(HD * a, HD * a + HD)
            c = SEQ + SL * s
            return [PS[h, b, 0:256].rearrange("p (g e m t) -> p g e m t", g=KVH, e=2, m=4)[:, :, a, :, :]] + \
                [x[h, :, c:c + SL].rearrange("p (g m) t -> p g m t", g=KVH) for x in (XH, XL)]

        def parts(n):
            return range(1 if n < NATT - NS else 2)

        def att_dve(v):
            invert(v, RC[2], True)
            v.wait_ge(rstd, RC[2] + 2)
            v.wait_ge(azero, 5)
            for j, groups in enumerate(TMU):
                u = U_KV + KV_UNITS[j]
                v.wait_ge(full, u + 1)
                for f, t in enumerate(groups):
                    k = PS[:, 2 * (u % 4) + f, 0:KVH * HD].rearrange("p (g d) -> p g d", g=KVH)
                    vv = PS[:, 2 * (u % 4) + f, KVH * HD:256].rearrange("p (g d) -> p g d", g=KVH)
                    for dup in range(2):
                        v.tensor_scalar(KD[:, t, :, dup, :], k, RT[:, t:t + 1], None, ALU.mult)
                        o = V4[:, :, dup, :] if t == TT - 1 else VZ[:, t, :, 2 * HD * dup:2 * HD * dup + HD]
                        mm = v.tensor_scalar(o, vv, RT[:, t:t + 1], None, ALU.mult)
                mm.then_inc(free, 3 if j == 0 else 1)
            for k in range(KT):
                rest_x(v, k, V_MIX + KT, XF[0] + 2 * KT)
            for n in (T_AQ + 2, T_AQ + 3):
                rest_tile(v, n)
            for g in range(KVH):
                u = U_KT + g
                v.wait_ge(full, u + 1)
                v.tensor_copy(KTD[:, g, :], PS[:, 2 * (u % 4), :])
                v.tensor_copy(KCT[:, g, :, WIN:WIN + SL], PS[:, 2 * (u % 4) + 1, 0:NS * SL]
                              .rearrange("p (s t) -> p s t", s=NS)).then_inc(free, 1)
            v.wait_ge(s_sink, 16)
            for half in range(2):
                rows = slice(CH * half, CH * half + CH)
                v.tensor_copy(SKP[rows, :].rearrange("p (m e) -> p m e", e=2),
                              SKB[rows, :].rearrange("p (m f e) -> p m f e", f=2, e=2)[:, :, half, :])
            v.tensor_tensor(SKT[:, :], SKB[:, :], HB[:, :], ALU.mult).then_inc(sink_v, 1)
            v.wait_ge(sink_v, 1)
            v.tensor_reduce(SKR[:, :], SKT[:, :].rearrange("p (g h) -> p g h", g=KVH), AX.X, ALU.add).then_inc(sink_v, 1)
            with v.Fori(0, 2) as i:
                for j in range(4):
                    v.wait_ge(full, U_Q + j + 1 + 4 * i)
                    v.scalar_tensor_tensor(out=qf_view(i, j), in0=unit(U_Q + j).rearrange("p a (c q) -> p a c q", q=CH),
                                           scalar=HD ** -0.5, in1=RB[:, :].rearrange("p (a c q) -> p a c q", a=2, q=CH),
                                           op0=ALU.mult, op1=ALU.mult).then_inc(free, 1)
                    rest_tile(v, T_AQ + 4 + j, i)
            for g in range(KVH):
                u = U_KC + g
                v.wait_ge(full, u + 1)
                v.tensor_copy(KCT[:, g, :, 0:WIN].rearrange("p (b s) k -> p b s k", b=2),
                              PS[:, 2 * (u % 4):2 * (u % 4) + 2, :].rearrange("p b (s k) -> p b s k", k=WIN))\
                    .then_inc(free, 1)

            def maxima(n):
                v.wait_ge(a_sc, n + 1)
                b = n % 2
                sc = PS[:, 2 * b:2 * b + 2, 0:sum(key_parts(n))]
                sink = SKP[:, 2 * (n % 4):2 * (n % 4) + 2] if n < NATT - NS else SKR[:, :]
                v.tensor_reduce(NM[:, b, :], sc, AX.X, ALU.max).then_inc(a_chain, 1)
                v.wait_ge(a_chain, 2 * n + 1)
                v.tensor_tensor(NM[:, b, :], NM[:, b, :], sink, ALU.max).then_inc(a_chain, 1)
                v.wait_ge(a_chain, 2 * n + 2)
                v.tensor_tensor(SE[:, b, :], sink, NM[:, b, :], ALU.subtract)
                v.tensor_scalar(NM[:, b, :], NM[:, b, :], -1.0, None, ALU.mult).then_inc(a_nm, 1)

            def normalise(n):
                b = n % 2
                v.wait_ge(a_ex, n + 1)
                v.tensor_tensor(ES[:, b, :], ES[:, b, :], SE[:, b, :], ALU.add).then_inc(a_sum, 1)
                v.wait_ge(a_sum, 2 * n + 1)
                v.reciprocal(ES[:, b, :], ES[:, b, :]).then_inc(a_sum, 1)
                v.wait_ge(a_sum, 2 * n + 2)
                for a in range(2):
                    w = prob_cols(n, a)
                    mm = v.tensor_scalar(P[:, b, w], P[:, b, w], ES[:, b, a:a + 1], None, ALU.mult)
                mm.then_inc(a_p, 1)

            def rest_out(n):
                v.wait_ge(a_oh, n + 1)
                for a in parts(n):
                    i_, oh, ol = heads_out(n, a)
                    mm = v.tensor_tensor(ol, i_, f32(oh), ALU.subtract)
                mm.then_inc(a_ol, 1)

            def spread_queries(g, e, cc, m):
                h = slice(HD * e, HD * e + HD)
                v.tensor_copy(QZ[h, 4 * cc:4 * cc + 4, g, e, m:4:2, :].rearrange("p s m t -> p m s t"),
                              QF[h, 2 * g:2 * g + 2, SEQ // CH + cc, m, :].rearrange("p m (s t) -> p m s t", t=SL))\
                    .then_inc(qz, 1)

            v.wait_ge(free, U_KC)
            for n in range(NATT + 3):
                if 4 <= n < 20:
                    spread_queries((n - 4) // 8, (n - 4) // 4 % 2, (n - 4) // 2 % 2, n % 2)
                if n < NATT:
                    maxima(n)
                if 1 <= n <= NATT:
                    normalise(n - 1)
                if n >= 3:
                    rest_out(n - 3)
            with v.Fori(0, 2) as i:
                for j in range(4):
                    v.wait_ge(full, U_AO + j + 1 + 4 * i)
                    xm = halves(X[:, bass.ds(4 * i + j, 1), :].rearrange("p a t -> p (a t)"))
                    v.tensor_tensor(xm, xm, unit(U_AO + j), ALU.add).then_inc(free, 1)
                    rest_tile(v, T_AO + 4 + j, i)
            for k in range(KT):
                rest_x(v, k, V_FFN + KT, XF[1])

        def prob_cols(n, a):
            return slice(256 * a, 256 * a + sum(key_parts(n)))

        def att_act(act):
            roots(act, U_KV + 1, 2, True)
            act.wait_ge(full, U_KV + 6)
            for k in range(KT):
                round_x(act, k, V_MIX + KT)
            for n in (T_AQ + 2, T_AQ + 3):
                round_tile(act, n)
            with act.Fori(0, 2) as i:
                for j in range(4):
                    act.wait_ge(full, U_Q + j + 1 + 4 * i)
                    round_tile(act, T_AQ + 4 + j, i)

            def exponentials(n):
                b = n % 2
                act.wait_ge(a_nm, n + 1)
                if n >= 2:
                    act.wait_ge(a_tr, n - 1)
                for a in range(2):
                    w = prob_cols(n, a)
                    act.activation(P[:, b, w], PS[:, 2 * b + a, 0:w.stop - w.start], ACT.Exp, bias=NM[:, b, a:a + 1], accum_out=ES[:, b, a:a + 1])
                act.activation(SE[:, b, :], SE[:, b, :], ACT.Exp).then_inc(a_ex, 1)

            def to_sbuf(n):
                act.wait_ge(a_tr, n + 1)
                if n >= 2:
                    act.wait_ge(a_o, n - 1)
                b = n % 2
                o, i_ = [x.rearrange("p (a k) -> p a k", a=2) for x in (PT[:, b, :], PS[:, 4 + b, :])]
                parts = key_parts(n)
                if parts[-1] == CH:
                    w = 128 * len(parts)
                    k = 128 if len(parts) == 2 else CH
                    act.activation(o[0:k, :, 0:w], i_[0:k, :, 0:w], ACT.Copy).then_inc(a_pt, 1)
                else:
                    for x, k in enumerate(parts):
                        w = slice(128 * x, 128 * x + 128)
                        mm = act.activation(o[0:k, :, w], i_[0:k, :, w], ACT.Copy)
                    mm.then_inc(a_pt, 1)

            def round_out(n):
                act.wait_ge(a_o, n + 1)
                for a in parts(n):
                    i_, oh, _ = heads_out(n, a)
                    mm = act.activation(oh, i_, ACT.Copy)
                mm.then_inc(a_oh, 1)

            act.wait_ge(free, U_AO)
            for n in range(NATT + 3):
                if 2 <= n < NATT + 2:
                    to_sbuf(n - 2)
                if n < NATT:
                    exponentials(n)
                if n >= 3:
                    round_out(n - 3)
            with act.Fori(0, 2) as i:
                for j in range(4):
                    act.wait_ge(full, U_AO + j + 1 + 4 * i)
                    round_tile(act, T_AO + 4 + j, i)
                    act.wait_ge(free, U_AO + j + 1 + 4 * i)
                    square_x(act, j, 3, 4 * i + j, i)
            for k in range(KT):
                round_x(act, k, V_FFN + KT)

        Y_UNITS = [0, 1, 2, 4, 5]

        def final_pe(pe):
            def group(t):
                u = U_Y + Y_UNITS[t]
                pe.wait_ge(free, u - 3)
                for k in range(KT):
                    if t == 0:
                        pe.wait_ge(free, U_Y - 2 - KT + k + 1)
                    mm = pe.transpose(PS[:, 2 * (u % 4) + k // 4, 128 * (k % 4):128 * (k % 4) + 128],
                                      X[:, k, 128 * t:128 * t + 128], ident[:, :])
                mm.then_inc(full, 1)

            for t in range(3):
                group(t)
            pe.wait_ge(ss_done, (KT + 1) * 5)
            stat_rows(pe, U_Y + 3)
            group(3)
            group(4)

        def final_act(act):
            act.wait_ge(full, U_Y + 4)
            act.activation(RT[:, :], PS[:, 2 * ((U_Y + 3) % 4), 0:TT], ACT.Sqrt, bias=eps[:, 0:1],
                           scale=1.0 / D).then_inc(rt_sq, 1)

        def final_dve(v):
            v.wait_ge(rt_sq, RC[4] + 1)
            v.reciprocal(RT[:, :], RT[:, :]).then_inc(rstd, 1)
            v.wait_ge(rstd, RC[4] + 1)
            v.wait_ge(s_nfb, 16)
            for t in range(TT):
                u = U_Y + Y_UNITS[t]
                v.wait_ge(full, u + 1)
                v.scalar_tensor_tensor(out=YO[:, t, :], in0=PS[:, 2 * (u % 4):2 * (u % 4) + 2, :].rearrange("p b c -> p (b c)"),
                                       scalar=RT[:, t:t + 1], in1=NFB[:, :], op0=ALU.mult, op1=ALU.mult)\
                    .then_inc(free, 2 if t == 2 else 1)

        def final_sp(sp):
            yp = O["y_p"][0].rearrange("(t p) d -> p t d", p=128)
            ys = O["y_s"].rearrange("s l d -> (s l) d")
            sp.wait_ge(full, U_F[1] + fu(NIT - 1) + 12)
            sp.dma_start(NFB[:, :], A["norm_final"].rearrange("(o n) -> o n", o=1).to_broadcast([128, D])).then_inc(s_nfb, 16)
            tail_stores(sp, 1)
            for t in range(TT):
                sp.wait_ge(free, U_Y + Y_UNITS[t] + 1)
                sp.dma_start(yp[:, t, :] if t < TT - 1 else ys, YO[:, t, :]).then_inc(s_y, 16)
            sp.wait_ge(s_y, 16 * TT)
            sp.wait_ge(s_tout, 2 * 128)
            sp.wait_ge(s_out, 16 * N_OUT)


        def front_sp(sp):
            xp = A["x_prompt"][0].rearrange("(t p) d -> p t d", p=128)
            xs = A["x_sample"].rearrange("s l d -> (s l) d")
            vecs = ((0, A["norm_mix"].rearrange("l (k p) -> (l k) p", p=128)),
                    (16, A["norm_ffn"].rearrange("l (k p) -> (l k) p", p=128)),
                    (32, A["norm_kv"].rearrange("(k p) -> k p", p=128)),
                    (40, A["norm_final"].rearrange("(k p) -> k p", p=128)),
                    (48, A["gla_g_onorm"][0].rearrange("(k p) -> k p", p=128)),
                    (50, A["gla_b_g2"][0].rearrange("(k p) -> k p", p=128)))
            for t, (r, v) in enumerate(vecs):
                if t < TT:
                    sp.dma_start(XIN[:, t, :], xp[:, t, :] if t < TT - 1 else xs).then_inc(s_xin, 16)
                sp.dma_start(NRAW[r:r + v.shape[0], :], v).then_inc(s_const, 16)
            for p, (w, c) in enumerate(pieces[:2]):
                sp.dma_start(WRAW[:, p, :, :], w.rearrange("(k p) n -> p k n", p=128)[:, :, c:c + 256])\
                    .then_inc(s_raw[p], 16)
            sp.dma_start(SKB[:, :], A["att_sinks"].to_broadcast([128, NH])).then_inc(s_sink, 16)
            for o, c in (("k_s", "cache_k"), ("v_s", "cache_v")):
                sp.dma_start(O[o][:, 0:WIN - SL], A[c][:, SL:WIN]).then_inc(s_out, 16)
            sp.wait_ge(s_setup, 1)
            sp.dma_start(G2[128 - RANK:128, :], A["gla_w_g2"][0]).then_inc(s_g2, 16)
            sp.wait_ge(free, U_X + KT)
            sp.dma_start(XSP, X[:, :, :]).then_inc(s_spill, 16)

            def piece(p):
                w, c = pieces[p]
                sp.wait_ge(lo_done, 2 * p - 2)
                sp.dma_start(WRAW[:, p % 2, :, :], w.rearrange("(k p) n -> p k n", p=128)[:, :, c:c + 256])\
                    .then_inc(s_raw[p % 2], 16)

            for p in range(2, T_WO // 2 + 2):
                piece(p)
            for h in range(H):
                if h == 0:
                    sp.wait_ge(full, U_Z + 4)
                else:
                    sp.wait_ge(st_done, 8 * (h - 1) + 4)
                    sp.dma_start(O["gla_s"][0, :, h - 1].rearrange("s p d -> p s d"), S0[:, :, :]).then_inc(s_sout, 16)
                    sp.wait_ge(s_sout, 16 * h)
                sp.dma_start(S0[:, :, :], A["state_gla"][0, :, h].rearrange("s p d -> p s d")).then_inc(s_s0, 16)
                if h:
                    sp.wait_ge(st_done, 8 * h)
                    sp.dma_start(O["gla_p"][0, 0, h - 1], ST[:, :]).then_inc(s_pout, 16)
            sp.wait_ge(st_done, 8 * H)
            sp.dma_start(O["gla_s"][0, :, H - 1].rearrange("s p d -> p s d"), S0[:, :, :]).then_inc(s_sout, 16)
            sp.dma_start(O["gla_p"][0, 0, H - 1], ST[:, :]).then_inc(s_pout, 16)
            sp.wait_ge(att, STEPS)
            sp.dma_start(X[:, :, :], XSP).then_inc(s_xback, 16)
            for p in range(T_WO // 2 + 2, T_WO // 2 + 4):
                piece(p)
            sp.wait_ge(full, U_WO)
            conv_loads(sp, 0)
            sp.wait_ge(s_sout, 16 * H)
            sp.wait_ge(s_pout, 16 * H)

        def front_pool(pool):
            pool.memset(G2[:, :], 0.0).then_inc(s_setup, 1)
            pool.memset(ident[:, :], 0.0).then_inc(s_setup, 1)
            pool.memset(ones[:, :], 1.0).then_inc(s_setup, 1)
            pool.memset(EPSC[:, 0:1], EPS)
            pool.memset(EPSC[:, 1:2], DK * EPS).then_inc(s_setup, 1)
            pool.memset(EV[:, :], 1.0).then_inc(s_setup, 1)
            pool.wait_ge(s_setup, 5)
            pool.affine_select(out=ident[:, :], in_=ident[:, :], compare_op=ALU.not_equal, fill=1.0, base=0,
                               pattern=[[-1, 128]], channel_multiplier=1).then_inc(s_setup, 1)
            pool.affine_select(out=EV[:, :], in_=EV[:, :], compare_op=ALU.is_ge, fill=0.0, base=0,
                               pattern=[[-2 * SL, 4]], channel_multiplier=1).then_inc(s_setup, 1)
            pool.wait_ge(s_setup, 7)
            pool.affine_select(out=EV[:, :], in_=EV[:, :], compare_op=ALU.is_ge, fill=0.0, base=SL - 1,
                               pattern=[[2 * SL, 4]], channel_multiplier=-1).then_inc(s_setup, 1)
            clear_sums(pool, 0)
            for k in range(KT):
                add_squares(pool, k, 0)
            pool.memset(HB[:, :], 1.0).then_inc(azero, 1)
            pool.wait_ge(azero, 1)
            bands = [[0, KVH], [-SL, 4], [-HD, 2]]
            pool.affine_select(out=HB[:, :], in_=HB[:, :], compare_op=ALU.is_ge, fill=0.0, base=0,
                               pattern=bands, channel_multiplier=1).then_inc(azero, 1)
            pool.wait_ge(azero, 2)
            pool.affine_select(out=HB[:, :], in_=HB[:, :], compare_op=ALU.is_ge, fill=0.0, base=SL - 1,
                               pattern=[[0, KVH], [SL, 4], [HD, 2]], channel_multiplier=-1).then_inc(azero, 1)
            pool.wait_ge(s_spill, 16)
            pool.wait_ge(xl_done, KT)
            pool.memset(MASK[:, :, :], 0.0).then_inc(s_mask, 1)
            pool.wait_ge(s_mask, 1)
            n = 1
            m0 = MASK[:, 0, :].rearrange("p (b r) -> p b r", r=BLK)
            views = [(m0, 128 // BLK, BLK)]
            for l in range(1, 4):
                hf = BLK << (l - 1)
                views.append((MASK[:, l, :].rearrange("p (s two r) -> p s two r", two=2, r=hf)[:, :, 1, :], 64 // hf, hf))
            for v, _, _ in views:
                pool.memset(v, 1.0).then_inc(s_mask, 1)
                n += 1
            pool.wait_ge(s_mask, n)
            for l, (v, ns, w) in enumerate(views):
                sup = w if l == 0 else 2 * w
                pool.affine_select(out=v, in_=v, compare_op=ALU.is_ge, fill=0.0, base=0,
                                   pattern=[[-sup, ns], [0, w]], channel_multiplier=1).then_inc(s_mask, 1)
                n += 1
            pool.wait_ge(s_mask, n)
            pool.affine_select(out=m0, in_=m0, compare_op=ALU.is_ge, fill=0.0, base=0,
                               pattern=[[BLK, 128 // BLK], [1, BLK]], channel_multiplier=-1).then_inc(s_mask, 1)
            for l, (v, ns, w) in list(enumerate(views))[1:]:
                pool.affine_select(out=v, in_=v, compare_op=ALU.is_ge, fill=0.0, base=w - 1,
                                   pattern=[[2 * w, ns], [0, w]], channel_multiplier=-1).then_inc(s_mask, 1)
            pool.wait_ge(full, U_Z + 4)
            pool.memset(QM[:, :], 0.0).then_inc(zset, 1)
            pool_kr(pool, 0)
            pool_operands(pool, 0)
            for h in range(H):
                if h:
                    pool_kr(pool, h)
                pool_levels(pool, h)
                if h:
                    pool_operands(pool, h)
                pool_level_operands(pool, h)
            clear_sums(pool, 1)
            with pool.Fori(0, 2) as i:
                for k in range(4):
                    add_squares(pool, k, 1, i)

        NMASK = 1 + 4 + 4 + 4

        def kq_view(i, j):
            return QK[:, bass.ds(4 * i + j, 1), :].rearrange("p a t -> p (a t)")

        def front_pe(pe):
            pe.wait_ge(s_setup, 8)
            pe.wait_ge(s_const, 16 * 6)
            pe.transpose(PS[:, 0, 0:NVEC], NRAW[:, :], ident[0:NVEC, 0:NVEC]).then_inc(full, 1)
            pe.wait_ge(s_xin, 16 * TT)
            for k in range(KT):
                u = U_X + k
                if u >= 4:
                    pe.wait_ge(free, u - 3)
                for t in range(TT):
                    mm = pe.transpose(PS[:, 2 * (u % 4) + t // 4, 128 * (t % 4):128 * (t % 4) + 128],
                                      XIN[:, t, 128 * k:128 * k + 128], ident[:, :])
                mm.then_inc(full, 1)
            fm_tile(pe, T_GL + 1, U_GL, fresh=0)
            stat_cols(pe, U_GL + 1, 0)
            stat_rows(pe, U_GL + 2)
            with pe.Fori(0, 2) as i:
                for j in range(4):
                    fm_tile(pe, T_KQ + j, U_KQ + j, i)
            pe.wait_ge(s_g2, 16)
            for h in range(H):
                u = U_Z + h
                pe.wait_ge(free, u - 3)
                for f in range(2):
                    mm = pe.matmul(PS[:, 2 * (u % 4) + f, 0:HALF], G2[:, DK * h:DK * h + DK],
                                   GLS[:, f * HALF:(f + 1) * HALF], start=True, stop=True)
                mm.then_inc(full, 1)
            for t0, u0 in ((T_V, U_V), (T_R, U_R)):
                with pe.Fori(0, 2) as i:
                    for q in range(2):
                        for j, groups in enumerate(TMU):
                            tm_unit(pe, t0 + 2 * q, u0 + 4 * q + j, groups, i)
            gla_pe(pe)
            pe.wait_ge(att, STEPS)
            pe.wait_ge(osq, STEPS)
            pe.wait_ge(st_done, 8 * H)
            pe.wait_ge(ogh, H - 1)
            for gs in (range(4), range(4, TT)):
                for part in (range(KT - 2), range(KT - 2, KT)):
                    for g in gs:
                        u = U_OT + g
                        if g == 4:
                            pe.wait_ge(free, u - 3)
                        if part[0]:
                            pe.wait_ge(ogn, g + 1)
                        for kt in part:
                            mm = pe.transpose(PS[:, 2 * (u % 4) + kt // 4, 128 * (kt % 4):128 * (kt % 4) + 128],
                                              RS[:, g, 128 * kt:128 * kt + 128], ident[:, :])
                        if part[0]:
                            mm.then_inc(full, 1)
            fm_tile_halves(pe, T_WO, U_WO, (U_OT + 3, U_OT + TT))
            for j in range(1, 4):
                fm_tile(pe, T_WO + j, U_WO + j)
            for j in range(4, 8):
                fm_tile(pe, T_WO + j, U_WO + j)

        def front_dve(v):
            v.wait_ge(full, 1)
            v.tensor_copy(NW[:, :], PS[:, 0, 0:NVEC]).then_inc(free, 1)
            v.wait_ge(free, 1)
            for k in range(KT):
                u = U_X + k
                v.wait_ge(full, u + 1)
                v.tensor_copy(X[:, k, 0:512], PS[:, 2 * (u % 4), :])
                v.tensor_copy(X[:, k, 512:T], PS[:, 2 * (u % 4) + 1, 0:T - 512]).then_inc(free, 1)
                if k:
                    rest_x(v, k - 1, V_MIX, 0)
                if k in (3, 5):
                    rest_tile(v, k // 2 - 1)
            rest_x(v, KT - 1, V_MIX, 0)
            rest_tile(v, 2)
            rest_tile(v, 3)
            v.wait_ge(s_setup, 8)
            v.tensor_reduce(EO[:, 0:1], EV[:, :], AX.X, ALU.add).then_inc(dve, 1)
            v.wait_ge(dve, 1)
            v.tensor_scalar(EO[:, 1:2], EO[:, 0:1], -1.0, 1.0, ALU.mult, ALU.add).then_inc(dve, 1)
            invert(v, 0, True)
            v.wait_ge(rstd, 2)
            v.tensor_tensor(halves(GLS[:, :]), unit(U_GL), halves(RB[:, :]), ALU.mult).then_inc(free, 3)
            for n in (4, 5):
                rest_tile(v, n)
            with v.Fori(0, 2) as i:
                for j in range(4):
                    v.wait_ge(full, U_KQ + j + 1 + 4 * i)
                    v.tensor_tensor(halves(kq_view(i, j)), unit(U_KQ + j), halves(RB[:, :]), ALU.mult)\
                        .then_inc(free, 1)
                    rest_tile(v, T_KQ + 4 + j, i)
            v.wait_ge(s_spill, 16)
            v.wait_ge(xh_done, KT)
            v.wait_ge(sq_done, KT)
            v.memset(M16[:, :], 1.0).then_inc(dve, 1)
            v.memset(M128[:, :], 1.0).then_inc(dve, 1)
            v.wait_ge(dve, 4)
            v.memset(M16[:, 0:T:BLK], 0.0).then_inc(dve, 1)
            v.memset(M128[:, 0:SEQ:128], 0.0).then_inc(dve, 1)
            v.memset(M128[:, SEQ:T:SL], 0.0).then_inc(dve, 1)
            for h in range(H):
                v.wait_ge(full, U_Z + h + 1)
                v.wait_ge(s_mn, h + 1)
                v.tensor_scalar(halves(LA[:, h, :]), unit(U_Z + h), NW[:, V_BG + h:V_BG + h + 1], 0.0,
                                ALU.add, ALU.min).then_inc(free, 1)
            v.wait_ge(s_mn, H + 2)
            v.wait_ge(free, U_V)
            v.tensor_tensor(LA[:, :, :], LA[:, :, :], AB[:, :, :], ALU.subtract).then_inc(s_la, 1)
            v.wait_ge(s_la, 1)
            v.wait_ge(dve, 7)
            with v.Fori(0, 2) as i:
                for q in range(2):
                    for j, groups in enumerate(TMU):
                        u = U_V + 4 * q + j
                        v.wait_ge(full, u + 1 + 8 * i)
                        for f, t in enumerate(groups):
                            mm = v.tensor_scalar(V[:, t, bass.ds(256 * q + 512 * i, 256)],
                                                 PS[:, 2 * (u % 4) + f, 0:256], RT[:, t:t + 1], None, ALU.mult)
                        mm.then_inc(free, 1)
                    for n in range(2):
                        rest_tile(v, T_V + 4 + 2 * q + n, i)
            gla_sums(v, 0)
            gla_operands(v, 0)
            gla_queries(v, 0)
            with v.Fori(0, 2) as i:
                for n in range(4):
                    rest_tile(v, T_R + 4 + n, i)
            gla_dve(v)
            head_inverse(v, H - 1)
            v.wait_ge(rt_h, 2 * H)
            v.wait_ge(og, STEPS)
            for g in range(TT):
                scale_head(v, H - 1, g).then_inc(ogn, 1)
            for g in range(TT):
                u = U_OT + g
                v.wait_ge(xh_done, KT + g + 1)
                for e in range(2):
                    i_, oh, ol = ot_views(u, g, e)
                    mm = v.scalar_tensor_tensor(out=ol, in0=i_, scalar=NW[:, V_ON + e:V_ON + e + 1], in1=f32(oh),
                                                op0=ALU.mult, op1=ALU.subtract)
                mm.then_inc(free, 1)
            v.wait_ge(s_xback, 16)
            with v.Fori(0, 2) as i:
                for j in range(4):
                    v.wait_ge(full, U_WO + j + 1 + 4 * i)
                    xm = halves(X[:, bass.ds(4 * i + j, 1), :].rearrange("p a t -> p (a t)"))
                    v.tensor_tensor(xm, xm, unit(U_WO + j), ALU.add).then_inc(free, 1)
                    rest_tile(v, T_WO + 4 + j, i)
            for k in range(KT):
                rest_x(v, k, V_FFN, XF[0])

        def head_root(act, h):
            c = slice(TT * h, TT * h + TT)
            act.wait_ge(osq, TT * (h + 1))
            act.activation(RH[:, c], SSH[:, c], ACT.Sqrt, scale=1.0 / DV, bias=eps[:, 1:2]).then_inc(rt_h, 1)

        def head_inverse(v, h):
            c = slice(TT * h, TT * h + TT)
            v.wait_ge(rt_h, 2 * h + 1)
            v.reciprocal(RH[:, c], RH[:, c]).then_inc(rt_h, 1)

        def scale_head(e, h, g):
            r_, n = RS[:, g, DV * h:DV * h + DV], RH[:, TT * h + g:TT * h + g + 1]
            if h == H - 1:
                return e.tensor_scalar(r_, r_, n, None, ALU.mult)
            return e.activation(r_, r_, ACT.Copy, scale=n)

        def ot_views(u, g, e):
            b = 2 * (u % 4)
            i_ = PS[:, b:b + 2, :].rearrange("p b (c e q) -> p b c e q", c=2, e=2)[:, :, :, e, :]
            o_ = [x[:, :, 128 * g:128 * g + 128].rearrange("p (b c e) q -> p b c e q", b=2, c=2)[:, :, :, e, :]
                  for x in (XH, XL)]
            return i_, o_[0], o_[1]

        def front_act(act):
            for k in range(KT):
                act.wait_ge(free, U_X + k + 1)
                round_x(act, k, V_MIX)
                square_x(act, k, 0)
                if k in (1, 3):
                    round_tile(act, k // 2)
            round_tile(act, 2)
            round_tile(act, 3)
            roots(act, U_GL + 1, 0, True)
            act.wait_ge(full, U_GL + 1)
            for n in (4, 5):
                round_tile(act, n)
            with act.Fori(0, 2) as i:
                for j in range(4):
                    act.wait_ge(full, U_KQ + j + 1 + 4 * i)
                    round_tile(act, T_KQ + 4 + j, i)
            for h in range(H):
                act.wait_ge(full, U_Z + h + 1)
                act.activation(halves(AB[:, h, :]), unit(U_Z + h), ACT.Abs, bias=NW[:, V_BG + h:V_BG + h + 1])\
                    .then_inc(s_mn, 1)
            act.wait_ge(s_mn, H)
            act.activation(AB[:, :, :], AB[:, :, :], ACT.Exp, scale=-1.0).then_inc(s_mn, 1)
            act.wait_ge(s_mn, H + 1)
            act.activation(AB[:, :, :], AB[:, :, :], ACT.Ln, bias=1.0).then_inc(s_mn, 1)
            with act.Fori(0, 2) as i:
                for q in range(2):
                    act.wait_ge(full, U_V + 4 * q + 4 + 8 * i)
                    for n in range(2):
                        round_tile(act, T_V + 4 + 2 * q + n, i)
            gla_exps(act, 0)
            act.wait_ge(free, U_R)
            act.wait_ge(s_la, 1)
            with act.Fori(0, 2) as i:
                for q in range(2):
                    for j, groups in enumerate(TMU):
                        u = U_R + 4 * q + j
                        act.wait_ge(full, u + 1 + 8 * i)
                        for f, t in enumerate(groups):
                            mm = act.activation(RS[:, t, bass.ds(256 * q + 512 * i, 256)],
                                                PS[:, 2 * (u % 4) + f, 0:256], ACT.Silu, scale=RT[:, t:t + 1])
                        mm.then_inc(free, 1)
                    for n in range(2):
                        round_tile(act, T_R + 4 + 2 * q + n, i)
            gla_act(act)
            head_root(act, H - 1)
            for g in range(TT):
                u = U_OT + g
                act.wait_ge(full, u + 1)
                for e in range(2):
                    i_, oh, _ = ot_views(u, g, e)
                    mm = act.activation(oh, i_, ACT.Copy, scale=NW[:, V_ON + e:V_ON + e + 1])
                mm.then_inc(xh_done, 1)
            with act.Fori(0, 2) as i:
                for j in range(4):
                    act.wait_ge(full, U_WO + j + 1 + 4 * i)
                    round_tile(act, T_WO + 4 + j, i)
                    act.wait_ge(free, U_WO + j + 1 + 4 * i)
                    square_x(act, j, 1, 4 * i + j, i)
            for k in range(KT):
                round_x(act, k, V_FFN)

        def gla_pe(pe):
            pe.wait_ge(free, U_OT)
            pe.wait_ge(s_mask, NMASK)

            def scores(n):
                h, g = n // TT, GO[n % TT]
                s = h % 2
                if n % TT == 0:
                    pe.wait_ge(prep, 2 * h + 1)
                    pe.wait_ge(prepp, h + 1)
                if n % TT == 1:
                    pe.wait_ge(prepl, h + 1)
                    pe.wait_ge(preplp, h + 1)
                if n >= 2:
                    pe.wait_ge(kt_done, n - 1)
                pe.transpose(PS[:, 6 + n % 2, 0:128], kr(s)[:, 128 * g:128 * g + 128], ident[:, :])\
                    .then_inc(tr_full, 1)
                if n >= 2:
                    pe.wait_ge(att, n - 1)
                c = slice(128 * g, 128 * g + 128)
                mm = pe.matmul(PS[:, n % 2, 0:128], kd(s)[:, c], qd(s)[:, c], start=True, stop=True)
                if g < TT - 1:
                    for l in range(1, 4):
                        mm = pe.matmul(PS[:, n % 2, 128 * l:128 * l + 128], kl(s, l)[:, c], ql(s, l)[:, c],
                                       start=True, stop=True)
                mm.then_inc(sc_full, 1)

            def outputs(n):
                h, j = n // TT, n % TT
                g = GO[j]
                s = h % 2
                pe.wait_ge(att, n + 1)
                if n >= 2:
                    pe.wait_ge(og, n - 1)
                o = PS[:, 2 + n % 2, 0:DV]
                vv = V[:, g, DV * h:DV * h + DV]
                mm = pe.matmul(o, AT[:, n % 2, :], vv, start=True, stop=(j == 1))
                if j == 0:
                    pe.wait_ge(prep, 2 * h + 2)
                    pe.wait_ge(s_s0, 16 * (h + 1))
                    for q in range(NS):
                        mm = pe.matmul(o, QM[:, 128 * q:128 * q + 128], S0[:, q, :], start=False, stop=(q == NS - 1))
                elif j >= 2:
                    pe.wait_ge(st_done, 8 * h + 4 + j - 1)
                    mm = pe.matmul(o, QI[:, s, 128 * g:128 * g + 128], ST[:, :], start=False, stop=True)
                mm.then_inc(o_full, 1)
                pe.wait_ge(kt_done, n + 1)
                for x in range(4 if j == 0 else 1):
                    cnt = 8 * h + x if j == 0 else 8 * h + 4 + j - 1
                    if cnt >= 2:
                        pe.wait_ge(st_done, cnt - 1)
                    b = 4 + cnt % 2
                    if j:
                        mm = pe.matmul(PS[:, b, 0:DV], KTK[:, 2 * (n % 2), :], vv, start=True, stop=True)
                    else:
                        for e in range(2):
                            r = slice(32 * x, 32 * x + 32)
                            mm = pe.matmul(PS[:, b, DV * e:DV * e + DV], KTK[r, 2 * (n % 2) + e, :],
                                           V[r, g, DV * h:DV * h + DV], start=True, stop=True,
                                           tile_position=(32 * x, 0))
                    mm.then_inc(st_full, 1)

            scores(0)
            outputs(0)
            for n in range(1, STEPS + 1):
                if n < STEPS:
                    scores(n)
                if n > 1:
                    outputs(n - 1)

        def span(ap, l, odd):
            hf = BLK << (l - 1)
            return ap.rearrange("p (s two r) -> p s two r", two=2, r=hf)[:, :, odd, :]

        def gla_sums(v, h):
            if h:
                v.wait_ge(exps, h)
                v.wait_ge(argk, h)
                v.wait_ge(argp, h)
            v.tensor_tensor_scan(B16[:, :], M16[:, :], LA[:, h, :], 0.0, ALU.mult, ALU.add).then_inc(cum, 1)
            v.tensor_tensor_scan(B128[:, :], M128[:, :], LA[:, h, :], 0.0, ALU.mult, ALU.add).then_inc(cum, 1)

        def gla_levels(v, h):
            s = h % 2
            v.wait_ge(cum, 2 * h + 2)
            if h >= 2:
                v.wait_ge(sc_full, TT * (h - 1))
            for l in range(1, 4):
                hf = BLK << (l - 1)
                even, odd = span(B128[:, 0:SEQ], l, 0), span(B128[:, 0:SEQ], l, 1)
                mm = v.tensor_tensor(span(ql(s, l), l, 1), odd,
                                     even[:, :, hf - 1:hf].to_broadcast([128, SEQ // (2 * hf), hf]), ALU.subtract)
            mm.then_inc(argl, 1)

        def gla_operands(v, h):
            s = h % 2
            v.wait_ge(exps, h + 1)
            v.tensor_tensor(kd(s), kd(s), QK[:, h, :], ALU.mult)
            v.tensor_tensor(qd(s), qd(s), QK[:, H + h, :], ALU.mult).then_inc(prep, 1)

        def gla_queries(v, h):
            s = h % 2
            v.wait_ge(prep, 2 * h + 1)
            v.wait_ge(zset, 1)
            if h:
                v.wait_ge(o_full, TT * (h - 1) + 1)
            qs = qd(s)[:, SEQ:T].rearrange("p (s t) -> p s t", t=SL)
            n = NS - 1
            v.tensor_copy(QM[:, 0:n * (128 + SL)].rearrange("p (s c) -> p s c", s=n)[:, :, 0:SL], qs[:, 0:n, :])
            v.tensor_copy(QM[:, n * (128 + SL):n * (128 + SL) + SL], qs[:, n, :]).then_inc(prep, 1)

        def gla_level_operands(v, h):
            s = h % 2
            v.wait_ge(expl, h + 1)
            for l in range(1, 4):
                mm = v.tensor_tensor(span(ql(s, l), l, 1), span(ql(s, l), l, 1), span(QK[:, H + h, 0:SEQ], l, 1), ALU.mult)
            mm.then_inc(prepl, 1)

        def pool_kr(pool, h):
            s = h % 2
            pool.wait_ge(cum, 2 * h + 2)
            if h >= 2:
                pool.wait_ge(tr_full, TT * (h - 1))
            b = B128[:, 0:SEQ].rearrange("p (g t) -> p g t", t=128)
            pool.tensor_tensor(kr(s)[:, 0:SEQ].rearrange("p (g t) -> p g t", t=128),
                               b[:, :, 127:128].to_broadcast([128, TT - 1, 128]), b, ALU.subtract)
            bs = B16[:, SEQ:T].rearrange("p (s t) -> p s t", t=SL)
            pool.tensor_tensor(kr(s)[:, SEQ:T].rearrange("p (s t) -> p s t", t=SL),
                               bs[:, :, SL - 1:SL].to_broadcast([128, NS, SL]), bs, ALU.subtract).then_inc(argk, 1)

        def pool_operands(pool, h):
            s = h % 2
            pool.wait_ge(exps, h + 1)
            pool.tensor_tensor(kr(s), kr(s), QK[:, h, :], ALU.mult)
            pool.tensor_tensor(QI[:, s, :], QI[:, s, :], QK[:, H + h, 0:SEQ], ALU.mult).then_inc(prepp, 1)

        def pool_levels(pool, h):
            s = h % 2
            if h == 0:
                pool.wait_ge(full, U_OT)
            if h >= 2:
                pool.wait_ge(sc_full, TT * (h - 1))
            for l in range(1, 4):
                hf = BLK << (l - 1)
                even = span(B128[:, 0:SEQ], l, 0)
                mm = pool.tensor_tensor(span(kl(s, l), l, 0),
                                        even[:, :, hf - 1:hf].to_broadcast([128, SEQ // (2 * hf), hf]), even, ALU.subtract)
            mm.then_inc(argp, 1)
            if h < 2:
                for l in range(1, 4):
                    pool.memset(span(ql(s, l), l, 0), 0.0)
                    pool.memset(span(kl(s, l), l, 1), 0.0)

        def pool_level_operands(pool, h):
            s = h % 2
            pool.wait_ge(expl, h + 1)
            for l in range(1, 4):
                mm = pool.tensor_tensor(span(kl(s, l), l, 0), span(kl(s, l), l, 0), span(QK[:, h, 0:SEQ], l, 0), ALU.mult)
            mm.then_inc(preplp, 1)

        def gla_exps(act, h):
            s = h % 2
            c = 1.0 / GATE
            act.wait_ge(cum, 2 * h + 2)
            if h >= 2:
                act.wait_ge(st_done, 8 * (h - 1))
                act.wait_ge(o_full, TT * (h - 1))
            act.activation(kd(s), B16[:, :], ACT.Exp, scale=-c)
            act.activation(qd(s), B16[:, :], ACT.Exp, scale=c)
            act.activation(QI[:, s, :], B128[:, 0:SEQ], ACT.Exp, scale=c)
            act.activation(DEC[:, s, 0:4], B128[:, 127:SEQ:128], ACT.Exp, scale=c)
            act.activation(DEC[:, s, 4:12], B16[:, SEQ + SL - 1:T:SL], ACT.Exp, scale=c)
            act.wait_ge(argk, h + 1)
            act.activation(kr(s), kr(s), ACT.Exp, scale=c).then_inc(exps, 1)

        def gla_level_exps(act, h):
            s = h % 2
            c = 1.0 / GATE
            act.wait_ge(argl, h + 1)
            act.wait_ge(argp, h + 1)
            for l in range(1, 4):
                act.activation(span(ql(s, l), l, 1), span(ql(s, l), l, 1), ACT.Exp, scale=c)
                mm = act.activation(span(kl(s, l), l, 0), span(kl(s, l), l, 0), ACT.Exp, scale=c)
            mm.then_inc(expl, 1)

        def gla_dve(v):
            def mask(n):
                g = GO[n % TT]
                v.wait_ge(sc_full, n + 1)
                if n >= 2:
                    v.wait_ge(o_full, n - 1)
                if g == TT - 1:
                    v.tensor_tensor(AT[:, n % 2, :], PS[:, n % 2, 0:128], MASK[:, 0, :], ALU.mult).then_inc(att, 1)
                    return
                if n >= 1:
                    v.wait_ge(att, n)
                v.tensor_tensor(MPR[:, :], PS[:, n % 2, :], MASK[:, :, :].rearrange("p l q -> p (l q)"), ALU.mult)\
                    .then_inc(prod, 1)
                v.wait_ge(prod, 4 * (n // TT) + n % TT)
                v.tensor_reduce(AT[:, n % 2, :], MPR[:, :].rearrange("p (l q) -> p q l", l=4), AX.X, ALU.add)\
                    .then_inc(att, 1)

            def after(n):
                h, j = n // TT, n % TT
                g = GO[j]
                v.wait_ge(osq, n + 1)
                r = RS[:, g, DV * h:DV * h + DV]
                v.tensor_tensor(r, PS[:, 2 + n % 2, 0:DV], r, ALU.mult).then_inc(og, 1)
                for x in range(4 if j == 0 else 1):
                    cnt = 8 * h + x if j == 0 else 8 * h + 4 + j - 1
                    v.wait_ge(st_full, cnt + 1)
                    b = 4 + cnt % 2
                    if j == 0:
                        for e in range(2):
                            q = 2 * x + e
                            mm = v.scalar_tensor_tensor(out=S0[:, q, :], in0=S0[:, q, :],
                                                        scalar=DEC[:, h % 2, 4 + q:5 + q],
                                                        in1=PS[:, b, DV * e:DV * e + DV], op0=ALU.mult, op1=ALU.add)
                        mm.then_inc(st_done, 1)
                    elif j == 1:
                        if h:
                            v.wait_ge(s_pout, 16 * h)
                        v.tensor_copy(ST[:, :], PS[:, b, 0:DV]).then_inc(st_done, 1)
                    else:
                        v.wait_ge(st_done, cnt)
                        v.scalar_tensor_tensor(out=ST[:, :], in0=ST[:, :], scalar=DEC[:, h % 2, j - 1:j],
                                               in1=PS[:, b, 0:DV], op0=ALU.mult, op1=ALU.add).then_inc(st_done, 1)

            gla_levels(v, 0)
            mask(0)
            gla_level_operands(v, 0)
            gla_sums(v, 1)
            gla_levels(v, 1)
            after(0)
            for n in range(1, STEPS + 1):
                h = n // TT
                if n < STEPS:
                    mask(n)
                if n > 1:
                    after(n - 1)
                if n % TT == 0 and h + 1 < H:
                    gla_sums(v, h + 1)
                    gla_levels(v, h + 1)
                if n % TT == 2 and h + 1 < H:
                    gla_operands(v, h + 1)
                if n % TT == 3 and h + 1 < H:
                    gla_queries(v, h + 1)
                if n % TT == 2 and h:
                    head_inverse(v, h - 1)
                if n % TT == 4 and h + 1 < H:
                    gla_level_operands(v, h + 1)

        def gla_act(act):
            def keys(n):
                act.wait_ge(tr_full, n + 1)
                if n >= 2:
                    act.wait_ge(st_full, stc(n - 2))
                if GO[n % TT] == TT - 1:
                    act.activation(KTK[:, 2 * (n % 2), :], PS[:, 6 + n % 2, 0:128], ACT.Copy, scale=EO[:, 0:1])
                    act.activation(KTK[:, 2 * (n % 2) + 1, :], PS[:, 6 + n % 2, 0:128], ACT.Copy,
                                   scale=EO[:, 1:2]).then_inc(kt_done, 1)
                else:
                    act.activation(KTK[:, 2 * (n % 2), :], PS[:, 6 + n % 2, 0:128], ACT.Copy).then_inc(kt_done, 1)

            def out_squares(m):
                act.wait_ge(o_full, m + 1)
                if m:
                    act.wait_ge(osq, m)
                c = TT * (m // TT) + GO[m % TT]
                act.activation(JNK[:, :], PS[:, 2 + m % 2, 0:DV], ACT.Square, accum_out=SSH[:, c:c + 1])\
                    .then_inc(osq, 1)

            gla_level_exps(act, 0)
            keys(0)
            out_squares(0)
            for n in range(1, STEPS + 1):
                if n < STEPS:
                    keys(n)
                if n > 1:
                    out_squares(n - 1)
                if n % TT == 1 and n // TT + 1 < H:
                    gla_exps(act, n // TT + 1)
                    gla_level_exps(act, n // TT + 1)
                h = n // TT - 1
                if n % TT == 2 and h >= 0:
                    head_root(act, h)
                if n % TT == 3 and h >= 0:
                    act.wait_ge(rt_h, 2 * h + 2)
                    act.wait_ge(og, TT * (h + 1))
                    for g in range(TT):
                        mm = scale_head(act, h, g)
                    mm.then_inc(ogh, 1)

        def stc(n):
            return 8 * (n // TT) + 4 + n % TT

        block = ctx.enter_context(nc.Block())

        @block.sync
        def _(sp):
            front_sp(sp)
            ffn_sp(sp, 0)
            att_sp(sp)
            ffn_sp(sp, 1)
            final_sp(sp)

        @block.gpsimd
        def _(pool):
            front_pool(pool)
            ffn_pool(pool, 0)
            clear_sums(pool, 2)
            for k in range(KT):
                add_squares(pool, k, 2)
            att_pool(pool)
            clear_sums(pool, 3)
            with pool.Fori(0, 2) as i:
                for k in range(4):
                    add_squares(pool, k, 3, i)
            ffn_pool(pool, 1)
            clear_sums(pool, 4)
            for k in range(KT):
                add_squares(pool, k, 4)

        @block.scalar
        def _(act):
            front_act(act)
            ffn_act(act, 0, False, V_KV, 2)
            att_act(act)
            ffn_act(act, 1, True, None, 4)
            final_act(act)

        @block.vector
        def _(v):
            front_dve(v)
            ffn_dve(v, 0, False, V_KV, XF[0] + KT)
            att_dve(v)
            ffn_dve(v, 1, True, None, 0)
            final_dve(v)

        @block.tensor
        def _(pe):
            front_pe(pe)
            ffn_pe(pe, 0)
            att_pe(pe)
            ffn_pe(pe, 1)
            final_pe(pe)


INPUTS = ("x_prompt", "x_sample", "state_gla", "cache_k", "cache_v", "state_ffn_conv", "norm_mix", "norm_ffn",
          "norm_kv", "norm_final", "gla_w_in", "gla_w_g2", "gla_b_g2", "gla_g_onorm", "gla_w_out", "w_kv", "att_w_q",
          "att_sinks", "att_w_o", "ffn_w_up", "ffn_conv_w", "ffn_conv_b", "ffn_w_down")
OUTPUTS = (("y_p", (1, SEQ, D)), ("y_s", (NS, SL, D)), ("gla_p", (1, 1, H, DK, DV)), ("k_p", (1, WIN, KVH, HD)),
           ("v_p", (1, WIN, KVH, HD)), ("conv_p", (2, 1, 2, 2 * DFF)), ("gla_s", (1, NS, H, DK, DV)),
           ("k_s", (NS, WIN, KVH, HD)), ("v_s", (NS, WIN, KVH, HD)), ("conv_s", (2, NS, 2, 2 * DFF)))


def kernel(**inputs):
    import numpy as np
    import concourse.bacc as bacc
    from concourse.bass_utils import run_bass_kernel_spmd

    nc = bacc.Bacc("TRN2", target_bir_lowering=False, num_devices=1)
    arrays, A, O = {}, {}, {}
    for name in INPUTS:
        a = np.ascontiguousarray(inputs[name])
        arrays[f"in_{name}_dram"] = a
        A[name] = nc.dram_tensor(f"in_{name}_dram", a.shape, mybir.dt.from_np(a.dtype), kind="ExternalInput").ap()
    for i, (name, shape) in enumerate(OUTPUTS):
        O[name] = nc.dram_tensor(f"out_{i}_dram", shape, F32, kind="ExternalOutput").ap()
    build(nc, A, O)
    r = run_bass_kernel_spmd(nc, [arrays], core_ids=[0])
    return tuple(r.results[0][f"out_{i}_dram"] for i in range(len(OUTPUTS)))
```

```python
from contextlib import ExitStack

import concourse.bass as bass
from concourse import mybir

ALU = mybir.AluOpType
ACT = mybir.ActivationFunctionType
AX = mybir.AxisListType
F32 = mybir.dt.float32
F32R = mybir.dt.float32r
BF16 = mybir.dt.bfloat16

D = 1024
SEQ = 512
NS, SL = 8, 16
T = SEQ + NS * SL
KT = D // 128
TT = T // 128
HALF = T // 2
H, DK, DV, RANK = 4, 128, 256, 16
BLK = 16
GATE = 16.0
DFF = 2816
FT = DFF // 128
NIT = FT // 2
CW = SEQ + 2 + NS * (SL + 2)
CC = CW - 2
NH, HD, KVH, WIN, CH = 16, 64, 2, 128, 64
EPS = 1e-6


def build(nc, A, O):
    ctx = ExitStack()
    with ctx:
        top = [16512]

        def at(name, shape, dt, offset):
            return nc.alloc_sbuf_tensor_at(name, shape, dt, offset=offset)

        def size(shape, dt):
            n = 2 if dt == BF16 else 4
            for s in shape[1:]:
                n *= s
            return (n + 31) // 32 * 32

        def sb(name, shape, dt=F32):
            o = top[0]
            top[0] += size(shape, dt)
            return at(name, shape, dt, o)

        def area(n):
            o = top[0]
            top[0] += (n + 31) // 32 * 32
            return o

        def sem(name):
            return ctx.enter_context(nc.semaphore(name))

        x_area, xs_area = area(4 * KT * T), area(8 * KT * T)
        X = at("x_res", [128, KT, T], F32, x_area)
        XH = at("x_hi", [128, KT, T], F32R, xs_area)
        XL = at("x_lo", [128, KT, T], F32R, xs_area + 4 * KT * T)
        WRAW = sb("w_raw", [128, 2, KT, 256])
        DRAW_AREA = top[0]
        DRAW = sb("d_raw", [128, 2, D])
        WH = sb("w_hi", [128, 4, KT, 128], F32R)
        WL = sb("w_lo", [128, 4, KT, 128], F32R)
        d_area = area(4 * 4 * D)
        DH = at("d_hi", [128, 2, D], F32R, d_area)
        DL = at("d_lo", [128, 2, D], F32R, d_area + 8 * D)
        e_area = area(12 * KT * T)
        ident = sb("ident", [128, 128])
        ones = sb("ones", [128, 128])
        RB = sb("rstd_cols", [128, T])
        RT = sb("rstd_rows", [128, TT])
        SS = sb("sum_sq", [128, T])
        NVEC = 54
        NW = sb("vectors", [128, NVEC])
        CWT = sb("conv_taps", [128, 4, 2 * FT])
        k_area = top[0]
        KTK = sb("keys_rows", [128, 4, 128])
        m_area = area(2048)
        MPR = at("masked_scores", [128, 512], F32, m_area)
        AT = sb("scores", [128, 2, 128])
        ST = sb("gla_state", [128, DV])
        DEC = sb("decay", [128, 2, 12])
        JNK = sb("unused_out", [128, DV], BF16)
        SSH = sb("head_sq", [128, 20])
        RH = sb("head_rstd", [128, 20])
        EO = sb("even_odd", [128, 2])
        HB = sb("head_bands", [128, NH])
        SKB = sb("sinks_by_head", [128, NH])
        SKT = sb("sinks_banded", [128, NH])
        SKP = sb("sinks_pairs", [128, NH // 2])
        SKR = sb("sinks_rows", [128, KVH])
        NM = sb("neg_max", [128, 2, 2])
        SE = sb("sink_exp", [128, 2, 2])
        ES = sb("exp_sum", [128, 2, 2])
        SSF = sb("final_sums", [128, TT])
        TBL = sb("table_out", [128, 1])
        eps = sb("eps", [128, 2])
        EV = sb("bands", [128, 4])
        assert top[0] <= 229344, top[0]

        QK = at("kq_cols", [128, 2 * H, T], F32, e_area)
        V = at("v_rows", [128, TT, H * DV], F32, e_area + 4 * KT * T)
        RS = at("r_rows", [128, TT, H * DV], F32, e_area + 8 * KT * T)
        XIN = at("x_in", [128, TT, D], F32, e_area + 4 * KT * T)
        AB = at("gate_tail", [128, H, T], F32, e_area + 8 * KT * T)
        NRAW = at("vectors_raw", [NVEC, 128], F32, e_area)
        SQ = at("squares", [128, 2, T], F32, e_area + 12 * KT * T - 8 * T)
        GLS = at("gate_low", [128, T], F32, d_area)
        G2 = at("gate_up", [128, H * DK], F32, d_area + 4 * T)
        QI = at("q_inter", [128, 2, SEQ], F32, d_area)
        QM = at("q_by_seq", [128, NS * 128], F32, d_area + 4096)
        S0 = at("seq_states", [128, NS, DV], F32, d_area + 8192)
        LA = at("log_gate", [128, H, T], F32, x_area)
        M16 = at("carry16", [128, T], BF16, x_area + 4 * H * T)
        M128 = at("carry128", [128, T], BF16, x_area + 4 * H * T + 2 * T)
        B16 = at("cum16", [128, T], F32, x_area + 4 * H * T + 4 * T)
        B128 = at("cum128", [128, T], F32, x_area + 4 * H * T + 8 * T)
        MASK = at("score_mask", [128, 4, 128], F32, x_area + 4 * H * T + 12 * T)
        SET = [at("gla_operands0", [128, 3 * T], F32, DRAW_AREA),
               at("gla_operands1", [128, 3 * T], F32, xs_area + 8 * 6 * SEQ)]
        SETL = at("gla_level_operands", [128, 2, 6 * SEQ], F32, xs_area)

        def qd(s): return SET[s][:, 0:T]
        def kd(s): return SET[s][:, T:2 * T]
        def kr(s): return SET[s][:, 2 * T:3 * T]
        def ql(s, l): return SETL[:, s, (l - 1) * SEQ:l * SEQ]
        def kl(s, l): return SETL[:, s, (l + 2) * SEQ:(l + 3) * SEQ]

        fo = [e_area]

        def fb(name, shape, dt=F32):
            o = fo[0]
            fo[0] += size(shape, dt)
            assert fo[0] <= e_area + 12 * KT * T - 8 * T
            return at(name, shape, dt, o)

        UB = fb("up_rows", [128, 4, CW])
        CB = fb("conv_out", [128, 4, CC])
        Y = fb("gated", [128, 2, T])
        YH = fb("gated_hi", [128, 2, T], F32R)
        YL = fb("gated_lo", [128, 2, T], F32R)
        TLC = fb("tail_cols", [128, NIT, 4, 18])
        TLR = fb("tail_rows", [72, NIT, 128])
        STR = fb("conv_state", [64, NIT, 128])
        STC = fb("conv_state_cols", [128, NIT, 64])
        CRAW = fb("taps_raw", [2 * FT, 4, 128])

        KCR = at("cache_k_rows", [128, NS, KVH, 2, HD], F32, e_area)
        P = at("probs", [128, 2, 512], F32, e_area)
        PT = at("probs_cols", [128, 2, 512], F32, e_area + 4096)
        KTD = at("keys_cols", [128, KVH, SEQ], F32, e_area + 8192)
        VZ = at("v_0_v", [128, TT - 1, KVH, 3 * HD], F32, e_area + 12288)
        QZ = at("q_0_q", [128, NS, KVH, 2, 4, SL], F32, e_area + 18432)
        KCT = at("seq_keys_cols", [128, KVH, NS, WIN + SL], F32, e_area + 26624)
        QF = at("q_cols", [128, KT // 2, T // CH, 2, CH], F32, e_area + 35840)
        KD = at("keys_twice", [128, TT, KVH, 2, HD], F32, d_area)
        V4 = at("v_new_rows", [128, KVH, 2, HD], F32, d_area + 5120)
        VN = at("v_new", [SL, NS, KVH, 2, HD], F32, d_area + 6144)
        VCD = at("cache_v", [128, NS, KVH, 2, HD], F32, DRAW_AREA)
        VS = at("v_0_v_shifted", [128, TT - 1, KVH, 3 * HD], F32, k_area)
        NFB = at("norm_final_rows", [128, D], F32, xs_area + 4 * KT * T)
        FSQ = at("final_squares", [128, D], F32, e_area + 12 * KT * T - 8 * T)
        YO = at("y_rows", [128, TT, D], F32, xs_area)

        PS = ctx.enter_context(nc.psum_tensor("ps", [128, 8, 512], F32))
        XSP = nc.dram_tensor("x_spill", [128, KT, T], F32, kind="Internal").ap()

        s_const = sem("s_const")
        s_xin = sem("s_xin")
        s_raw = [sem("s_raw0"), sem("s_raw1")]
        s_draw = sem("s_draw")
        s_setup = sem("s_setup")
        full = sem("full")
        free = sem("free")
        hi_done = sem("hi_done")
        lo_done = sem("lo_done")
        dhi = sem("dhi")
        dlo = sem("dlo")
        xh_done = sem("xh_done")
        xl_done = sem("xl_done")
        sq_done = sem("sq_done")
        ss_done = sem("ss_done")
        rt_sq = sem("rt_sq")
        rstd = sem("rstd")
        s_spill = sem("s_spill")
        s_g2 = sem("s_g2")
        s_mask = sem("s_mask")
        rt_h = sem("rt_h")
        cum = sem("cum")
        prod = sem("prod")
        s_xback = sem("s_xback")
        dve = sem("dve")
        s_mn = sem("s_mn")
        s_la = sem("s_la")
        argk = sem("argk")
        argl = sem("argl")
        argp = sem("argp")
        exps = sem("exps")
        expl = sem("expl")
        prep = sem("prep")
        prepp = sem("prepp")
        prepl = sem("prepl")
        preplp = sem("preplp")
        zset = sem("zset")
        tr_full = sem("tr_full")
        kt_done = sem("kt_done")
        sc_full = sem("sc_full")
        att = sem("att")
        o_full = sem("o_full")
        osq = sem("osq")
        og = sem("og")
        st_full = sem("st_full")
        st_done = sem("st_done")
        s_s0 = sem("s_s0")
        s_sout = sem("s_sout")
        s_pout = sem("s_pout")
        ogh = sem("ogh")
        ot_part = sem("ot_part")
        oth = sem("oth")
        ogn = sem("ogn")
        t0_done = sem("t0_done")
        conv = sem("conv")
        silu = sem("silu")
        y_done = sem("y_done")
        yh = sem("yh")
        yl = sem("yl")
        st_c = sem("st_c")
        tl_g = sem("tl_g")
        s_str = sem("s_str")
        s_tout = sem("s_tout")
        ysq = sem("ysq")
        s_stat = sem("s_stat")
        s_table = sem("s_table")
        s_out = sem("s_out")
        s_sink = sem("s_sink")
        s_cache = sem("s_cache")
        s_vs = sem("s_vs")
        s_vn = sem("s_vn")
        s_nfb = sem("s_nfb")
        s_y = sem("s_y")
        azero = sem("azero")
        sink_v = sem("sink_v")
        qz = sem("qz")
        a_sc = sem("a_sc")
        a_chain = sem("a_chain")
        a_sum = sem("a_sum")
        a_nm = sem("a_nm")
        a_ex = sem("a_ex")
        a_p = sem("a_p")
        a_tr = sem("a_tr")
        a_pt = sem("a_pt")
        a_o = sem("a_o")
        a_oh = sem("a_oh")
        a_ol = sem("a_ol")

        T_GL, T_KQ, T_V, T_R, T_WO = 0, 2, 10, 18, 26
        T_F = [34, 96]
        T_KV, T_AQ, T_AO = 78, 80, 88
        w_in = A["gla_w_in"][0]
        pieces = [(w_in, 2 * H * DK + 2 * H * DV + RANK - 128)]
        pieces += [(w_in, H * DK + 256 * n) for n in range(2)] + [(w_in, 256 * n) for n in range(2)]
        pieces += [(w_in, 2 * H * DK + 256 * n) for n in range(8)]
        pieces += [(A["gla_w_out"][0], 256 * n) for n in range(4)]
        later = {T_KV // 2: (A["w_kv"], 0)}
        later.update({T_AQ // 2 + n: (A["att_w_q"][0], 256 * n) for n in range(4)})
        later.update({T_AO // 2 + n: (A["att_w_o"][0], 256 * n) for n in range(4)})
        U_C, U_X, U_GL, U_KQ, U_Z, U_V, U_R = 0, 1, 9, 12, 20, 24, 40
        U_OT, U_WO = 56, 61
        FFN_UNITS = 6 + 12 * (NIT - 1) + 2 + KT
        U_KV = 69 + FFN_UNITS
        U_Q, U_KT, U_KC = U_KV + 4, U_KV + 8, U_KV + 10
        U_AO = U_KC + 6
        U_F = [69, U_AO + KT]
        U_Y = U_F[1] + FFN_UNITS
        XF = [KT, 4 * KT]
        XLF = [KT, 4 * KT]
        NORM_F = [1, 3]
        RC = [0, 2, 3, 5, 6]
        STATS_READ = [0, U_GL + 3, U_F[0] + 3, U_Q + 1]
        GO = [TT - 1] + list(range(TT - 1))
        STEPS = H * TT
        TMU = [[0], [1], [2, 3], [4]]
        NATT = (TT - 1) * KT + NS
        V_MIX, V_FFN, V_KV, V_FIN, V_ON, V_BG = 0, 16, 32, 40, 48, 50

        def unit(u, n=HALF):
            return PS[:, 2 * (u % 4):2 * (u % 4) + 2, 0:n]

        def halves(ap):
            return ap.rearrange("p (a b) -> p a b", a=2)

        def f32(ap):
            return ap.bitcast(F32)

        def round_tile(act, n0, i=0, inc=1):
            p0 = n0 // 2
            act.wait_ge(s_raw[p0 % 2], 16 * (p0 // 2 + 1) + 16 * i)
            half = (n0 % 2) * 128
            act.activation(WH[:, n0 % 4, :, :], WRAW[:, p0 % 2, :, half:half + 128],
                           ACT.Copy).then_inc(hi_done, inc)

        def rest_tile(v, n0, i=0, inc=1):
            p0 = n0 // 2
            half = (n0 % 2) * 128
            v.wait_ge(hi_done, n0 + 1 + 4 * i)
            v.tensor_tensor(WL[:, n0 % 4, :, :], WRAW[:, p0 % 2, :, half:half + 128],
                            f32(WH[:, n0 % 4, :, :]), ALU.subtract).then_inc(lo_done, inc)

        def fm_tile(pe, n0, u0, i=0, wstep=4, ustep=4, fresh=None):
            pe.wait_ge(lo_done, n0 + 1 + wstep * i)
            if u0 >= 4:
                pe.wait_ge(free, u0 - 3 + ustep * i)
            for k in range(KT):
                if fresh is not None:
                    pe.wait_ge(xl_done, fresh + k + 1)
                for a, (w, x) in enumerate(((WH, XH), (WH, XL), (WL, XH))):
                    for f in range(2):
                        mm = pe.matmul(PS[:, 2 * (u0 % 4) + f, 0:HALF], w[:, n0 % 4, k, :],
                                       x[:, k, f * HALF:(f + 1) * HALF],
                                       start=(k == 0 and a == 0), stop=(k == KT - 1 and a == 2))
            mm.then_inc(full, 1)

        def fm_half(pe, n0, u0, f):
            for k in range(KT):
                for a, (w, x) in enumerate(((WH, XH), (WH, XL), (WL, XH))):
                    mm = pe.matmul(PS[:, 2 * (u0 % 4) + f, 0:HALF], w[:, n0 % 4, k, :],
                                   x[:, k, f * HALF:(f + 1) * HALF],
                                   start=(k == 0 and a == 0), stop=(k == KT - 1 and a == 2))
            return mm

        def tm_unit(pe, n0, u0, groups, i=0, fresh=None):
            pe.wait_ge(lo_done, n0 + 2 + 4 * i)
            pe.wait_ge(free, u0 - 3 + 8 * i)
            for f, t in enumerate(groups):
                for k in range(KT):
                    if fresh is not None:
                        pe.wait_ge(xl_done, fresh + k + 1)
                    for a, (x, w) in enumerate(((XH, WH), (XH, WL), (XL, WH))):
                        mm = pe.matmul(PS[:, 2 * (u0 % 4) + f, 0:256], x[:, k, 128 * t:128 * t + 128],
                                       w[:, n0 % 4:n0 % 4 + 2, k, :],
                                       start=(k == 0 and a == 0), stop=(k == KT - 1 and a == 2))
            mm.then_inc(full, 1)

        def stat_cols(pe, u, norm):
            pe.wait_ge(ss_done, (KT + 1) * (norm + 1))
            pe.wait_ge(free, u - 3)
            for f in range(2):
                mm = pe.matmul(PS[:, 2 * (u % 4) + f, 0:HALF], ones[:, :], SS[:, f * HALF:(f + 1) * HALF],
                               start=True, stop=True)
            mm.then_inc(full, 1)

        def stat_rows(pe, u):
            pe.wait_ge(free, u - 3)
            for t in range(TT):
                mm = pe.matmul(PS[:, 2 * (u % 4), t:t + 1], SS[:, 128 * t:128 * t + 128], ones[:, 0:1],
                               start=True, stop=True)
            mm.then_inc(full, 1)

        tables = [0]

        def load_table(act, f):
            if tables[0]:
                act.wait_ge(s_table, tables[0])
            act.activation(TBL[:, :], eps[:, 0:1], f).then_inc(s_table, 1)
            tables[0] += 1

        def root_cols(act, u):
            act.wait_ge(full, u + 1)
            act.activation(halves(RB[:, :]), unit(u), ACT.Sqrt, bias=eps[:, 0:1], scale=1.0 / D).then_inc(rt_sq, 1)

        def root_rows(act, u):
            act.wait_ge(full, u + 1)
            act.activation(RT[:, :], PS[:, 2 * (u % 4), 0:TT], ACT.Sqrt, bias=eps[:, 0:1],
                           scale=1.0 / D).then_inc(rt_sq, 1)

        def roots(act, u, rows):
            load_table(act, ACT.Sqrt)
            root_cols(act, u)
            if rows:
                root_rows(act, u + 1)


        def invert(v, count, rows):
            v.wait_ge(rt_sq, count + 1)
            v.reciprocal(RB[:, :], RB[:, :]).then_inc(rstd, 1)
            if rows:
                v.wait_ge(rt_sq, count + 2)
                v.reciprocal(RT[:, :], RT[:, :]).then_inc(rstd, 1)

        def round_x(act, k, vec):
            act.activation(XH[:, k, :], X[:, k, :], ACT.Copy, scale=NW[:, vec + k:vec + k + 1]).then_inc(xh_done, 1)

        def rest_x(v, k, vec, base):
            v.wait_ge(xh_done, base + k + 1)
            v.scalar_tensor_tensor(out=XL[:, k, :], in0=X[:, k, :], scalar=NW[:, vec + k:vec + k + 1],
                                   in1=f32(XH[:, k, :]), op0=ALU.mult, op1=ALU.subtract).then_inc(xl_done, 1)

        def square_x(act, k, norm, k2=None, i=0):
            n = KT * norm + k
            if n >= 2:
                act.wait_ge(ss_done, (KT + 1) * norm + k + 4 * i)
            x = X[:, k, :] if k2 is None else X[:, bass.ds(k2, 1), :].rearrange("p a t -> p (a t)")
            act.activation(SQ[:, k % 2, :], x, ACT.Square).then_inc(sq_done, 1)

        def add_and_resplit(v, n0, u0, vec, base):
            for j in range(KT):
                add_x(v, j, u0 + j)
                if j < KT - 1:
                    rest_tile(v, n0 + 4 + j)
            for k in range(KT):
                if k == 2:
                    rest_tile(v, n0 + 4 + KT - 1)
                rest_x(v, k, vec, base)

        def square_and_resplit(act, n0, u0, norm, vec):
            for j in range(KT - 1):
                act.wait_ge(full, u0 + j + 1)
                round_tile(act, n0 + 4 + j)
                act.wait_ge(free, u0 + j + 1)
                square_x(act, j, norm)
            act.wait_ge(full, u0 + KT)
            for k in range(KT):
                if k == 2:
                    round_tile(act, n0 + 4 + KT - 1)
                if k == 4:
                    act.wait_ge(free, u0 + KT)
                    square_x(act, KT - 1, norm)
                if k == KT - 1:
                    act.wait_ge(free, u0 + KT)
                round_x(act, k, vec)

        def clear_sums(pool, norm):
            if norm:
                pool.wait_ge(full, STATS_READ[norm])
            pool.memset(SS[:, :], 0.0).then_inc(ss_done, 1)

        def add_squares(pool, k, norm, i=0):
            n = (KT + 1) * norm + k
            pool.wait_ge(sq_done, KT * norm + k + 1 + 4 * i)
            pool.wait_ge(ss_done, n + 1 + 4 * i)
            pool.tensor_tensor(SS[:, :], SS[:, :], SQ[:, k % 2, :], ALU.add).then_inc(ss_done, 1)

        def add_x(v, m, u0, i=0, ustep=12, inc=1):
            v.wait_ge(full, u0 + 1 + ustep * i)
            v.tensor_tensor(halves(X[:, m, :]), halves(X[:, m, :]), unit(u0), ALU.add).then_inc(free, inc)

        def fu(i0):
            return 0 if i0 == 0 else 6 + 12 * (i0 - 1)

        def fpos(first, last=False):
            if last:
                return [0, 1], list(range(4, 12)), [2, 3]
            return ([1, 3], None, [4, 5]) if first else ([0, 1], list(range(2, 10)), [10, 11])

        TAILS = (range(6), range(6, NIT))

        def ffn_pe(pe, L):
            t0, u0 = T_F[L], U_F[L]

            def up(js, us, base, i0, i, first):
                for j, u in zip(js, us):
                    fm_tile(pe, t0 + 4 * i0 + j, u0 + base + u, i, 4, 12, fresh=XLF[L] if first and j == 0 else None)
                    if first and j == 0:
                        stat_cols(pe, u0 + 2, NORM_F[L])

            def down(base, us, i0, i):
                for m, u in enumerate(us):
                    w = u0 + base + u
                    if m == 0:
                        pe.wait_ge(yl, 2 * (NIT * L + i0) + 2 + 2 * i)
                    pe.wait_ge(dlo, 4 * (NIT * L + i0) + m // 2 + 1 + 4 * i)
                    pe.wait_ge(free, w - 3 + 12 * i)
                    for k in range(2):
                        for a, (wt, y) in enumerate(((DH, YH), (DH, YL), (DL, YH))):
                            for f in range(2):
                                mm = pe.matmul(PS[:, 2 * (w % 4) + f, 0:HALF], wt[:, k, 128 * m:128 * m + 128],
                                               y[:, k, f * HALF:(f + 1) * HALF],
                                               start=(k == 0 and a == 0), stop=(k == 1 and a == 2))
                    mm.then_inc(full, 1)

            def last_down(base):
                n = NIT * (L + 1)
                for ms, k in ((range(4), 0), (range(4), 1), (range(4, 8), None)):
                    for m in ms:
                        w = u0 + base + m
                        pe.wait_ge(yl, 2 * n - (1 if k == 0 else 0))
                        if k != 1:
                            pe.wait_ge(dlo, 4 * (n - 1) + m // 2 + 1)
                            pe.wait_ge(free, w - 3)
                        for kk in ([k] if k is not None else [0, 1]):
                            for a, (wt, y) in enumerate(((DH, YH), (DH, YL), (DL, YH))):
                                for f in range(2):
                                    mm = pe.matmul(PS[:, 2 * (w % 4) + f, 0:HALF], wt[:, kk, 128 * m:128 * m + 128],
                                                   y[:, kk, f * HALF:(f + 1) * HALF],
                                                   start=(kk == 0 and a == 0), stop=(kk == 1 and a == 2))
                        if k != 0:
                            mm.then_inc(full, 1)

            def step(i0, i, first=False):
                final = i0 == NIT - 1
                gu, du, vu = fpos(first, final)
                b = fu(i0)
                up([0, 1], gu, b, i0, i, first)
                if final:
                    up([2, 3], vu, b, i0, i, first)
                if du:
                    down(b, du, i0 - 1, i)
                if not final:
                    up([2, 3], vu, b, i0, i, first)

            pe.wait_ge(s_str, 96 * (L + 1))
            pe.wait_ge(free, u0 - 3)
            for n in range(NIT):
                b = 2 * (u0 % 4) + n // 8
                pe.transpose(PS[:, b, 64 * (n % 8):64 * (n % 8) + 64], STR[:, n, :], ident[0:64, 0:64])
            for c in range(4):
                o = 64 * (NIT - 8) + 2 * FT * c
                mm = pe.transpose(PS[:, b, o:o + 2 * FT], CRAW[:, c, :], ident[0:2 * FT, 0:2 * FT])
            mm.then_inc(full, 1)
            step(0, 0, True)
            with pe.Fori(0, NIT - 2) as i:
                step(1, i)
            step(NIT - 1, 0)
            last_down(fu(NIT - 1) + 12)
            pe.wait_ge(tl_g, 2 * NIT * (L + 1))
            for q, ns in enumerate(TAILS):
                u = u0 + FFN_UNITS - 2 + q
                pe.wait_ge(free, u - 3)
                for j, n in enumerate(ns):
                    mm = pe.transpose(PS[0:72, 2 * (u % 4) + j // 4, 128 * (j % 4):128 * (j % 4) + 128],
                                      TLC[:, n, :, :].rearrange("p a b -> p (a b)"), ident[:, :])
                mm.then_inc(full, 1)

        def ffn_dve(v, L, last, nextvec, nextx):
            t0, u0 = T_F[L], U_F[L]

            def evac(j, u, i, i0, first):
                w = u0 + u
                if first and j == 0:
                    invert(v, RC[NORM_F[L]], False)
                    v.wait_ge(rstd, RC[NORM_F[L]] + 1)
                    inc = 2
                else:
                    inc = 1
                v.wait_ge(full, w + 1 + 12 * i)
                if j == 0 and not first:
                    v.wait_ge(tl_g, 2 * (NIT * L + i0) + 2 * i)
                if j == 0:
                    v.tensor_copy(UB[:, :, SEQ + 2:CW].rearrange("p a (s c) -> p a s c", s=NS)[:, :, :, 0:2],
                                  STC[:, bass.ds(i0 + i, 1), :].rearrange("p o (a s r) -> p (o a) s r", a=4, s=NS))
                b = 2 * (w % 4)
                nb = SEQ - HALF
                v.tensor_tensor(UB[:, j, 2:2 + HALF], PS[:, b, 0:HALF], RB[:, 0:HALF], ALU.mult)
                v.tensor_tensor(UB[:, j, 2 + HALF:2 + SEQ], PS[:, b + 1, 0:nb], RB[:, HALF:SEQ], ALU.mult)
                v.tensor_tensor(UB[:, j, SEQ + 2:CW].rearrange("p (s c) -> p s c", s=NS)[:, :, 2:2 + SL],
                                PS[:, b + 1, nb:HALF].rearrange("p (s c) -> p s c", s=NS),
                                RB[:, SEQ:T].rearrange("p (s c) -> p s c", s=NS), ALU.mult).then_inc(free, inc)

            def tile_col(j, i0, i):
                return (FT if j >= 2 else 0) + j % 2 + 2 * i0 + 2 * i

            def conv_taps(j, i0, i):
                c = tile_col(j, i0, i)
                n = 4 * (NIT * L + i0) + j
                v.wait_ge(t0_done, n + 1 + 4 * i)
                v.scalar_tensor_tensor(out=CB[:, j, :], in0=UB[:, j, 1:1 + CC], scalar=CWT[:, 1, bass.ds(c, 1)],
                                       in1=CB[:, j, :], op0=ALU.mult, op1=ALU.add).then_inc(conv, 1)
                v.wait_ge(conv, 2 * n + 1 + 8 * i)
                v.scalar_tensor_tensor(out=CB[:, j, :], in0=UB[:, j, 2:2 + CC], scalar=CWT[:, 2, bass.ds(c, 1)],
                                       in1=CB[:, j, :], op0=ALU.mult, op1=ALU.add).then_inc(conv, 1)

            def gate(j, i0, i):
                n = 2 * (NIT * L + i0) + j
                v.wait_ge(silu, n + 1 + 2 * i)
                v.wait_ge(conv, 8 * (NIT * L + i0) + 2 * (j + 2) + 2 + 8 * i)
                v.tensor_tensor(Y[:, j, 0:SEQ], CB[:, j, 0:SEQ], CB[:, 2 + j, 0:SEQ], ALU.mult)
                a = CB[:, j, SEQ:CC].rearrange("p (s c) -> p s c", s=NS)[:, :, 2:2 + SL]
                b = CB[:, 2 + j, SEQ:CC].rearrange("p (s c) -> p s c", s=NS)[:, :, 2:2 + SL]
                v.tensor_tensor(Y[:, j, SEQ:T].rearrange("p (s c) -> p s c", s=NS), a, b, ALU.mult).then_inc(y_done, 1)

            def rest_y(j, i0, i):
                n = 2 * (NIT * L + i0) + j
                v.wait_ge(yh, n + 1 + 2 * i)
                v.tensor_tensor(YL[:, j, :], Y[:, j, :], f32(YH[:, j, :]), ALU.subtract).then_inc(yl, 1)

            def rest_down(c, i0, i):
                v.wait_ge(dhi, 4 * (NIT * L + i0) + c + 1 + 4 * i)
                v.tensor_tensor(DL[:, :, 256 * c:256 * c + 256], DRAW[:, :, 256 * c:256 * c + 256],
                                f32(DH[:, :, 256 * c:256 * c + 256]), ALU.subtract).then_inc(dlo, 1)

            def gate_tiles(i0, i, first, ahead):
                b = fu(i0)
                for j, u in zip((0, 1), fpos(first)[0]):
                    evac(j, b + u, i, i0, first)
                    if ahead:
                        rest_tile(v, t0 + 4 * i0 + j + 4, i)
                    conv_taps(j, i0, i)

            def value_tiles(i0, i, vu, ahead, split):
                b = fu(i0)
                for j, u in zip((2, 3), vu):
                    if j == 3 and split:
                        rest_y(0, i0, i)
                    evac(j, b + u, i, i0, False)
                    if ahead:
                        rest_tile(v, t0 + 4 * i0 + j + 4, i)
                    conv_taps(j, i0, i)
                    gate(j - 2, i0, i)
                if split:
                    rest_y(1, i0, i)

            def add_down(i0, i, du):
                for m, u in enumerate(du):
                    add_x(v, m, u0 + fu(i0) + u, i)
                    if m == 7 and i0 == NIT - 1:
                        rest_y(0, i0, i)
                    if m % 2:
                        rest_down(m // 2, i0, i)

            def step(i0, i):
                _, du, vu = fpos(False)
                gate_tiles(i0, i, False, True)
                add_down(i0, i, du)
                value_tiles(i0, i, vu, True, True)

            def first_step():
                gate_tiles(0, 0, True, True)
                for c in range(4):
                    rest_down(c, 0, 0)
                value_tiles(0, 0, fpos(True)[2], True, True)

            def last_step():
                _, du, vu = fpos(False, True)
                gate_tiles(NIT - 1, 0, False, not last)
                value_tiles(NIT - 1, 0, vu, not last, False)
                add_down(NIT - 1, 0, du)
                rest_y(1, NIT - 1, 0)

            v.memset(UB[:, :, 0:2], 0.0)
            v.wait_ge(full, u0 + 1)
            b = 2 * (u0 % 4)
            v.tensor_copy(STC[:, 0:8, :].rearrange("p n c -> p (n c)"), PS[:, b, :])
            v.tensor_copy(STC[:, 8:NIT, :].rearrange("p n c -> p (n c)"), PS[:, b + 1, 0:64 * (NIT - 8)]).then_inc(st_c, 1)
            v.tensor_copy(CWT[:, :, :].rearrange("p c t -> p (c t)"),
                          PS[:, b + 1, 64 * (NIT - 8):64 * (NIT - 8) + 8 * FT]).then_inc(free, 1)
            v.wait_ge(st_c, L + 1)
            first_step()
            with v.Fori(0, NIT - 2) as i:
                step(1, i)
            last_step()
            b = fu(NIT - 1) + 12
            for m in range(8):
                if m == 7 and nextvec is not None:
                    rest_x(v, 6, nextvec, nextx)
                add_x(v, m, u0 + b + m)
                if 0 < m < 7 and nextvec is not None:
                    rest_x(v, m - 1, nextvec, nextx)
            if nextvec is not None:
                rest_x(v, 7, nextvec, nextx)
            for q, ns in enumerate(TAILS):
                u = u0 + FFN_UNITS - 2 + q
                v.wait_ge(full, u + 1)
                o = TLR[:, ns[0]:ns[-1] + 1, :].rearrange("p n c -> p (n c)")
                v.tensor_copy(o[:, 0:512], PS[0:72, 2 * (u % 4), :])
                v.tensor_copy(o[:, 512:128 * len(ns)], PS[0:72, 2 * (u % 4) + 1, 0:128 * len(ns) - 512]).then_inc(free, 1)

        def ffn_act(act, L, last, nextvec, nextnorm):
            t0, u0 = T_F[L], U_F[L]

            def tap0(j, i0, i, w):
                c = (FT if j >= 2 else 0) + j % 2 + 2 * i0 + 2 * i
                act.wait_ge(free, w + 1 + 12 * i)
                act.activation(CB[:, j, :], UB[:, j, 0:CC], ACT.Identity, scale=CWT[:, 0, bass.ds(c, 1)],
                               bias=CWT[:, 3, bass.ds(c, 1)]).then_inc(t0_done, 1)

            def do_silu(j, i0, i):
                act.wait_ge(conv, 8 * (NIT * L + i0) + 2 * j + 2 + 8 * i)
                act.activation(CB[:, j, :], CB[:, j, :], ACT.Silu).then_inc(silu, 1)

            def round_y(j, i0, i):
                act.wait_ge(y_done, 2 * (NIT * L + i0) + j + 1 + 2 * i)
                act.activation(YH[:, j, :], Y[:, j, :], ACT.Copy).then_inc(yh, 1)

            def round_down(c, i0, i):
                act.activation(DH[:, :, 256 * c:256 * c + 256], DRAW[:, :, 256 * c:256 * c + 256],
                               ACT.Copy).then_inc(dhi, 1)

            def step(i0, i, first=False, ahead=True):
                final = i0 == NIT - 1
                gu, du, vu = fpos(first, final)
                b = fu(i0)
                n = NIT * L + i0

                def tile_ahead(j, w):
                    if ahead:
                        act.wait_ge(full, w + 1 + 12 * i)
                        round_tile(act, t0 + 4 * i0 + j + 4, i)

                def values():
                    for j, u in zip((2, 3), vu):
                        if j == 3 and not final:
                            round_y(0, i0, i)
                        tile_ahead(j, u0 + b + u)
                        tap0(j, i0, i, u0 + b + u)

                for j, u in zip((0, 1), gu):
                    w = u0 + b + u
                    if first and j == 0:
                        roots(act, u0 + 2, False)
                    tile_ahead(j, w)
                    if j == 1:
                        do_silu(0, i0, i)
                    tap0(j, i0, i, w)
                do_silu(1, i0, i)
                if final:
                    values()
                for c in range(4):
                    if c == 0:
                        act.wait_ge(s_draw, 16 * (n + 1) + 16 * i)
                    if du:
                        act.wait_ge(full, u0 + b + du[2 * c + 1] + 1 + 12 * i)
                    if final and c == 3:
                        round_y(0, i0, i)
                    round_down(c, i0, i)
                if not final:
                    values()
                round_y(1, i0, i)

            step(0, 0, True)
            with act.Fori(0, NIT - 2) as i:
                step(1, i)
            step(NIT - 1, 0, ahead=not last)
            b = fu(NIT - 1) + 12
            for m in range(8 if nextnorm is not None else 0):
                act.wait_ge(free, u0 + b + m + 1)
                round_x(act, m, nextvec)
                square_x(act, m, nextnorm)

        def ffn_pool(pool, L):
            u0 = U_F[L]

            def gather(jj, w, i0, i):
                pool.wait_ge(free, w + 1 + 12 * i)
                a = slice(2 * jj, 2 * jj + 2)
                to = TLC[:, bass.ds(i0 + i, 1), a, :].rearrange("p o a c -> p (o a) c")
                pool.tensor_tensor(to[:, :, 0:2], UB[:, a, SEQ:SEQ + 2],
                                   ones[:, 0:4].rearrange("p (a r) -> p a r", a=2), ALU.mult)
                pool.tensor_tensor(to[:, :, 2:18].rearrange("p a (s r) -> p a s r", s=NS),
                                   UB[:, a, SEQ + 2:CW].rearrange("p a (s c) -> p a s c", s=NS)[:, :, :, SL:SL + 2],
                                   ones[:, 0:4 * NS].rearrange("p (a s r) -> p a s r", a=2, s=NS), ALU.mult)\
                    .then_inc(tl_g, 1)

            def step(i0, i, first=False):
                gu, du, vu = fpos(first)
                b = fu(i0)
                gather(0, u0 + b + gu[1], i0, i)
                gather(1, u0 + b + vu[1], i0, i)

            step(0, 0, True)
            with pool.Fori(0, NIT - 2) as i:
                step(1, i)
            step(NIT - 1, 0)

        def conv_loads(sp, L):
            for j in range(4):
                src = A["state_ffn_conv"][L].rearrange("s r (h n two c) -> (s r) h n two c", h=2, two=2, c=128)
                sp.dma_start(STR[16 * j:16 * j + 16, :, :], src[:, j // 2, :, j % 2, :]).then_inc(s_str, 16)
            sp.dma_start(CRAW[:, 0:3, :], A["ffn_conv_w"][L].rearrange("c (t p) -> t c p", p=128)).then_inc(s_str, 16)
            sp.dma_start(CRAW[:, 3, :], A["ffn_conv_b"][L].rearrange("(t p) -> t p", p=128)).then_inc(s_str, 16)

        def tail_stores(sp, L):
            sp.wait_ge(free, U_F[L] + FFN_UNITS)
            for j in range(4):
                tail_store(sp, L, j)

        def tail_store(sp, L, j):
            for o, r in ((O["conv_p"][L, 0], slice(18 * j, 18 * j + 2)),
                         (O["conv_s"][L].rearrange("s r c -> (s r) c"), slice(18 * j + 2, 18 * j + 18))):
                sp.dma_start(o.rearrange("r (h n two c) -> r h n two c", h=2, two=2, c=128)[:, j // 2, :, j % 2, :],
                             TLR[r, :, :]).then_inc(s_tout, 16)

        def ffn_sp(sp, L):
            t0 = T_F[L]

            def step(i0, i):
                for q in range(2):
                    p0 = t0 // 2 + 2 * i0 + q
                    sp.wait_ge(lo_done, 2 * p0 - 2 + 4 * i)
                    src = A["ffn_w_up"][L].rearrange("(k p) n -> p k n", p=128)
                    sp.dma_start(WRAW[:, p0 % 2, :, :], src[:, :, bass.ds(q * DFF + 256 * i0 + 256 * i, 256)])\
                        .then_inc(s_raw[p0 % 2], 16)
                n = NIT * L + i0
                if n:
                    sp.wait_ge(dlo, 4 * n + 4 * i)
                sp.dma_start(DRAW[:, :, :], A["ffn_w_down"][L].rearrange("(t p) n -> p t n", p=128)
                             [:, bass.ds(2 * i0 + 2 * i, 2), :]).then_inc(s_draw, 16)
            step(0, 0)
            with sp.Fori(0, NIT - 1) as i:
                step(1, i)

        def later_piece(sp, p):
            w, c = later[p]
            sp.wait_ge(lo_done, 2 * p - 2)
            sp.dma_start(WRAW[:, p % 2, :, :], w.rearrange("(k p) n -> p k n", p=128)[:, :, c:c + 256])\
                .then_inc(s_raw[p % 2], 16)

        def att_sp(sp):
            for p in (T_KV // 2, T_AQ // 2):
                later_piece(sp, p)
            tail_stores(sp, 0)
            later_piece(sp, T_AQ // 2 + 1)
            sp.wait_ge(free, U_KV)
            sp.wait_ge(s_tout, 128)
            for dup in range(2):
                for g in range(KVH):
                    sp.dma_start(KCR[:, :, g, dup, :], A["cache_k"][:, :, g, :].rearrange("s k d -> k s d"))\
                        .then_inc(s_cache, 16)
            later_piece(sp, T_AQ // 2 + 2)
            sp.wait_ge(free, U_Q)
            sp.dma_start(VS[0:CH, :], VZ[CH:128, :]).then_inc(s_vs, 16)
            sp.dma_start(VS[CH:128, 0:TT - 2], VZ[0:CH, 1:TT - 1]).then_inc(s_vs, 16)
            for dup in range(2):
                for g in range(KVH):
                    sp.dma_start(VCD[:, :, g, dup, :], A["cache_v"][:, :, g, :].rearrange("s k d -> k s d")).then_inc(s_vn, 16)
            for p in range(T_AQ // 2 + 3, T_AO // 2 + 1):
                later_piece(sp, p)
            for s in range(NS):
                sp.dma_start(VN[:, s], V4[SL * s:SL * s + SL]).then_inc(s_vn, 16)
            for p in range(T_AO // 2 + 1, T_AO // 2 + 2):
                later_piece(sp, p)
            for s in range(NS):
                r = slice(SL * s, SL * s + SL)
                sp.dma_start(O["k_s"][s, WIN - SL:WIN], KD[r, TT - 1, :, 0, :]).then_inc(s_out, 16)
                sp.dma_start(O["v_s"][s, WIN - SL:WIN], V4[r, :, 0, :]).then_inc(s_out, 16)
            sp.dma_start(O["k_p"][0], KD[:, TT - 2, :, 0, :]).then_inc(s_out, 16)
            sp.dma_start(O["v_p"][0], VZ[:, TT - 2, :, 0:HD]).then_inc(s_out, 16)
            for p in range(T_AO // 2 + 2, T_AO // 2 + 4):
                later_piece(sp, p)
            sp.wait_ge(a_o, NATT)
            sp.wait_ge(s_out, 16 * N_OUT)
            conv_loads(sp, 1)

        def att_pool(pool):
            pool.wait_ge(free, U_KV)
            pool.wait_ge(s_tout, 128)
            pool.memset(QZ[:, :, :, :, :, :], 0.0).then_inc(azero, 1)
            pool.memset(VZ[:, :, :, HD:2 * HD], 0.0).then_inc(azero, 1)

        N_OUT = 2 + 2 * NS + 2

        def stat_bank(j):
            return 2 * ((U_KV + j) % 4) + 1

        def att_pe(pe):
            for j in range(2):
                tm_unit(pe, T_KV, U_KV + j, TMU[j], fresh=2 * KT if j == 0 else None)
            pe.wait_ge(ss_done, (KT + 1) * 3)
            for t in range(TT):
                mm = pe.matmul(PS[:, stat_bank(0), t:t + 1], SS[:, 128 * t:128 * t + 128], ones[:, 0:1],
                               start=True, stop=True)
            mm.then_inc(s_stat, 1)
            pe.wait_ge(free, U_KV)
            for f in range(2):
                mm = pe.matmul(PS[:, stat_bank(1 + 2 * f), 0:HALF], ones[:, :], SS[:, f * HALF:(f + 1) * HALF],
                               start=True, stop=True)
            mm.then_inc(s_stat, 1)
            for j in range(2, 4):
                tm_unit(pe, T_KV, U_KV + j, TMU[j])
            fm_tile(pe, T_AQ, U_Q, fresh=3 * KT)
            for j in range(1, 4):
                fm_tile(pe, T_AQ + j, u_q(j))
            for g in range(KVH):
                u = U_KT + g
                pe.wait_ge(free, u - 3)
                for t in range(TT):
                    mm = pe.transpose(PS[:, 2 * (u % 4) + t // 4, 128 * (t % 4):128 * (t % 4) + 128],
                                      KD[:, t, g, :, :].rearrange("p a d -> p (a d)"), ident[:, :])
                mm.then_inc(full, 1)
            pe.wait_ge(s_cache, 16 * 4)
            for g in range(KVH):
                u = U_KC + g
                pe.wait_ge(free, u - 3)
                for s in range(NS):
                    mm = pe.transpose(PS[:, 2 * (u % 4) + s // 4, 128 * (s % 4):128 * (s % 4) + 128],
                                      KCR[:, s, g, :, :].rearrange("p a d -> p (a d)"), ident[:, :])
                mm.then_inc(full, 1)
            for j in range(4, 8):
                fm_tile(pe, T_AQ + j, u_q(j))
            pe.wait_ge(s_vs, 16 * 2)

            def scores(n):
                if n >= 2:
                    pe.wait_ge(a_ex, n - 1)
                if n < 2:
                    pe.wait_ge(free, u_q(5 + n) + 1)
                if n == 3:
                    pe.wait_ge(free, u_q(7) + 1)
                if n < NATT - NS:
                    c, m, g = step_of(n)
                    k0, nk = window(c)
                    for a in range(2):
                        h = slice(HD * a, HD * a + HD)
                        mm = pe.matmul(PS[:, score_bank(n) + a, 0:nk], QF[h, m // 2, c, :, :].rearrange("p m q -> p (m q)"),
                                       KTD[h, g, k0:k0 + nk], start=True, stop=True, tile_position=(HD * a, 0))
                else:
                    s = n - (NATT - NS)
                    if s == 0:
                        pe.wait_ge(qz, 16)
                    for g in range(KVH):
                        mm = pe.matmul(PS[:, score_bank(n) + g, 0:WIN + SL],
                                       QZ[:, s, g, :, :, :].rearrange("p e m t -> p (e m t)"), KCT[:, g, s, :],
                                       start=True, stop=True)
                mm.then_inc(a_sc, 1)

            def transposes(n):
                pe.wait_ge(a_p, n + 1)
                if n == 0:
                    pe.wait_ge(free, U_AO)
                if n >= 2:
                    pe.wait_ge(a_pt, n - 1)
                for a in range(2):
                    for x, k in enumerate(key_parts(n)):
                        mm = pe.transpose(PS[0:k, prob_bank(n), 256 * a + 128 * x:256 * a + 128 * x + 128],
                                          P[:, n % 2, 256 * a + 128 * x:256 * a + 128 * x + k], ident[:, :])
                mm.then_inc(a_tr, 1)

            def values(n):
                pe.wait_ge(a_pt, n + 1)
                if n >= 2:
                    pe.wait_ge(a_ol, n - 1)
                b = out_bank(n)
                if n < NATT - NS:
                    c, m, g = step_of(n)
                    ops = [(a, x, k) for a in range(2) for x, k in enumerate(key_parts(n))]
                    for j, (a, x, k) in enumerate(ops):
                        vv = VS if c % 2 and c > 1 else VZ
                        t = max(c // 2 - 1, 0) + x
                        mm = pe.matmul(PS[:, b, 0:128], vv[0:k, t, g, HD * a:HD * a + 128],
                                       PT[0:k, n % 2, 256 * a + 128 * x:256 * a + 128 * x + 128],
                                       start=(j == 0), stop=(j == len(ops) - 1))
                else:
                    s = n - (NATT - NS)
                    if s == 0:
                        pe.wait_ge(s_vn, 16 * (NS + 4))
                    for g in range(KVH):
                        o = PS[:, b, 128 * g:128 * g + 128]
                        pe.matmul(o, VCD[:, s, g, :, :].rearrange("p e d -> p (e d)"),
                                  PT[:, n % 2, 256 * g:256 * g + 128], start=True, stop=False)
                        mm = pe.matmul(o, VN[:, s, g, :, :].rearrange("p e d -> p (e d)"),
                                       PT[0:SL, n % 2, 256 * g + 128:256 * g + 256], start=False, stop=True)
                mm.then_inc(a_o, 1)

            for n in range(NATT + 3):
                if n < NATT:
                    scores(n)
                if n == NATT + 1:
                    pe.wait_ge(lo_done, T_AO + 1)
                    pe.wait_ge(a_ex, NATT - 1)
                    pe.wait_ge(a_ol, 4 * HALF // CH)
                    fm_half(pe, T_AO, U_AO, 0)
                if 2 <= n < NATT + 2:
                    transposes(n - 2)
                if n >= 3:
                    values(n - 3)
            pe.wait_ge(a_ol, NATT)
            fm_half(pe, T_AO, U_AO, 1).then_inc(full, 1)
            for j in range(1, KT):
                fm_tile(pe, T_AO + j, U_AO + j)

        def score_bank(n):
            return 2 * ((U_AO + n % 2) % 4)

        def prob_bank(n):
            return 2 * ((U_AO + 2) % 4) + n % 2

        def out_bank(n):
            return 2 * ((U_AO + 3) % 4) + n % 2

        def u_q(j):
            return U_Q + j + (4 if j >= 4 else 0)

        def step_of(n):
            c, m = n // 4, 2 * (n % 4)
            return c, m, m // 4

        def window(c):
            return CH * max(c - 2, 0), CH * min(c + 1, 3)

        def key_parts(n):
            if n >= NATT - NS:
                return [WIN, SL]
            nk = window(step_of(n)[0])[1]
            return [nk] if nk <= 128 else [128, nk - 128]

        def heads_out(n, a):
            b = out_bank(n)
            if n < NATT - NS:
                c, m, _ = step_of(n)
                return [PS[:, b, 0:128].rearrange("p (m q) -> p m q", m=2)] + \
                    [x[:, m:m + 2, CH * c:CH * c + CH] for x in (XH, XL)]
            s = n - (NATT - NS)
            h = slice(HD * a, HD * a + HD)
            c = SEQ + SL * s
            return [PS[h, b, 0:256].rearrange("p (g e m t) -> p g e m t", g=KVH, e=2, m=4)[:, :, a, :, :]] + \
                [x[h, :, c:c + SL].rearrange("p (g m) t -> p g m t", g=KVH) for x in (XH, XL)]

        def parts(n):
            return range(1 if n < NATT - NS else 2)

        def att_dve(v):
            v.wait_ge(rt_sq, RC[2] + 1)
            v.reciprocal(RT[:, :], RT[:, :]).then_inc(rstd, 1)
            v.wait_ge(rstd, RC[2] + 1)
            v.wait_ge(azero, 5)
            for j, groups in enumerate(TMU):
                if j == 3:
                    for k in range(KT):
                        rest_x(v, k, V_MIX + KT, XF[0] + 2 * KT)
                u = U_KV + j
                v.wait_ge(full, u + 1)
                if j == 1:
                    v.wait_ge(rt_sq, RC[2] + 2)
                for f, t in enumerate(groups):
                    k = PS[:, 2 * (u % 4) + f, 0:KVH * HD].rearrange("p (g d) -> p g d", g=KVH)
                    vv = PS[:, 2 * (u % 4) + f, KVH * HD:256].rearrange("p (g d) -> p g d", g=KVH)
                    for dup in range(2):
                        v.tensor_scalar(KD[:, t, :, dup, :], k, RT[:, t:t + 1], None, ALU.mult)
                        o = V4[:, :, dup, :] if t == TT - 1 else VZ[:, t, :, 2 * HD * dup:2 * HD * dup + HD]
                        mm = v.tensor_scalar(o, vv, RT[:, t:t + 1], None, ALU.mult)
                mm.then_inc(free, 1)
            for n in (T_AQ + 2, T_AQ + 3):
                rest_tile(v, n)
            v.wait_ge(s_sink, 16)
            for half in range(2):
                rows = slice(CH * half, CH * half + CH)
                v.tensor_copy(SKP[rows, :].rearrange("p (m e) -> p m e", e=2),
                              SKB[rows, :].rearrange("p (m f e) -> p m f e", f=2, e=2)[:, :, half, :])
            v.tensor_tensor(SKT[:, :], SKB[:, :], HB[:, :], ALU.mult).then_inc(sink_v, 1)
            v.wait_ge(sink_v, 1)
            v.tensor_reduce(SKR[:, :], SKT[:, :].rearrange("p (g h) -> p g h", g=KVH), AX.X, ALU.add).then_inc(sink_v, 1)
            v.reciprocal(RB[:, :], RB[:, :]).then_inc(rstd, 1)
            v.wait_ge(rstd, RC[2] + 2)
            for j in range(KT):
                if j == 4:
                    for g in range(KVH):
                        u = U_KT + g
                        v.wait_ge(full, u + 1)
                        v.tensor_copy(KTD[:, g, :], PS[:, 2 * (u % 4), :])
                        v.tensor_copy(KCT[:, g, :, WIN:WIN + SL], PS[:, 2 * (u % 4) + 1, 0:NS * SL]
                                      .rearrange("p (s t) -> p s t", s=NS)).then_inc(free, 1)
                    for g in range(KVH):
                        u = U_KC + g
                        v.wait_ge(full, u + 1)
                        v.tensor_copy(KCT[:, g, :, 0:WIN].rearrange("p (b s) k -> p b s k", b=2),
                                      PS[:, 2 * (u % 4):2 * (u % 4) + 2, :].rearrange("p b (s k) -> p b s k", k=WIN))\
                            .then_inc(free, 1)
                v.wait_ge(full, u_q(j) + 1)
                v.scalar_tensor_tensor(out=QF[:, j // 2, :, j % 2, :].rearrange("p (a c) q -> p a c q", a=2),
                                       in0=unit(u_q(j)).rearrange("p a (c q) -> p a c q", q=CH),
                                       scalar=HD ** -0.5, in1=RB[:, :].rearrange("p (a c q) -> p a c q", a=2, q=CH),
                                       op0=ALU.mult, op1=ALU.mult).then_inc(free, 1)
                if j < KT - 1:
                    rest_tile(v, T_AQ + 4 + j)

            def maxima(n):
                v.wait_ge(a_sc, n + 1)
                b = n % 2
                sc = PS[:, score_bank(n):score_bank(n) + 2, 0:sum(key_parts(n))]
                sink = SKP[:, 2 * (n % 4):2 * (n % 4) + 2] if n < NATT - NS else SKR[:, :]
                v.tensor_reduce(NM[:, b, :], sc, AX.X, ALU.max).then_inc(a_chain, 1)
                v.wait_ge(a_chain, 2 * n + 1)
                v.tensor_tensor(NM[:, b, :], NM[:, b, :], sink, ALU.max).then_inc(a_chain, 1)
                v.wait_ge(a_chain, 2 * n + 2)
                v.tensor_tensor(SE[:, b, :], sink, NM[:, b, :], ALU.subtract)
                v.tensor_scalar(NM[:, b, :], NM[:, b, :], -1.0, None, ALU.mult).then_inc(a_nm, 1)

            def normalise(n):
                b = n % 2
                v.wait_ge(a_ex, n + 1)
                v.tensor_tensor(ES[:, b, :], ES[:, b, :], SE[:, b, :], ALU.add).then_inc(a_sum, 1)
                v.wait_ge(a_sum, 2 * n + 1)
                v.reciprocal(ES[:, b, :], ES[:, b, :]).then_inc(a_sum, 1)
                v.wait_ge(a_sum, 2 * n + 2)
                for a in range(2):
                    w = prob_cols(n, a)
                    mm = v.tensor_scalar(P[:, b, w], P[:, b, w], ES[:, b, a:a + 1], None, ALU.mult)
                mm.then_inc(a_p, 1)

            def rest_out(n):
                v.wait_ge(a_oh, n + 1)
                for a in parts(n):
                    i_, oh, ol = heads_out(n, a)
                    mm = v.tensor_tensor(ol, i_, f32(oh), ALU.subtract)
                mm.then_inc(a_ol, 1)

            def spread_queries(g, e, cc, m):
                h = slice(HD * e, HD * e + HD)
                v.tensor_copy(QZ[h, 4 * cc:4 * cc + 4, g, e, m:4:2, :].rearrange("p s m t -> p m s t"),
                              QF[h, 2 * g:2 * g + 2, SEQ // CH + cc, m, :].rearrange("p m (s t) -> p m s t", t=SL))\
                    .then_inc(qz, 1)

            v.wait_ge(free, U_AO)
            for n in range(NATT + 4):
                if 4 <= n < 20:
                    spread_queries((n - 4) // 8, (n - 4) // 4 % 2, (n - 4) // 2 % 2, n % 2)
                if n < NATT:
                    maxima(n)
                if n == 3:
                    rest_tile(v, T_AQ + 4 + KT - 1)
                if 1 <= n <= NATT:
                    normalise(n - 1)
                if n >= 4:
                    rest_out(n - 4)
            add_and_resplit(v, T_AO, U_AO, V_FFN + KT, XF[1])

        def prob_cols(n, a):
            return slice(256 * a, 256 * a + sum(key_parts(n)))

        def att_act(act):
            load_table(act, ACT.Sqrt)
            act.wait_ge(s_stat, 1)
            act.activation(RT[:, :], PS[:, stat_bank(0), 0:TT], ACT.Sqrt, bias=eps[:, 0:1], scale=1.0 / D).then_inc(rt_sq, 1)
            act.wait_ge(s_stat, 2)
            for f in range(2):
                mm = act.activation(RB[:, f * HALF:(f + 1) * HALF], PS[:, stat_bank(1 + 2 * f), 0:HALF], ACT.Sqrt,
                                    bias=eps[:, 0:1], scale=1.0 / D)
            mm.then_inc(rt_sq, 1)
            act.wait_ge(full, U_KV + 4)
            for k in range(KT):
                round_x(act, k, V_MIX + KT)
            for n in (T_AQ + 2, T_AQ + 3):
                round_tile(act, n)
            for j in range(KT - 1):
                act.wait_ge(full, u_q(j) + 1)
                round_tile(act, T_AQ + 4 + j)
            load_table(act, ACT.Exp)

            def exponentials(n):
                b = n % 2
                act.wait_ge(a_nm, n + 1)
                if n >= 2:
                    act.wait_ge(a_tr, n - 1)
                for a in range(2):
                    w = prob_cols(n, a)
                    act.activation(P[:, b, w], PS[:, score_bank(n) + a, 0:w.stop - w.start], ACT.Exp,
                                   bias=NM[:, b, a:a + 1], accum_out=ES[:, b, a:a + 1])
                act.activation(SE[:, b, :], SE[:, b, :], ACT.Exp).then_inc(a_ex, 1)

            def to_sbuf(n):
                act.wait_ge(a_tr, n + 1)
                if n >= 2:
                    act.wait_ge(a_o, n - 1)
                b = n % 2
                o, i_ = [x.rearrange("p (a k) -> p a k", a=2) for x in (PT[:, b, :], PS[:, prob_bank(n), :])]
                parts = key_parts(n)
                if parts[-1] == CH:
                    w = 128 * len(parts)
                    k = 128 if len(parts) == 2 else CH
                    act.activation(o[0:k, :, 0:w], i_[0:k, :, 0:w], ACT.Copy).then_inc(a_pt, 1)
                else:
                    for x, k in enumerate(parts):
                        w = slice(128 * x, 128 * x + 128)
                        mm = act.activation(o[0:k, :, w], i_[0:k, :, w], ACT.Copy)
                    mm.then_inc(a_pt, 1)

            def round_out(n):
                act.wait_ge(a_o, n + 1)
                for a in parts(n):
                    i_, oh, _ = heads_out(n, a)
                    mm = act.activation(oh, i_, ACT.Copy)
                mm.then_inc(a_oh, 1)

            act.wait_ge(full, U_KC + 2)
            for n in range(NATT + 4):
                if n >= 4:
                    round_out(n - 4)
                if 2 <= n < NATT + 2:
                    to_sbuf(n - 2)
                if n < NATT:
                    exponentials(n)
                if n == 2:
                    round_tile(act, T_AQ + 4 + KT - 1)
            square_and_resplit(act, T_AO, U_AO, 3, V_FFN + KT)

        def final_pe(pe):
            for t in range(TT):
                u = U_Y + t
                pe.wait_ge(free, u - 3)
                for k in range(KT):
                    if t == 0:
                        pe.wait_ge(free, U_Y - 2 - KT + k + 1)
                    mm = pe.transpose(PS[:, 2 * (u % 4) + k // 4, 128 * (k % 4):128 * (k % 4) + 128],
                                      X[:, k, 128 * t:128 * t + 128], ident[:, :])
                mm.then_inc(full, 1)

        def final_act(act):
            load_table(act, ACT.Sqrt)
            for t in range(TT):
                u = U_Y + t
                act.wait_ge(full, u + 1)
                if t:
                    act.wait_ge(ysq, t)
                act.activation(FSQ[:, :], rows_unit(u), ACT.Square, accum_out=SSF[:, t:t + 1]).then_inc(ysq, 1)
                act.wait_ge(ysq, t + 1)
                act.activation(RT[:, t:t + 1], SSF[:, t:t + 1], ACT.Sqrt, bias=eps[:, 0:1], scale=1.0 / D).then_inc(rt_sq, 1)

        def rows_unit(u):
            return PS[:, 2 * (u % 4):2 * (u % 4) + 2, :].rearrange("p b c -> p (b c)")

        def final_dve(v):
            v.wait_ge(s_nfb, 16)
            for t in range(TT):
                u = U_Y + t
                v.wait_ge(rt_sq, RC[4] + t + 1)
                v.reciprocal(RT[:, t:t + 1], RT[:, t:t + 1]).then_inc(rstd, 1)
                v.wait_ge(rstd, RC[4] + t + 1)
                v.scalar_tensor_tensor(out=YO[:, t, :], in0=rows_unit(u), scalar=RT[:, t:t + 1], in1=NFB[:, :],
                                       op0=ALU.mult, op1=ALU.mult).then_inc(free, 1)

        def final_sp(sp):
            yp = O["y_p"][0].rearrange("(t p) d -> p t d", p=128)
            ys = O["y_s"].rearrange("s l d -> (s l) d")
            sp.wait_ge(full, U_F[1] + fu(NIT - 1) + 12)
            sp.dma_start(NFB[:, :], A["norm_final"].rearrange("(o n) -> o n", o=1).to_broadcast([128, D])).then_inc(s_nfb, 16)
            for t in range(TT):
                sp.wait_ge(free, U_Y + t + 1)
                sp.dma_start(yp[:, t, :] if t < TT - 1 else ys, YO[:, t, :]).then_inc(s_y, 16)
                if t < 4:
                    tail_store(sp, 1, t)
            sp.wait_ge(s_y, 16 * TT)
            sp.wait_ge(s_tout, 2 * 128)
            sp.wait_ge(s_out, 16 * N_OUT)


        def front_sp(sp):
            xp = A["x_prompt"][0].rearrange("(t p) d -> p t d", p=128)
            xs = A["x_sample"].rearrange("s l d -> (s l) d")
            vecs = ((0, A["norm_mix"].rearrange("l (k p) -> (l k) p", p=128)),
                    (16, A["norm_ffn"].rearrange("l (k p) -> (l k) p", p=128)),
                    (32, A["norm_kv"].rearrange("(k p) -> k p", p=128)),
                    (40, A["norm_final"].rearrange("(k p) -> k p", p=128)),
                    (48, A["gla_g_onorm"][0].rearrange("(k p) -> k p", p=128)),
                    (50, A["gla_b_g2"][0].rearrange("(k p) -> k p", p=128)))
            for t, (r, v) in enumerate(vecs):
                if t < TT:
                    sp.dma_start(XIN[:, t, :], xp[:, t, :] if t < TT - 1 else xs).then_inc(s_xin, 16)
                sp.dma_start(NRAW[r:r + v.shape[0], :], v).then_inc(s_const, 16)
            for p, (w, c) in enumerate(pieces[:2]):
                n = 256 if p else 128
                sp.dma_start(WRAW[:, p, :, 0:n], w.rearrange("(k p) n -> p k n", p=128)[:, :, c:c + n])\
                    .then_inc(s_raw[p], 16)
            sp.dma_start(SKB[:, :], A["att_sinks"].to_broadcast([128, NH])).then_inc(s_sink, 16)
            for o, c in (("k_s", "cache_k"), ("v_s", "cache_v")):
                sp.dma_start(O[o][:, 0:WIN - SL], A[c][:, SL:WIN]).then_inc(s_out, 16)
            sp.wait_ge(s_setup, 1)
            sp.dma_start(G2[128 - RANK:128, :], A["gla_w_g2"][0]).then_inc(s_g2, 16)
            def piece(p):
                w, c = pieces[p]
                sp.wait_ge(lo_done, 2 * p - 2)
                sp.dma_start(WRAW[:, p % 2, :, :], w.rearrange("(k p) n -> p k n", p=128)[:, :, c:c + 256])\
                    .then_inc(s_raw[p % 2], 16)

            for p in range(2, T_WO // 2 + 2):
                piece(p)
                if p == 4:
                    sp.wait_ge(free, U_X + KT)
                    sp.dma_start(XSP, X[:, :, :]).then_inc(s_spill, 16)
            for h in range(H):
                if h == 0:
                    sp.wait_ge(full, U_Z + 4)
                else:
                    sp.wait_ge(st_done, 8 * (h - 1) + 4)
                    sp.dma_start(O["gla_s"][0, :, h - 1].rearrange("s p d -> p s d"), S0[:, :, :]).then_inc(s_sout, 16)
                    sp.wait_ge(s_sout, 16 * h)
                sp.dma_start(S0[:, :, :], A["state_gla"][0, :, h].rearrange("s p d -> p s d")).then_inc(s_s0, 16)
                if h:
                    sp.wait_ge(st_done, 8 * h)
                    sp.dma_start(O["gla_p"][0, 0, h - 1], ST[:, :]).then_inc(s_pout, 16)
            sp.wait_ge(st_done, 8 * H)
            sp.dma_start(O["gla_s"][0, :, H - 1].rearrange("s p d -> p s d"), S0[:, :, :]).then_inc(s_sout, 16)
            sp.dma_start(O["gla_p"][0, 0, H - 1], ST[:, :]).then_inc(s_pout, 16)
            sp.wait_ge(att, STEPS)
            sp.dma_start(X[:, :, :], XSP).then_inc(s_xback, 16)
            for p in range(T_WO // 2 + 2, T_WO // 2 + 4):
                piece(p)
            sp.wait_ge(full, U_WO)
            conv_loads(sp, 0)
            sp.wait_ge(s_sout, 16 * H)
            sp.wait_ge(s_pout, 16 * H)

        def front_pool(pool):
            pool.memset(G2[:, :], 0.0).then_inc(s_setup, 1)
            pool.memset(ident[:, :], 0.0).then_inc(s_setup, 1)
            pool.memset(ones[:, :], 1.0).then_inc(s_setup, 1)
            pool.memset(eps[:, 0:1], EPS)
            pool.memset(eps[:, 1:2], DK * EPS).then_inc(s_setup, 1)
            pool.memset(EV[:, :], 1.0).then_inc(s_setup, 1)
            pool.wait_ge(s_setup, 5)
            pool.affine_select(out=ident[:, :], in_=ident[:, :], compare_op=ALU.not_equal, fill=1.0, base=0,
                               pattern=[[-1, 128]], channel_multiplier=1).then_inc(s_setup, 1)
            pool.affine_select(out=EV[:, :], in_=EV[:, :], compare_op=ALU.is_ge, fill=0.0, base=0,
                               pattern=[[-2 * SL, 4]], channel_multiplier=1).then_inc(s_setup, 1)
            pool.wait_ge(s_setup, 7)
            pool.affine_select(out=EV[:, :], in_=EV[:, :], compare_op=ALU.is_ge, fill=0.0, base=SL - 1,
                               pattern=[[2 * SL, 4]], channel_multiplier=-1).then_inc(s_setup, 1)
            clear_sums(pool, 0)
            for k in range(KT):
                add_squares(pool, k, 0)
            pool.memset(HB[:, :], 1.0).then_inc(azero, 1)
            pool.wait_ge(azero, 1)
            bands = [[0, KVH], [-SL, 4], [-HD, 2]]
            pool.affine_select(out=HB[:, :], in_=HB[:, :], compare_op=ALU.is_ge, fill=0.0, base=0,
                               pattern=bands, channel_multiplier=1).then_inc(azero, 1)
            pool.wait_ge(azero, 2)
            pool.affine_select(out=HB[:, :], in_=HB[:, :], compare_op=ALU.is_ge, fill=0.0, base=SL - 1,
                               pattern=[[0, KVH], [SL, 4], [HD, 2]], channel_multiplier=-1).then_inc(azero, 1)
            pool.wait_ge(s_spill, 16)
            pool.wait_ge(xl_done, KT)
            pool.memset(MASK[:, :, :], 0.0).then_inc(s_mask, 1)
            pool.wait_ge(s_mask, 1)
            n = 1
            m0 = MASK[:, 0, :].rearrange("p (b r) -> p b r", r=BLK)
            views = [(m0, 128 // BLK, BLK)]
            for l in range(1, 4):
                hf = BLK << (l - 1)
                views.append((MASK[:, l, :].rearrange("p (s two r) -> p s two r", two=2, r=hf)[:, :, 1, :], 64 // hf, hf))
            for v, _, _ in views:
                pool.memset(v, 1.0).then_inc(s_mask, 1)
                n += 1
            pool.wait_ge(s_mask, n)
            for l, (v, ns, w) in enumerate(views):
                sup = w if l == 0 else 2 * w
                pool.affine_select(out=v, in_=v, compare_op=ALU.is_ge, fill=0.0, base=0,
                                   pattern=[[-sup, ns], [0, w]], channel_multiplier=1).then_inc(s_mask, 1)
                n += 1
            pool.wait_ge(s_mask, n)
            pool.affine_select(out=m0, in_=m0, compare_op=ALU.is_ge, fill=0.0, base=0,
                               pattern=[[BLK, 128 // BLK], [1, BLK]], channel_multiplier=-1).then_inc(s_mask, 1)
            for l, (v, ns, w) in list(enumerate(views))[1:]:
                pool.affine_select(out=v, in_=v, compare_op=ALU.is_ge, fill=0.0, base=w - 1,
                                   pattern=[[2 * w, ns], [0, w]], channel_multiplier=-1).then_inc(s_mask, 1)
            pool.wait_ge(full, U_Z + 4)
            pool.memset(QM[:, :], 0.0).then_inc(zset, 1)
            pool_kr(pool, 0)
            pool_operands(pool, 0)
            for h in range(H):
                if h:
                    pool_kr(pool, h)
                pool_levels(pool, h)
                if h:
                    pool_operands(pool, h)
                pool_level_operands(pool, h)
            clear_sums(pool, 1)
            for k in range(KT):
                add_squares(pool, k, 1)

        NMASK = 1 + 4 + 4 + 4

        def kq_view(i, j):
            return QK[:, bass.ds(4 * i + j, 1), :].rearrange("p a t -> p (a t)")

        def front_pe(pe):
            pe.wait_ge(s_setup, 8)
            pe.wait_ge(s_const, 16 * 6)
            pe.transpose(PS[:, 0, 0:NVEC], NRAW[:, :], ident[0:NVEC, 0:NVEC]).then_inc(full, 1)
            pe.wait_ge(s_xin, 16 * TT)
            for k in range(KT):
                u = U_X + k
                if u >= 4:
                    pe.wait_ge(free, u - 3)
                for t in range(TT):
                    mm = pe.transpose(PS[:, 2 * (u % 4) + t // 4, 128 * (t % 4):128 * (t % 4) + 128],
                                      XIN[:, t, 128 * k:128 * k + 128], ident[:, :])
                mm.then_inc(full, 1)
            fm_tile(pe, T_GL, U_GL, fresh=0)
            stat_cols(pe, U_GL + 1, 0)
            stat_rows(pe, U_GL + 2)
            with pe.Fori(0, 2) as i:
                for j in range(4):
                    fm_tile(pe, T_KQ + j, U_KQ + j, i)
            pe.wait_ge(s_g2, 16)
            for h in range(H):
                u = U_Z + h
                pe.wait_ge(free, u - 3)
                for f in range(2):
                    mm = pe.matmul(PS[:, 2 * (u % 4) + f, 0:HALF], G2[:, DK * h:DK * h + DK],
                                   GLS[:, f * HALF:(f + 1) * HALF], start=True, stop=True)
                mm.then_inc(full, 1)
            for t0, u0 in ((T_V, U_V), (T_R, U_R)):
                with pe.Fori(0, 2) as i:
                    for q in range(2):
                        for j, groups in enumerate(TMU):
                            tm_unit(pe, t0 + 2 * q, u0 + 4 * q + j, groups, i)
            gla_pe(pe)
            pe.wait_ge(att, STEPS)
            pe.wait_ge(osq, STEPS)
            pe.wait_ge(st_done, 8 * H)
            pe.wait_ge(ogh, H - 1)
            for n, (g, p) in enumerate(OT_PARTS):
                if n == 0:
                    pe.wait_ge(osq, STEPS)
                if g == TT - 1 and p == 0:
                    pe.wait_ge(free, U_OT + g - 3)
                if p:
                    pe.wait_ge(ogn, g + 1)
                for kt in range(4 * p, 4 * p + 4):
                    mm = pe.transpose(PS[:, 2 * ((U_OT + g) % 4) + p, 128 * (kt % 4):128 * (kt % 4) + 128],
                                      RS[:, g, 128 * kt:128 * kt + 128], ident[:, :])
                mm.then_inc(full if p else ot_part, 1)
            pe.wait_ge(lo_done, T_WO + 1)
            pe.wait_ge(free, U_OT + 3)
            fm_half(pe, T_WO, U_WO, 0)
            pe.wait_ge(free, U_OT + TT)
            fm_half(pe, T_WO, U_WO, 1).then_inc(full, 1)
            for j in range(1, 4):
                fm_tile(pe, T_WO + j, U_WO + j)
            for j in range(4, 8):
                fm_tile(pe, T_WO + j, U_WO + j)

        def front_dve(v):
            v.wait_ge(full, 1)
            v.tensor_copy(NW[:, :], PS[:, 0, 0:NVEC]).then_inc(free, 1)
            v.wait_ge(free, 1)
            for k in range(KT):
                u = U_X + k
                v.wait_ge(full, u + 1)
                v.tensor_copy(X[:, k, 0:512], PS[:, 2 * (u % 4), :])
                v.tensor_copy(X[:, k, 512:T], PS[:, 2 * (u % 4) + 1, 0:T - 512]).then_inc(free, 1)
                if k:
                    rest_x(v, k - 1, V_MIX, 0)
                if k == 4:
                    rest_tile(v, T_GL, inc=2)
            rest_x(v, KT - 1, V_MIX, 0)
            rest_tile(v, 2)
            rest_tile(v, 3)
            v.wait_ge(s_setup, 8)
            v.tensor_reduce(EO[:, 0:1], EV[:, :], AX.X, ALU.add).then_inc(dve, 1)
            v.wait_ge(dve, 1)
            v.tensor_scalar(EO[:, 1:2], EO[:, 0:1], -1.0, 1.0, ALU.mult, ALU.add).then_inc(dve, 1)
            invert(v, 0, True)
            v.wait_ge(rstd, 2)
            v.tensor_tensor(halves(GLS[:, :]), unit(U_GL), halves(RB[:, :]), ALU.mult).then_inc(free, 3)
            for n in (4, 5):
                rest_tile(v, n)
            with v.Fori(0, 2) as i:
                for j in range(4):
                    v.wait_ge(full, U_KQ + j + 1 + 4 * i)
                    v.tensor_tensor(halves(kq_view(i, j)), unit(U_KQ + j), halves(RB[:, :]), ALU.mult)\
                        .then_inc(free, 1)
                    rest_tile(v, T_KQ + 4 + j, i)
            v.wait_ge(s_spill, 16)
            v.wait_ge(xh_done, KT)
            v.wait_ge(sq_done, KT)
            v.memset(M16[:, :], 1.0).then_inc(dve, 1)
            v.memset(M128[:, :], 1.0).then_inc(dve, 1)
            v.wait_ge(dve, 4)
            v.memset(M16[:, 0:T:BLK], 0.0).then_inc(dve, 1)
            v.memset(M128[:, 0:SEQ:128], 0.0).then_inc(dve, 1)
            v.memset(M128[:, SEQ:T:SL], 0.0).then_inc(dve, 1)
            for h in range(H):
                v.wait_ge(full, U_Z + h + 1)
                v.wait_ge(s_mn, h + 1)
                v.tensor_scalar(halves(LA[:, h, :]), unit(U_Z + h), NW[:, V_BG + h:V_BG + h + 1], 0.0,
                                ALU.add, ALU.min).then_inc(free, 1)
            v.wait_ge(s_mn, H + 2)
            v.wait_ge(free, U_V)
            v.tensor_tensor(LA[:, :, :], LA[:, :, :], AB[:, :, :], ALU.subtract).then_inc(s_la, 1)
            v.wait_ge(s_la, 1)
            v.wait_ge(dve, 7)
            with v.Fori(0, 2) as i:
                for q in range(2):
                    for j, groups in enumerate(TMU):
                        u = U_V + 4 * q + j
                        v.wait_ge(full, u + 1 + 8 * i)
                        for f, t in enumerate(groups):
                            mm = v.tensor_scalar(V[:, t, bass.ds(256 * q + 512 * i, 256)],
                                                 PS[:, 2 * (u % 4) + f, 0:256], RT[:, t:t + 1], None, ALU.mult)
                        mm.then_inc(free, 1)
                    for n in range(2):
                        rest_tile(v, T_V + 4 + 2 * q + n, i)
            gla_sums(v, 0)
            gla_operands(v, 0)
            gla_queries(v, 0)
            for n in range(6):
                rest_tile(v, T_R + 4 + n)
            gla_dve(v)
            head_inverse(v, H - 1)
            v.wait_ge(rt_h, 2 * H)
            v.wait_ge(og, STEPS)
            for g in range(TT):
                scale_head(v, H - 1, g).then_inc(ogn, 1)
            for n, (g, p) in enumerate(OT_PARTS):
                v.wait_ge(oth, n + 1)
                for e in range(2):
                    i_, oh, ol = ot_views(g, p, e)
                    mm = v.scalar_tensor_tensor(out=ol, in0=i_, scalar=NW[:, V_ON + e:V_ON + e + 1], in1=f32(oh),
                                                op0=ALU.mult, op1=ALU.subtract)
                if p:
                    mm.then_inc(free, 1)
            v.wait_ge(s_xback, 16)
            add_and_resplit(v, T_WO, U_WO, V_FFN, XF[0])

        def head_root(act, h):
            c = slice(TT * h, TT * h + TT)
            act.wait_ge(osq, TT * (h + 1))
            act.activation(RH[:, c], SSH[:, c], ACT.Sqrt, scale=1.0 / DV, bias=eps[:, 1:2]).then_inc(rt_h, 1)

        def head_inverse(v, h):
            c = slice(TT * h, TT * h + TT)
            v.wait_ge(rt_h, 2 * h + 1)
            v.reciprocal(RH[:, c], RH[:, c]).then_inc(rt_h, 1)

        def scale_head(e, h, g):
            r_, n = RS[:, g, DV * h:DV * h + DV], RH[:, TT * h + g:TT * h + g + 1]
            if h == H - 1:
                return e.tensor_scalar(r_, r_, n, None, ALU.mult)
            return e.activation(r_, r_, ACT.Copy, scale=n)

        OT_PARTS = [(g, p) for p in range(2) for g in range(4)] + [(TT - 1, 0), (TT - 1, 1)]

        def ot_views(g, p, e):
            i_ = PS[:, 2 * ((U_OT + g) % 4) + p, :].rearrange("p (c e q) -> p c e q", c=2, e=2)[:, :, e, :]
            o_ = [x[:, 4 * p:4 * p + 4, 128 * g:128 * g + 128].rearrange("p (c e) q -> p c e q", e=2)[:, :, e, :]
                  for x in (XH, XL)]
            return i_, o_[0], o_[1]

        def front_act(act):
            for k in range(KT):
                act.wait_ge(free, U_X + k + 1)
                round_x(act, k, V_MIX)
                square_x(act, k, 0)
                if k == 2:
                    round_tile(act, T_GL, inc=2)
            round_tile(act, 2)
            round_tile(act, 3)
            roots(act, U_GL + 1, True)
            act.wait_ge(full, U_GL + 1)
            for n in (4, 5):
                round_tile(act, n)
            with act.Fori(0, 2) as i:
                for j in range(4):
                    act.wait_ge(full, U_KQ + j + 1 + 4 * i)
                    round_tile(act, T_KQ + 4 + j, i)
            for h in range(H):
                act.wait_ge(full, U_Z + h + 1)
                act.activation(halves(AB[:, h, :]), unit(U_Z + h), ACT.Abs, bias=NW[:, V_BG + h:V_BG + h + 1])\
                    .then_inc(s_mn, 1)
            act.wait_ge(s_mn, H)
            act.activation(AB[:, :, :], AB[:, :, :], ACT.Exp, scale=-1.0).then_inc(s_mn, 1)
            act.wait_ge(s_mn, H + 1)
            act.activation(AB[:, :, :], AB[:, :, :], ACT.Ln, bias=1.0).then_inc(s_mn, 1)
            with act.Fori(0, 2) as i:
                for q in range(2):
                    act.wait_ge(full, U_V + 4 * q + 4 + 8 * i)
                    for n in range(2):
                        round_tile(act, T_V + 4 + 2 * q + n, i)
            gla_exps(act, 0)
            act.wait_ge(free, U_R)
            act.wait_ge(s_la, 1)
            for q in range(4):
                for j, groups in enumerate(TMU):
                    u = U_R + 4 * q + j
                    act.wait_ge(full, u + 1)
                    for f, t in enumerate(groups):
                        mm = act.activation(RS[:, t, 256 * q:256 * q + 256], PS[:, 2 * (u % 4) + f, 0:256], ACT.Silu,
                                            scale=RT[:, t:t + 1])
                    mm.then_inc(free, 1)
                if q < 3:
                    for n in range(2):
                        round_tile(act, T_R + 4 + 2 * q + n)
            gla_act(act)
            head_root(act, H - 1)
            for n, (g, p) in enumerate(OT_PARTS):
                if p:
                    act.wait_ge(full, U_OT + g + 1)
                else:
                    act.wait_ge(ot_part, g + 1)
                for e in range(2):
                    i_, oh, _ = ot_views(g, p, e)
                    mm = act.activation(oh, i_, ACT.Copy, scale=NW[:, V_ON + e:V_ON + e + 1])
                mm.then_inc(oth, 1)
            square_and_resplit(act, T_WO, U_WO, 1, V_FFN)

        def gla_pe(pe):
            pe.wait_ge(free, U_OT)
            pe.wait_ge(s_mask, NMASK)

            def scores(n):
                h, g = n // TT, GO[n % TT]
                s = h % 2
                if n % TT == 0:
                    pe.wait_ge(prep, 2 * h + 1)
                    pe.wait_ge(prepp, h + 1)
                if n % TT == 1:
                    pe.wait_ge(prepl, h + 1)
                    pe.wait_ge(preplp, h + 1)
                if n >= 2:
                    pe.wait_ge(kt_done, n - 1)
                pe.transpose(PS[:, 6 + n % 2, 0:128], kr(s)[:, 128 * g:128 * g + 128], ident[:, :])\
                    .then_inc(tr_full, 1)
                if n >= 2:
                    pe.wait_ge(att, n - 1)
                c = slice(128 * g, 128 * g + 128)
                mm = pe.matmul(PS[:, n % 2, 0:128], kd(s)[:, c], qd(s)[:, c], start=True, stop=True)
                if g < TT - 1:
                    for l in range(1, 4):
                        mm = pe.matmul(PS[:, n % 2, 128 * l:128 * l + 128], kl(s, l)[:, c], ql(s, l)[:, c],
                                       start=True, stop=True)
                mm.then_inc(sc_full, 1)

            def outputs(n):
                h, j = n // TT, n % TT
                g = GO[j]
                s = h % 2
                pe.wait_ge(att, n + 1)
                if n >= 2:
                    pe.wait_ge(og, n - 1)
                o = PS[:, 2 + n % 2, 0:DV]
                vv = V[:, g, DV * h:DV * h + DV]
                mm = pe.matmul(o, AT[:, n % 2, :], vv, start=True, stop=(j == 1))
                if j == 0:
                    pe.wait_ge(prep, 2 * h + 2)
                    pe.wait_ge(s_s0, 16 * (h + 1))
                    for q in range(NS):
                        mm = pe.matmul(o, QM[:, 128 * q:128 * q + 128], S0[:, q, :], start=False, stop=(q == NS - 1))
                elif j >= 2:
                    pe.wait_ge(st_done, 8 * h + 4 + j - 1)
                    mm = pe.matmul(o, QI[:, s, 128 * g:128 * g + 128], ST[:, :], start=False, stop=True)
                mm.then_inc(o_full, 1)
                pe.wait_ge(kt_done, n + 1)
                for x in range(4 if j == 0 else 1):
                    cnt = 8 * h + x if j == 0 else 8 * h + 4 + j - 1
                    if cnt >= 2:
                        pe.wait_ge(st_done, cnt - 1)
                    b = 4 + cnt % 2
                    if j:
                        mm = pe.matmul(PS[:, b, 0:DV], KTK[:, 2 * (n % 2), :], vv, start=True, stop=True)
                    else:
                        for e in range(2):
                            r = slice(32 * x, 32 * x + 32)
                            mm = pe.matmul(PS[:, b, DV * e:DV * e + DV], KTK[r, 2 * (n % 2) + e, :],
                                           V[r, g, DV * h:DV * h + DV], start=True, stop=True,
                                           tile_position=(32 * x, 0))
                    mm.then_inc(st_full, 1)

            scores(0)
            outputs(0)
            for n in range(1, STEPS + 1):
                if n < STEPS:
                    scores(n)
                if n > 1:
                    outputs(n - 1)

        def span(ap, l, odd):
            hf = BLK << (l - 1)
            return ap.rearrange("p (s two r) -> p s two r", two=2, r=hf)[:, :, odd, :]

        def gla_sums(v, h):
            if h:
                v.wait_ge(exps, h)
                v.wait_ge(argk, h)
                v.wait_ge(argp, h)
            v.tensor_tensor_scan(B16[:, :], M16[:, :], LA[:, h, :], 0.0, ALU.mult, ALU.add).then_inc(cum, 1)
            v.tensor_tensor_scan(B128[:, :], M128[:, :], LA[:, h, :], 0.0, ALU.mult, ALU.add).then_inc(cum, 1)

        def gla_levels(v, h):
            s = h % 2
            v.wait_ge(cum, 2 * h + 2)
            if h >= 2:
                v.wait_ge(sc_full, TT * (h - 1))
            for l in range(1, 4):
                hf = BLK << (l - 1)
                even, odd = span(B128[:, 0:SEQ], l, 0), span(B128[:, 0:SEQ], l, 1)
                mm = v.tensor_tensor(span(ql(s, l), l, 1), odd,
                                     even[:, :, hf - 1:hf].to_broadcast([128, SEQ // (2 * hf), hf]), ALU.subtract)
            mm.then_inc(argl, 1)

        def gla_operands(v, h):
            s = h % 2
            v.wait_ge(exps, h + 1)
            v.tensor_tensor(kd(s), kd(s), QK[:, h, :], ALU.mult)
            v.tensor_tensor(qd(s), qd(s), QK[:, H + h, :], ALU.mult).then_inc(prep, 1)

        def gla_queries(v, h):
            s = h % 2
            v.wait_ge(prep, 2 * h + 1)
            v.wait_ge(zset, 1)
            if h:
                v.wait_ge(o_full, TT * (h - 1) + 1)
            qs = qd(s)[:, SEQ:T].rearrange("p (s t) -> p s t", t=SL)
            n = NS - 1
            v.tensor_copy(QM[:, 0:n * (128 + SL)].rearrange("p (s c) -> p s c", s=n)[:, :, 0:SL], qs[:, 0:n, :])
            v.tensor_copy(QM[:, n * (128 + SL):n * (128 + SL) + SL], qs[:, n, :]).then_inc(prep, 1)

        def gla_level_operands(v, h):
            s = h % 2
            v.wait_ge(expl, h + 1)
            for l in range(1, 4):
                mm = v.tensor_tensor(span(ql(s, l), l, 1), span(ql(s, l), l, 1), span(QK[:, H + h, 0:SEQ], l, 1), ALU.mult)
            mm.then_inc(prepl, 1)

        def pool_kr(pool, h):
            s = h % 2
            pool.wait_ge(cum, 2 * h + 2)
            if h >= 2:
                pool.wait_ge(tr_full, TT * (h - 1))
            b = B128[:, 0:SEQ].rearrange("p (g t) -> p g t", t=128)
            pool.tensor_tensor(kr(s)[:, 0:SEQ].rearrange("p (g t) -> p g t", t=128),
                               b[:, :, 127:128].to_broadcast([128, TT - 1, 128]), b, ALU.subtract)
            bs = B16[:, SEQ:T].rearrange("p (s t) -> p s t", t=SL)
            pool.tensor_tensor(kr(s)[:, SEQ:T].rearrange("p (s t) -> p s t", t=SL),
                               bs[:, :, SL - 1:SL].to_broadcast([128, NS, SL]), bs, ALU.subtract).then_inc(argk, 1)

        def pool_operands(pool, h):
            s = h % 2
            pool.wait_ge(exps, h + 1)
            pool.tensor_tensor(kr(s), kr(s), QK[:, h, :], ALU.mult)
            pool.tensor_tensor(QI[:, s, :], QI[:, s, :], QK[:, H + h, 0:SEQ], ALU.mult).then_inc(prepp, 1)

        def pool_levels(pool, h):
            s = h % 2
            if h == 0:
                pool.wait_ge(full, U_OT)
            if h >= 2:
                pool.wait_ge(sc_full, TT * (h - 1))
            for l in range(1, 4):
                hf = BLK << (l - 1)
                even = span(B128[:, 0:SEQ], l, 0)
                mm = pool.tensor_tensor(span(kl(s, l), l, 0),
                                        even[:, :, hf - 1:hf].to_broadcast([128, SEQ // (2 * hf), hf]), even, ALU.subtract)
            mm.then_inc(argp, 1)
            if h < 2:
                for l in range(1, 4):
                    pool.memset(span(ql(s, l), l, 0), 0.0)
                    pool.memset(span(kl(s, l), l, 1), 0.0)

        def pool_level_operands(pool, h):
            s = h % 2
            pool.wait_ge(expl, h + 1)
            for l in range(1, 4):
                mm = pool.tensor_tensor(span(kl(s, l), l, 0), span(kl(s, l), l, 0), span(QK[:, h, 0:SEQ], l, 0), ALU.mult)
            mm.then_inc(preplp, 1)

        def gla_exps(act, h):
            s = h % 2
            c = 1.0 / GATE
            act.wait_ge(cum, 2 * h + 2)
            if h >= 2:
                act.wait_ge(st_done, 8 * (h - 1))
                act.wait_ge(o_full, TT * (h - 1))
            act.activation(kd(s), B16[:, :], ACT.Exp, scale=-c)
            act.activation(qd(s), B16[:, :], ACT.Exp, scale=c)
            act.activation(QI[:, s, :], B128[:, 0:SEQ], ACT.Exp, scale=c)
            act.activation(DEC[:, s, 0:4], B128[:, 127:SEQ:128], ACT.Exp, scale=c)
            act.activation(DEC[:, s, 4:12], B16[:, SEQ + SL - 1:T:SL], ACT.Exp, scale=c)
            act.wait_ge(argk, h + 1)
            act.activation(kr(s), kr(s), ACT.Exp, scale=c).then_inc(exps, 1)

        def gla_level_exps(act, h):
            s = h % 2
            c = 1.0 / GATE
            act.wait_ge(argl, h + 1)
            act.wait_ge(argp, h + 1)
            for l in range(1, 4):
                act.activation(span(ql(s, l), l, 1), span(ql(s, l), l, 1), ACT.Exp, scale=c)
                mm = act.activation(span(kl(s, l), l, 0), span(kl(s, l), l, 0), ACT.Exp, scale=c)
            mm.then_inc(expl, 1)

        def gla_dve(v):
            def mask(n):
                g = GO[n % TT]
                v.wait_ge(sc_full, n + 1)
                if n >= 2:
                    v.wait_ge(o_full, n - 1)
                if g == TT - 1:
                    v.tensor_tensor(AT[:, n % 2, :], PS[:, n % 2, 0:128], MASK[:, 0, :], ALU.mult).then_inc(att, 1)
                    return
                if n >= 1:
                    v.wait_ge(att, n)
                v.tensor_tensor(MPR[:, :], PS[:, n % 2, :], MASK[:, :, :].rearrange("p l q -> p (l q)"), ALU.mult)\
                    .then_inc(prod, 1)
                v.wait_ge(prod, 4 * (n // TT) + n % TT)
                v.tensor_reduce(AT[:, n % 2, :], MPR[:, :].rearrange("p (l q) -> p q l", l=4), AX.X, ALU.add)\
                    .then_inc(att, 1)

            def after(n):
                h, j = n // TT, n % TT
                g = GO[j]
                v.wait_ge(osq, n + 1)
                r = RS[:, g, DV * h:DV * h + DV]
                v.tensor_tensor(r, PS[:, 2 + n % 2, 0:DV], r, ALU.mult).then_inc(og, 1)
                for x in range(4 if j == 0 else 1):
                    cnt = 8 * h + x if j == 0 else 8 * h + 4 + j - 1
                    v.wait_ge(st_full, cnt + 1)
                    b = 4 + cnt % 2
                    if j == 0:
                        for e in range(2):
                            q = 2 * x + e
                            mm = v.scalar_tensor_tensor(out=S0[:, q, :], in0=S0[:, q, :],
                                                        scalar=DEC[:, h % 2, 4 + q:5 + q],
                                                        in1=PS[:, b, DV * e:DV * e + DV], op0=ALU.mult, op1=ALU.add)
                        mm.then_inc(st_done, 1)
                    elif j == 1:
                        if h:
                            v.wait_ge(s_pout, 16 * h)
                        v.tensor_copy(ST[:, :], PS[:, b, 0:DV]).then_inc(st_done, 1)
                    else:
                        v.wait_ge(st_done, cnt)
                        v.scalar_tensor_tensor(out=ST[:, :], in0=ST[:, :], scalar=DEC[:, h % 2, j - 1:j],
                                               in1=PS[:, b, 0:DV], op0=ALU.mult, op1=ALU.add).then_inc(st_done, 1)

            mask(0)
            gla_levels(v, 0)
            gla_level_operands(v, 0)
            after(0)
            gla_sums(v, 1)
            gla_levels(v, 1)
            for n in range(1, STEPS + 1):
                h = n // TT
                if n < STEPS:
                    mask(n)
                if n > 1:
                    after(n - 1)
                if n in (3, 4):
                    rest_tile(v, T_WO + n - 1)
                if n % TT == 0 and h + 1 < H:
                    gla_sums(v, h + 1)
                    gla_levels(v, h + 1)
                if n % TT == 2 and h + 1 < H:
                    gla_operands(v, h + 1)
                if n % TT == 3 and h + 1 < H:
                    gla_queries(v, h + 1)
                if n % TT == 2 and h:
                    head_inverse(v, h - 1)
                if n % TT == 4 and h + 1 < H:
                    gla_level_operands(v, h + 1)

        def gla_act(act):
            def keys(n):
                act.wait_ge(tr_full, n + 1)
                if n >= 2:
                    act.wait_ge(st_full, stc(n - 2))
                if GO[n % TT] == TT - 1:
                    act.activation(KTK[:, 2 * (n % 2), :], PS[:, 6 + n % 2, 0:128], ACT.Copy, scale=EO[:, 0:1])
                    act.activation(KTK[:, 2 * (n % 2) + 1, :], PS[:, 6 + n % 2, 0:128], ACT.Copy,
                                   scale=EO[:, 1:2]).then_inc(kt_done, 1)
                else:
                    act.activation(KTK[:, 2 * (n % 2), :], PS[:, 6 + n % 2, 0:128], ACT.Copy).then_inc(kt_done, 1)

            def out_squares(m):
                act.wait_ge(o_full, m + 1)
                if m:
                    act.wait_ge(osq, m)
                c = TT * (m // TT) + GO[m % TT]
                act.activation(JNK[:, :], PS[:, 2 + m % 2, 0:DV], ACT.Square, accum_out=SSH[:, c:c + 1])\
                    .then_inc(osq, 1)

            keys(0)
            gla_level_exps(act, 0)
            out_squares(0)
            for n in range(1, STEPS + 1):
                if n < STEPS:
                    keys(n)
                if n > 1:
                    out_squares(n - 1)
                if n in (2, 3):
                    round_tile(act, T_WO + n)
                if n % TT == 1 and n // TT + 1 < H:
                    gla_exps(act, n // TT + 1)
                    gla_level_exps(act, n // TT + 1)
                h = n // TT - 1
                if n % TT == 2 and h >= 0:
                    head_root(act, h)
                if n % TT == 3 and h >= 0:
                    act.wait_ge(rt_h, 2 * h + 2)
                    act.wait_ge(og, TT * (h + 1))
                    for g in range(TT):
                        mm = scale_head(act, h, g)
                    mm.then_inc(ogh, 1)

        def stc(n):
            return 8 * (n // TT) + 4 + n % TT

        block = ctx.enter_context(nc.Block())

        @block.sync
        def _(sp):
            front_sp(sp)
            ffn_sp(sp, 0)
            att_sp(sp)
            ffn_sp(sp, 1)
            final_sp(sp)

        @block.gpsimd
        def _(pool):
            front_pool(pool)
            ffn_pool(pool, 0)
            clear_sums(pool, 2)
            for k in range(KT):
                add_squares(pool, k, 2)
            att_pool(pool)
            clear_sums(pool, 3)
            with pool.Fori(0, 2) as i:
                for k in range(4):
                    add_squares(pool, k, 3, i)
            ffn_pool(pool, 1)

        @block.scalar
        def _(act):
            front_act(act)
            ffn_act(act, 0, False, V_KV, 2)
            att_act(act)
            ffn_act(act, 1, True, None, None)
            final_act(act)

        @block.vector
        def _(v):
            front_dve(v)
            ffn_dve(v, 0, False, V_KV, XF[0] + KT)
            att_dve(v)
            ffn_dve(v, 1, True, None, 0)
            final_dve(v)

        @block.tensor
        def _(pe):
            front_pe(pe)
            ffn_pe(pe, 0)
            att_pe(pe)
            ffn_pe(pe, 1)
            final_pe(pe)


INPUTS = ("x_prompt", "x_sample", "state_gla", "cache_k", "cache_v", "state_ffn_conv", "norm_mix", "norm_ffn",
          "norm_kv", "norm_final", "gla_w_in", "gla_w_g2", "gla_b_g2", "gla_g_onorm", "gla_w_out", "w_kv", "att_w_q",
          "att_sinks", "att_w_o", "ffn_w_up", "ffn_conv_w", "ffn_conv_b", "ffn_w_down")
OUTPUTS = (("y_p", (1, SEQ, D)), ("y_s", (NS, SL, D)), ("gla_p", (1, 1, H, DK, DV)), ("k_p", (1, WIN, KVH, HD)),
           ("v_p", (1, WIN, KVH, HD)), ("conv_p", (2, 1, 2, 2 * DFF)), ("gla_s", (1, NS, H, DK, DV)),
           ("k_s", (NS, WIN, KVH, HD)), ("v_s", (NS, WIN, KVH, HD)), ("conv_s", (2, NS, 2, 2 * DFF)))


def kernel(**inputs):
    import numpy as np
    import concourse.bacc as bacc
    from concourse.bass_utils import run_bass_kernel_spmd

    nc = bacc.Bacc("TRN2", target_bir_lowering=False, num_devices=1)
    arrays, A, O = {}, {}, {}
    for name in INPUTS:
        a = np.ascontiguousarray(inputs[name])
        arrays[f"in_{name}_dram"] = a
        A[name] = nc.dram_tensor(f"in_{name}_dram", a.shape, mybir.dt.from_np(a.dtype), kind="ExternalInput").ap()
    for i, (name, shape) in enumerate(OUTPUTS):
        O[name] = nc.dram_tensor(f"out_{i}_dram", shape, F32, kind="ExternalOutput").ap()
    build(nc, A, O)
    r = run_bass_kernel_spmd(nc, [arrays], core_ids=[0])
    return tuple(r.results[0][f"out_{i}_dram"] for i in range(len(OUTPUTS)))
```
